# Optimizing a Trainium2 kernel written in Bass

```python
import math
import jax, jax.numpy as jnp
from jax import lax
import numpy as np

D_MODEL = 1024
BATCH = 1
SEQ = 256
DEPTH = 2

N_A_LAYERS = DEPTH // 2
N_B_LAYERS = DEPTH - N_A_LAYERS
PLE_DIM = 256
DN_ALPHA = (2.0 * DEPTH) ** 0.25
DN_BETA = (8.0 * DEPTH) ** -0.25
NORM_EPS = 1e-5

ML_HEADS = 8
ML_QK_DIM = D_MODEL // (2 * ML_HEADS)
ML_V_DIM = D_MODEL // ML_HEADS
ML_CHUNK = 64
ML_Q_END = ML_HEADS * ML_QK_DIM
ML_K_END = 2 * ML_HEADS * ML_QK_DIM
ML_V_END = ML_K_END + ML_HEADS * ML_V_DIM
ML_I_END = ML_V_END + ML_HEADS
ML_F_END = ML_I_END + ML_HEADS
ML_IN_COLS = ML_F_END + D_MODEL

MLA_HEADS = 8
MLA_NOPE_DIM = 128
MLA_ROPE_DIM = 64
MLA_V_DIM = 128
MLA_KV_RANK = 256
MLA_Q_RANK = 384
ROPE_THETA = 10000.0
ATTN_BLOCK = 128

PEER_HEADS = 8
PEER_N_KEYS = 128
PEER_N_EXPERTS = PEER_N_KEYS * PEER_N_KEYS
PEER_KEY_DIM = 256
PEER_HALF = PEER_KEY_DIM // 2
PEER_TOPK = 16
PEER_BLOCK = 128


def layer_norm(x, g, b):
    xf = x.astype(jnp.float32)
    mu = jnp.mean(xf, -1, keepdims=True)
    var = jnp.mean(jnp.square(xf - mu), -1, keepdims=True)
    y = (xf - mu) * lax.rsqrt(var + NORM_EPS)
    return (y * g.astype(jnp.float32) + b.astype(jnp.float32)).astype(x.dtype)

def rms_norm(x, g):
    xf = x.astype(jnp.float32)
    y = xf * lax.rsqrt(jnp.mean(jnp.square(xf), -1, keepdims=True) + NORM_EPS)
    return (y * g.astype(jnp.float32)).astype(x.dtype)

def rope_angles(positions, dim):
    inv_freq = ROPE_THETA ** (-jnp.arange(0, dim, 2, dtype=jnp.float32) / dim)
    ang = positions.astype(jnp.float32)[..., None] * inv_freq
    return jnp.cos(ang), jnp.sin(ang)

def apply_rope(x, cos, sin):
    xf = x.astype(jnp.float32)
    x1, x2 = jnp.split(xf, 2, axis=-1)
    return jnp.concatenate([x1 * cos - x2 * sin, x1 * sin + x2 * cos], -1).astype(x.dtype)

def mlstm_chunk_step(carry, inp):
    C, n, m = carry
    q, k, v, ig, lf = inp
    L = q.shape[2]
    b = jnp.cumsum(lf, axis=-1)
    causal = jnp.tril(jnp.ones((L, L), dtype=bool))
    log_w = jnp.where(causal, b[..., :, None] - b[..., None, :] + ig[..., None, :], -jnp.inf)
    log_inter = b + m[..., None]
    m_t = jnp.maximum(log_inter, jnp.max(log_w, -1))
    w = jnp.exp(log_w - m_t[..., None])
    s_inter = jnp.exp(log_inter - m_t)
    qk = jnp.einsum('bhtd,bhsd->bhts', q, k) * w
    num = jnp.einsum('bhts,bhsv->bhtv', qk, v) + s_inter[..., None] * jnp.einsum('bhtd,bhdv->bhtv', q, C)
    den = jnp.sum(qk, -1) + s_inter * jnp.einsum('bhtd,bhd->bht', q, n)
    h = num / jnp.maximum(jnp.abs(den), jnp.exp(-m_t))[..., None]
    b_last = b[..., -1]
    log_src = b_last[..., None] - b + ig
    m_new = jnp.maximum(b_last + m, jnp.max(log_src, -1))
    w_src = jnp.exp(log_src - m_new[..., None])
    s_old = jnp.exp(b_last + m - m_new)
    C_new = s_old[..., None, None] * C + jnp.einsum('bhs,bhsd,bhsv->bhdv', w_src, k, v)
    n_new = s_old[..., None] * n + jnp.einsum('bhs,bhsd->bhd', w_src, k)
    return (C_new, n_new, m_new), h

def mlstm_mixer(x, w_in, b_if, hn_g, w_out):
    B, S, _ = x.shape
    H, L = ML_HEADS, ML_CHUNK
    nc = S // L
    proj = x @ w_in
    q, k, v = proj[..., :ML_Q_END], proj[..., ML_Q_END:ML_K_END], proj[..., ML_K_END:ML_V_END]
    gi, gf, og = proj[..., ML_V_END:ML_I_END], proj[..., ML_I_END:ML_F_END], proj[..., ML_F_END:]

    def to_chunks(t, d):
        return t.reshape(B, nc, L, H, d).transpose(1, 0, 3, 2, 4).astype(jnp.float32)

    def gate_chunks(t):
        return t.reshape(B, nc, L, H).transpose(1, 0, 3, 2)

    qc = to_chunks(q, ML_QK_DIM)
    kc = to_chunks(k, ML_QK_DIM) * (ML_QK_DIM ** -0.5)
    vc = to_chunks(v, ML_V_DIM)
    b_if = b_if.astype(jnp.float32)
    ig = gate_chunks(gi.astype(jnp.float32) + b_if[0])
    lf = gate_chunks(jax.nn.log_sigmoid(gf.astype(jnp.float32) + b_if[1]))
    init = (jnp.zeros((B, H, ML_QK_DIM, ML_V_DIM), jnp.float32),
            jnp.zeros((B, H, ML_QK_DIM), jnp.float32),
            jnp.zeros((B, H), jnp.float32))
    _, h = lax.scan(mlstm_chunk_step, init, (qc, kc, vc, ig, lf))
    h = h.transpose(1, 0, 3, 2, 4).reshape(B, S, H, ML_V_DIM)
    mu = jnp.mean(h, -1, keepdims=True)
    var = jnp.mean(jnp.square(h - mu), -1, keepdims=True)
    hn = (h - mu) * lax.rsqrt(var + NORM_EPS) * hn_g.astype(jnp.float32).reshape(H, ML_V_DIM)
    out = jax.nn.sigmoid(og.astype(jnp.float32)) * hn.reshape(B, S, H * ML_V_DIM)
    return out.astype(x.dtype) @ w_out

def mla_shared_kv(xs, w_down, kv_norm_g, w_up, cos, sin):
    B, S, _ = xs.shape
    ckr = xs @ w_down
    c_kv = rms_norm(ckr[..., :MLA_KV_RANK], kv_norm_g)
    kv = (c_kv @ w_up).reshape(B, S, MLA_HEADS, MLA_NOPE_DIM + MLA_V_DIM)
    k_nope = kv[..., :MLA_NOPE_DIM].transpose(0, 2, 1, 3)
    v = kv[..., MLA_NOPE_DIM:].transpose(0, 2, 1, 3)
    k_rope = apply_rope(ckr[..., MLA_KV_RANK:], cos, sin)
    return k_nope, k_rope, v

def mla_mixer(x, w_dq, q_norm_g, w_uq, w_out, k_nope, k_rope, v, cos, sin):
    B, S, _ = x.shape
    H = MLA_HEADS
    c_q = rms_norm(x @ w_dq, q_norm_g)
    q = (c_q @ w_uq).reshape(B, S, H, MLA_NOPE_DIM + MLA_ROPE_DIM).transpose(0, 2, 1, 3)
    q_nope = q[..., :MLA_NOPE_DIM]
    q_rope = apply_rope(q[..., MLA_NOPE_DIM:], cos[:, None], sin[:, None])
    nb = S // ATTN_BLOCK

    def blocks(t):
        return t.reshape(B, H, nb, ATTN_BLOCK, t.shape[-1]).transpose(2, 0, 1, 3, 4)

    scale = (MLA_NOPE_DIM + MLA_ROPE_DIM) ** -0.5
    key_pos = jnp.arange(S)

    def attend(args):
        idx, qn, qr = args
        s = jnp.einsum('bhqd,bhkd->bhqk', qn, k_nope) + jnp.einsum('bhqd,bkd->bhqk', qr, k_rope)
        s = s.astype(jnp.float32) * scale
        q_pos = idx * ATTN_BLOCK + jnp.arange(ATTN_BLOCK)
        s = jnp.where(key_pos[None, :] <= q_pos[:, None], s, -jnp.inf)
        p = jax.nn.softmax(s, axis=-1).astype(v.dtype)
        return jnp.einsum('bhqk,bhkd->bhqd', p, v)

    o = lax.map(attend, (jnp.arange(nb), blocks(q_nope), blocks(q_rope)))
    o = o.transpose(1, 0, 3, 2, 4).reshape(B, S, H * MLA_V_DIM)
    return o @ w_out

def peer_ffn(x, w_q, sub_keys, u, v):
    B, S, D = x.shape
    T = B * S
    K = PEER_TOPK
    xt = x.reshape(T, D)
    q = (xt @ w_q).reshape(T, PEER_HEADS, 2, PEER_HALF)
    s = jnp.einsum('thcd,hcnd->thcn', q, sub_keys).astype(jnp.float32)
    s1, i1 = lax.top_k(s[:, :, 0], K)
    s2, i2 = lax.top_k(s[:, :, 1], K)
    cand_s = (s1[..., :, None] + s2[..., None, :]).reshape(T, PEER_HEADS, K * K)
    cand_i = (i1[..., :, None] * PEER_N_KEYS + i2[..., None, :]).reshape(T, PEER_HEADS, K * K)
    top_s, top_pos = lax.top_k(cand_s, K)
    expert_idx = jnp.take_along_axis(cand_i, top_pos, axis=-1)
    gates = jax.nn.softmax(top_s, axis=-1).astype(x.dtype)
    nb = T // PEER_BLOCK

    def expert_block(args):
        xb, eb, gb = args
        ub = jnp.take(u, eb, axis=0)
        act = jax.nn.gelu(jnp.einsum('thkd,td->thk', ub, xb), approximate=False)
        vb = jnp.take(v, eb, axis=0)
        return jnp.einsum('thk,thkd->td', gb * act, vb)

    out = lax.map(expert_block, (xt.reshape(nb, PEER_BLOCK, D),
                                 expert_idx.reshape(nb, PEER_BLOCK, PEER_HEADS, K),
                                 gates.reshape(nb, PEER_BLOCK, PEER_HEADS, K)))
    return out.reshape(B, S, D)

def first_inputs(seed: int = 0) -> dict:
    key = jax.random.key(seed)
    ks = jax.random.split(key, 24)
    D = D_MODEL
    nrm = jax.random.normal
    f32 = jnp.float32
    x = nrm(ks[0], (BATCH, SEQ, D), f32)
    p = nrm(ks[1], (DEPTH, BATCH, SEQ, PLE_DIM), f32)
    positions = jnp.broadcast_to(jnp.arange(SEQ, dtype=jnp.int32), (BATCH, SEQ))
    ln_g = 1.0 + 0.05 * nrm(ks[2], (DEPTH, 2, D), f32)
    ln_b = 0.02 * nrm(ks[3], (DEPTH, 2, D), f32)
    a_w_in = nrm(ks[4], (N_A_LAYERS, D, ML_IN_COLS), f32) * D ** -0.5
    b_i = 0.1 * nrm(ks[5], (N_A_LAYERS, ML_HEADS), f32)
    b_f = jnp.linspace(3.0, 6.0, ML_HEADS, dtype=f32) + 0.1 * nrm(ks[6], (N_A_LAYERS, ML_HEADS), f32)
    a_b_if = jnp.stack([b_i, b_f], axis=1)
    a_hn_g = 1.0 + 0.05 * nrm(ks[7], (N_A_LAYERS, D), f32)
    a_w_out = nrm(ks[8], (N_A_LAYERS, D, D), f32) * (D ** -0.5 * DN_BETA)
    kv_w_down = nrm(ks[9], (D, MLA_KV_RANK + MLA_ROPE_DIM), f32) * D ** -0.5
    kv_norm_g = 1.0 + 0.05 * nrm(ks[10], (MLA_KV_RANK,), f32)
    kv_w_up = nrm(ks[11], (MLA_KV_RANK, MLA_HEADS * (MLA_NOPE_DIM + MLA_V_DIM)), f32) * MLA_KV_RANK ** -0.5
    b_w_dq = nrm(ks[12], (N_B_LAYERS, D, MLA_Q_RANK), f32) * D ** -0.5
    b_q_norm_g = 1.0 + 0.05 * nrm(ks[13], (N_B_LAYERS, MLA_Q_RANK), f32)
    b_w_uq = nrm(ks[14], (N_B_LAYERS, MLA_Q_RANK, MLA_HEADS * (MLA_NOPE_DIM + MLA_ROPE_DIM)), f32) * MLA_Q_RANK ** -0.5
    b_w_out = nrm(ks[15], (N_B_LAYERS, MLA_HEADS * MLA_V_DIM, D), f32) * ((MLA_HEADS * MLA_V_DIM) ** -0.5 * DN_BETA)
    peer_w_q = nrm(ks[16], (DEPTH, D, PEER_HEADS * PEER_KEY_DIM), f32) * D ** -0.5
    peer_sub_keys = nrm(ks[17], (DEPTH, PEER_HEADS, 2, PEER_N_KEYS, PEER_HALF), f32) * PEER_HALF ** -0.5
    peer_u = nrm(ks[18], (DEPTH, PEER_N_EXPERTS, D), f32) * D ** -0.5
    peer_v = nrm(ks[19], (DEPTH, PEER_N_EXPERTS, D), f32) * (DN_BETA * PEER_HEADS ** -0.5)
    ple_w_proj = nrm(ks[20], (DEPTH, PLE_DIM, D), f32) * (0.5 * PLE_DIM ** -0.5)
    ple_w_gate = nrm(ks[21], (DEPTH, D, D), f32) * D ** -0.5
    return {"x": x, "p": p, "positions": positions, "ln_g": ln_g, "ln_b": ln_b,
            "a_w_in": a_w_in, "a_b_if": a_b_if, "a_hn_g": a_hn_g, "a_w_out": a_w_out,
            "kv_w_down": kv_w_down, "kv_norm_g": kv_norm_g, "kv_w_up": kv_w_up,
            "b_w_dq": b_w_dq, "b_q_norm_g": b_q_norm_g, "b_w_uq": b_w_uq, "b_w_out": b_w_out,
            "peer_w_q": peer_w_q, "peer_sub_keys": peer_sub_keys, "peer_u": peer_u, "peer_v": peer_v,
            "ple_w_proj": ple_w_proj, "ple_w_gate": ple_w_gate}

def first_block(x, p, positions, ln_g, ln_b, a_w_in, a_b_if, a_hn_g, a_w_out,
              kv_w_down, kv_norm_g, kv_w_up, b_w_dq, b_q_norm_g, b_w_uq, b_w_out,
              peer_w_q, peer_sub_keys, peer_u, peer_v, ple_w_proj, ple_w_gate):
    cos, sin = rope_angles(positions, MLA_ROPE_DIM)
    shared = None
    for i in range(DEPTH):
        if i < N_A_LAYERS:
            mix = mlstm_mixer(x, a_w_in[i], a_b_if[i], a_hn_g[i], a_w_out[i])
        else:
            j = i - N_A_LAYERS
            if j == 0:
                shared = mla_shared_kv(x, kv_w_down, kv_norm_g, kv_w_up, cos, sin)
            k_nope, k_rope, v = shared
            mix = mla_mixer(x, b_w_dq[j], b_q_norm_g[j], b_w_uq[j], b_w_out[j],
                            k_nope, k_rope, v, cos, sin)
        x = layer_norm(DN_ALPHA * x + mix, ln_g[i, 0], ln_b[i, 0])
        x = layer_norm(DN_ALPHA * x + peer_ffn(x, peer_w_q[i], peer_sub_keys[i], peer_u[i], peer_v[i]),
                       ln_g[i, 1], ln_b[i, 1])
        x = x + jax.nn.sigmoid(x @ ple_w_gate[i]) * (p[i] @ ple_w_proj[i])
    return x


DEPTH_2 = 1

RET_HEADS = 4
RET_QK_DIM = 128
RET_V_DIM = 256
RET_CHUNK = 128
RET_QK_W = RET_HEADS * RET_QK_DIM
RET_V_W = RET_HEADS * RET_V_DIM
NA_HEADS = 8
NA_HEAD_DIM = 64
NA_W = NA_HEADS * NA_HEAD_DIM
GRID_W = 64
NA_WIN_ROWS = 8
NA_WIN_COLS = 16
NA_Q_BLOCK_COLS = 16
NA_K_BLOCK_COLS = 32
NA_REL_ROWS = 2 * NA_WIN_ROWS - 1
NA_REL_COLS = 2 * NA_WIN_COLS - 1
D_FF = 2816
RMS_EPS = 1e-6
ROPE_BASE = 10000.0
NEG_INF = -1e30
MIX_SPLITS = (RET_QK_W, RET_QK_W, RET_V_W, RET_V_W, NA_W, NA_W, NA_W, D_MODEL, D_MODEL)
MIX_IN_W = sum(MIX_SPLITS)


def _rms_norm(x, gain):
    xf = x.astype(jnp.float32)
    y = xf * lax.rsqrt(jnp.mean(xf * xf, axis=-1, keepdims=True) + RMS_EPS)
    return (y * gain.astype(jnp.float32)).astype(x.dtype)

def _swiglu(x, w_in, w_out):
    g, u = jnp.split(x @ w_in, 2, axis=-1)
    return (jax.nn.silu(g) * u) @ w_out

def _rotary(x, pos):
    half = x.shape[-1] // 2
    inv = 1.0 / (ROPE_BASE ** jnp.linspace(0.0, 1.0, half, dtype=jnp.float32))
    ang = pos[:, None] * inv[None, :]
    cos, sin = jnp.cos(ang), jnp.sin(ang)
    x1, x2 = x[..., :half], x[..., half:]
    return jnp.concatenate([x1 * cos - x2 * sin, x1 * sin + x2 * cos], axis=-1)

def _retention_one_dir(q, k, v, log_gamma, strict):
    B, H, S, DK = q.shape
    DV = v.shape[-1]
    C = RET_CHUNK
    N = S // C
    qc = q.reshape(B, H, N, C, DK)
    kc = k.reshape(B, H, N, C, DK)
    vc = v.reshape(B, H, N, C, DV)
    idx = jnp.arange(C, dtype=jnp.float32)
    diff = idx[:, None] - idx[None, :]
    lower = (diff > 0) if strict else (diff >= 0)
    intra = jnp.where(lower[None], jnp.exp(log_gamma[:, None, None] * jnp.where(lower, diff, 0.0)[None]), 0.0)
    scores = jnp.einsum('bhnqd,bhnkd->bhnqk', qc, kc) * intra[None, :, None]
    inner = jnp.einsum('bhnqk,bhnkv->bhnqv', scores, vc)
    k_dec = jnp.exp(log_gamma[:, None] * (C - 1 - idx)[None, :])
    upd = jnp.einsum('bhnkd,bhnkv->nbhdv', kc * k_dec[None, :, None, :, None], vc)
    chunk_dec = jnp.exp(log_gamma * C)[None, :, None, None]

    def step(state, u):
        return chunk_dec * state + u, state

    _, prev = lax.scan(step, jnp.zeros((B, H, DK, DV), jnp.float32), upd)
    q_dec = jnp.exp(log_gamma[:, None] * (idx + 1.0)[None, :])
    cross = jnp.einsum('bhnqd,nbhdv->bhnqv', qc * q_dec[None, :, None, :, None], prev)
    return (inner + cross).reshape(B, H, S, DV)

def _bidirectional_retention(q, k, v, decay_fwd_logit, decay_bwd_logit):
    lg_f = jax.nn.log_sigmoid(decay_fwd_logit.astype(jnp.float32))
    lg_b = jax.nn.log_sigmoid(decay_bwd_logit.astype(jnp.float32))
    y_f = _retention_one_dir(q, k, v, lg_f, strict=False)
    flip = lambda a: jnp.flip(a, axis=2)
    y_b = flip(_retention_one_dir(flip(q), flip(k), flip(v), lg_b, strict=True))
    return y_f + y_b

def _neighborhood_attention(q, k, v, rel_bias):
    B, S, NH, DH = q.shape
    rows = S // GRID_W
    kr = min(NA_WIN_ROWS, rows)
    ncb = GRID_W // NA_Q_BLOCK_COLS
    qg = (q * (DH ** -0.5)).reshape(B, rows, GRID_W, NH, DH)
    kg = k.reshape(B, rows, GRID_W, NH, DH)
    vg = v.reshape(B, rows, GRID_W, NH, DH)
    c0 = jnp.arange(ncb, dtype=jnp.int32) * NA_Q_BLOCK_COLS
    q_cols = c0[:, None] + jnp.arange(NA_Q_BLOCK_COLS, dtype=jnp.int32)[None, :]
    key_cols = (jnp.clip(c0 - NA_WIN_COLS // 2, 0, GRID_W - NA_K_BLOCK_COLS)[:, None]
                + jnp.arange(NA_K_BLOCK_COLS, dtype=jnp.int32)[None, :])
    win_start = jnp.clip(q_cols - NA_WIN_COLS // 2, 0, GRID_W - NA_WIN_COLS)
    kcb = key_cols[:, None, :]
    col_mask = (kcb >= win_start[:, :, None]) & (kcb < win_start[:, :, None] + NA_WIN_COLS)
    col_idx = jnp.clip(kcb - q_cols[:, :, None] + NA_WIN_COLS - 1, 0, NA_REL_COLS - 1)

    def row_block(r):
        rs = jnp.clip(r - kr // 2, 0, rows - kr)
        q_r = lax.dynamic_index_in_dim(qg, r, axis=1, keepdims=False).reshape(B, ncb, NA_Q_BLOCK_COLS, NH, DH)
        k_blk = lax.dynamic_slice_in_dim(kg, rs, kr, axis=1)[:, :, key_cols]
        v_blk = lax.dynamic_slice_in_dim(vg, rs, kr, axis=1)[:, :, key_cols]
        s = jnp.einsum('bnqhd,brnkhd->bhnqrk', q_r, k_blk).astype(jnp.float32)
        row_idx = rs + jnp.arange(kr, dtype=jnp.int32) - r + NA_WIN_ROWS - 1
        bias = rel_bias[:, row_idx[None, None, :, None], col_idx[:, :, None, :]].astype(jnp.float32)
        s = jnp.where(col_mask[:, :, None, :], s + bias, NEG_INF)
        p = jax.nn.softmax(s.reshape(B, NH, ncb, NA_Q_BLOCK_COLS, kr * NA_K_BLOCK_COLS), axis=-1)
        p = p.reshape(s.shape).astype(v.dtype)
        o = jnp.einsum('bhnqrk,brnkhd->bnqhd', p, v_blk)
        return o.reshape(B, GRID_W, NH, DH)

    out = lax.map(row_block, jnp.arange(rows, dtype=jnp.int32))
    return out.transpose(1, 0, 2, 3, 4).reshape(B, S, NH * DH)

def _token_mixing(u, w_in, decay_fwd, decay_bwd, rel_bias, w_ret_out, w_na_out, w_out, pos):
    B, S, _ = u.shape
    points = [sum(MIX_SPLITS[:i + 1]) for i in range(len(MIX_SPLITS) - 1)]
    rq, rk, rv, rg, nq, nk, nv, g_ret, g_na = jnp.split(u @ w_in, points, axis=-1)
    heads = lambda a, d: a.reshape(B, S, RET_HEADS, d).transpose(0, 2, 1, 3).astype(jnp.float32)
    q = _rotary(heads(rq, RET_QK_DIM), pos)
    k = _rotary(heads(rk, RET_QK_DIM), pos) * (RET_QK_DIM ** -0.5)
    y = _bidirectional_retention(q, k, heads(rv, RET_V_DIM), decay_fwd, decay_bwd)
    y = y * lax.rsqrt(jnp.mean(y * y, axis=-1, keepdims=True) + RMS_EPS)
    y = y.transpose(0, 2, 1, 3).reshape(B, S, RET_V_W).astype(u.dtype)
    y_ret = (jax.nn.silu(rg) * y) @ w_ret_out
    na_heads = lambda a: a.reshape(B, S, NA_HEADS, NA_HEAD_DIM)
    y_na = _neighborhood_attention(na_heads(nq), na_heads(nk), na_heads(nv), rel_bias) @ w_na_out
    merged = jax.nn.sigmoid(g_ret) * y_ret + jax.nn.sigmoid(g_na) * y_na
    return merged @ w_out

def second_inputs(seed: int = 0) -> dict:
    key = jax.random.key(seed)
    ks = jax.random.split(key, 20)
    f32 = jnp.float32

    def w(k, shape, fan_in):
        return jax.random.normal(k, (DEPTH_2,) + shape, f32) * (fan_in ** -0.5)

    def gain(k):
        return 1.0 + 0.05 * jax.random.normal(k, (DEPTH_2, D_MODEL), f32)

    gamma0 = 1.0 - 2.0 ** (-5.0 - np.arange(RET_HEADS, dtype=np.float32))
    logit0 = jnp.asarray(np.log(gamma0 / (1.0 - gamma0)), f32)
    return {
        "x": jax.random.normal(ks[0], (BATCH, SEQ, D_MODEL), f32),
        "ffn1_pre_norm": gain(ks[1]),
        "ffn1_w_in": w(ks[2], (D_MODEL, 2 * D_FF), D_MODEL),
        "ffn1_w_out": w(ks[3], (D_FF, D_MODEL), D_FF),
        "ffn1_post_norm": gain(ks[4]),
        "mix_pre_norm": gain(ks[5]),
        "w_mix_in": w(ks[6], (D_MODEL, MIX_IN_W), D_MODEL),
        "ret_decay_fwd": logit0[None] + 0.1 * jax.random.normal(ks[7], (DEPTH_2, RET_HEADS), f32),
        "ret_decay_bwd": logit0[None] + 0.1 * jax.random.normal(ks[8], (DEPTH_2, RET_HEADS), f32),
        "na_rel_bias": 0.02 * jax.random.normal(ks[9], (DEPTH_2, NA_HEADS, NA_REL_ROWS, NA_REL_COLS), f32),
        "w_ret_out": w(ks[10], (RET_V_W, D_MODEL), RET_V_W),
        "w_na_out": w(ks[11], (NA_W, D_MODEL), NA_W),
        "w_mix_out": w(ks[12], (D_MODEL, D_MODEL), D_MODEL),
        "mix_post_norm": gain(ks[13]),
        "ffn2_pre_norm": gain(ks[14]),
        "ffn2_w_in": w(ks[15], (D_MODEL, 2 * D_FF), D_MODEL),
        "ffn2_w_out": w(ks[16], (D_FF, D_MODEL), D_FF),
        "ffn2_post_norm": gain(ks[17]),
    }

def second_block(x, ffn1_pre_norm, ffn1_w_in, ffn1_w_out, ffn1_post_norm, mix_pre_norm, w_mix_in,
              ret_decay_fwd, ret_decay_bwd, na_rel_bias, w_ret_out, w_na_out, w_mix_out, mix_post_norm,
              ffn2_pre_norm, ffn2_w_in, ffn2_w_out, ffn2_post_norm):
    S = x.shape[1]
    pos = jnp.arange(S, dtype=jnp.float32)
    for l in range(DEPTH_2):
        h = _swiglu(_rms_norm(x, ffn1_pre_norm[l]), ffn1_w_in[l], ffn1_w_out[l])
        x = x + 0.5 * _rms_norm(h, ffn1_post_norm[l])
        m = _token_mixing(_rms_norm(x, mix_pre_norm[l]), w_mix_in[l], ret_decay_fwd[l], ret_decay_bwd[l],
                          na_rel_bias[l], w_ret_out[l], w_na_out[l], w_mix_out[l], pos)
        x = x + _rms_norm(m, mix_post_norm[l])
        h = _swiglu(_rms_norm(x, ffn2_pre_norm[l]), ffn2_w_in[l], ffn2_w_out[l])
        x = x + 0.5 * _rms_norm(h, ffn2_post_norm[l])
    return x


def setup_inputs(seed=0):
    out = dict(first_inputs(seed))
    for name, value in second_inputs(seed + 1).items():
        if name != "x":
            out[name + "_2"] = value
    return out


def reference(
    x, p, positions, ln_g, ln_b, a_w_in, a_b_if, a_hn_g, a_w_out, kv_w_down, kv_norm_g, kv_w_up,
    b_w_dq, b_q_norm_g, b_w_uq, b_w_out, peer_w_q, peer_sub_keys, peer_u, peer_v, ple_w_proj,
    ple_w_gate, ffn1_pre_norm_2, ffn1_w_in_2, ffn1_w_out_2, ffn1_post_norm_2, mix_pre_norm_2,
    w_mix_in_2, ret_decay_fwd_2, ret_decay_bwd_2, na_rel_bias_2, w_ret_out_2, w_na_out_2,
    w_mix_out_2, mix_post_norm_2, ffn2_pre_norm_2, ffn2_w_in_2, ffn2_w_out_2, ffn2_post_norm_2,
):
    x = first_block(
        x, p, positions, ln_g, ln_b, a_w_in, a_b_if, a_hn_g, a_w_out, kv_w_down, kv_norm_g,
        kv_w_up, b_w_dq, b_q_norm_g, b_w_uq, b_w_out, peer_w_q, peer_sub_keys, peer_u, peer_v,
        ple_w_proj, ple_w_gate,
    )
    return second_block(
        x, ffn1_pre_norm_2, ffn1_w_in_2, ffn1_w_out_2, ffn1_post_norm_2, mix_pre_norm_2,
        w_mix_in_2, ret_decay_fwd_2, ret_decay_bwd_2, na_rel_bias_2, w_ret_out_2, w_na_out_2,
        w_mix_out_2, mix_post_norm_2, ffn2_pre_norm_2, ffn2_w_in_2, ffn2_w_out_2,
        ffn2_post_norm_2,
    )


_drawn_inputs = setup_inputs


def setup_inputs(seed=0):
    import zlib

    import numpy as np

    out = dict(_drawn_inputs(seed))
    spreads = {}
    factors = {'kv_norm_g': 4.924, 'b_q_norm_g': 6.532, 'na_rel_bias_2': 8.0, 'ffn2_post_norm_2': 3.654}
    for name, (base, spread) in spreads.items():
        noise = np.random.default_rng([zlib.crc32(name.encode()), seed]).standard_normal(out[name].shape)
        drawn = base * np.exp(spread * noise) if base else spread * noise
        out[name] = __import__('jax').numpy.asarray(drawn.astype(out[name].dtype))
    for name, factor in factors.items():
        out[name] = (out[name] * factor).astype(out[name].dtype)
    return out
```

```python
from contextlib import ExitStack

import numpy as np

import concourse.bass as bass
from concourse import mybir

P = 128
D = 1024
T = 256
TB = T // P
KC = D // P
RING = 8
F32 = mybir.dt.float32
BF16 = mybir.dt.bfloat16
U32 = mybir.dt.uint32
I32 = mybir.dt.int32
ALU = mybir.AluOpType
ACT = mybir.ActivationFunctionType
AX = mybir.AxisListType.X
ds = bass.ds

LAYERS = 2
DN_ALPHA = (2.0 * LAYERS) ** 0.25
NORM_EPS = 1e-5
RMS_EPS = 1e-6
BIG = 1e30
LOWEST = -3.0e38
ROUND = 12582912.0
TWO_PI_A = 6.28125
TWO_PI_B = float(np.float32(2 * np.pi - 6.28125))
PI_BELOW = 3.1415925

H8 = 8
ML_SCALE = 64 ** -0.5
KV_RANK, ROPE, Q_RANK = 256, 64, 384
MLA_SCALE = (128 + 64) ** -0.5
TOPK = 16
EXPERT_TILES = 128
RET_H = 4
RET_SCALE = 128 ** -0.5
NA_SCALE = 64 ** -0.5
FF_TILES = 2816 // P

PEER_TILES = [("wq", 16), ("keys", 2), ("u", EXPERT_TILES), ("v", EXPERT_TILES), ("ple_proj", 2), ("ple_gate", 8)]
STREAM = (
    [("a_qk", 8), ("a_v", 8), ("a_og", 8), ("a_out", 8)]
    + [(f"{n}0", k) for n, k in PEER_TILES]
    + [("kv_q_down", 8), ("up_k", 2), ("up_v", 2), ("uq_nope", 3), ("uq_rope", 3), ("b_out", 8)]
    + [(f"{n}1", k) for n, k in PEER_TILES]
    + [("ffn1_in", 2 * FF_TILES), ("ffn1_out", FF_TILES)]
    + [("rqk", 8), ("rv", 8), ("rg", 8), ("nqk", 8), ("nv", 4), ("g_ret", 8), ("g_na", 8)]
    + [("ret_out", 8), ("na_out", 4), ("mix_out", 8)]
    + [("ffn2_in", 2 * FF_TILES), ("ffn2_out", FF_TILES)]
)

ACC_ORDER = ["a_v", "a_og", "a_out", "v0", "ple_proj0", "ple_gate0", "kv_q_down", "up_v", "uq_rope", "b_out",
             "v1", "ple_proj1", "ple_gate1", "ffn1_out", "rqk", "rv", "rg", "nv", "g_ret", "g_na",
             "ret_out", "na_out", "mix_out", "ffn2_out"]

TURN_ORDER = ["ml_out", "ln0_0", "ln0_1", "x1", "ln1_0", "ln1_1", "x2", "rms1", "rms2", "rqk", "ret", "merged", "rms3"]


def starts(items):
    out, at = {}, 0
    for name, n in items:
        out[name] = at
        at += n
    return out


def attention_order(name, first, last):
    heads = H8 if name != "ret" else RET_H
    out = [((name, s, 0), 1) for s in first]
    for h in range(heads):
        if h + 1 < heads:
            out += [((name, s, h + 1), 1) for s in first]
        out += [((name, s, h), 1) for s in last]
    return out


def peer_slots(layer):
    return [(f"wq{layer}", 16), (f"scores{layer}", 8), (f"u{layer}", EXPERT_TILES), (f"routes{layer}", 2),
            (f"gates{layer}", T // 4)]


def turn(name):
    return [(f"turn_{name}", 4)]


SLOT_ORDER = (
    [("gates", 1), ("a_qk", 8), ("gate_cols", 1)]
    + attention_order("ml", ["decay", "scores"], ["out"])
    + turn("ml_out") + turn("ln0_0") + peer_slots(0) + turn("ln0_1") + turn("x1")
    + [("latents", 3), ("up_k", 8), ("uq_nope", 8), ("rope", 2)]
    + attention_order("mla", ["scores"], ["probs", "out"])
    + turn("ln1_0") + peer_slots(1) + turn("ln1_1")
    + turn("rms1") + [("ffn1", 2 * FF_TILES)] + turn("rms2") + [("nqk", 8)] + turn("rqk")
    + attention_order("ret", ["scores"], ["out"])
    + attention_order("na", ["scores"], ["probs", "out"])
    + turn("ret") + turn("merged") + turn("rms3") + [("ffn2", 2 * FF_TILES)]
)
TILE = starts(STREAM)
SLOT = starts(SLOT_ORDER)
ACC = {name: n for n, name in enumerate(ACC_ORDER)}
TURN = {name: n for n, name in enumerate(TURN_ORDER)}

ROW_SETS = [2, 2, 2, 2, 1, 1, 1]


def program(nc, a, out):
    with ExitStack() as ctx:
        def sbuf(name, shape, dt=F32):
            return ctx.enter_context(nc.sbuf_tensor(name, shape, dt))

        def sem(name):
            return ctx.enter_context(nc.semaphore(name))

        ps = ctx.enter_context(nc.psum_tensor("ps", [P, 8, 512], F32))
        ring = sbuf("ring", [P, RING, D])
        big = sbuf("big", [P, EXPERT_TILES * T])
        X = sbuf("X", [P, TB, D])
        XT = sbuf("XT", [P, KC, T])
        SC = sbuf("SC", [P, 4096])
        TV = sbuf("TV", [P, TB, 2 * H8, TOPK])
        places = sbuf("places", [P, 2, 512])
        FV = sbuf("FV", [P, TB, H8, TOPK])
        FI = sbuf("FI", [P, TB, H8, TOPK], U32)
        HL = sbuf("HL", [P, 2, TB, H8, TOPK])
        ident = sbuf("ident", [P, P])
        iota = sbuf("iota", [P, P])
        zeros = sbuf("zeros", [P, 512], BF16)
        pT = sbuf("pT", [P, 2, T])
        cols = sbuf("cols", [P, 37])
        col = sbuf("col", [P, 6, 16])
        stats = sbuf("stats", [P, 16, 6])
        mv = sbuf("mv", [P, 16, 2])

        def buf(at, *shape):
            n = int(np.prod(shape))
            v = big[:, at:at + n]
            if len(shape) == 1:
                return v
            names = "abcd"[:len(shape)]
            return v.rearrange(f"p ({' '.join(names)}) -> p {' '.join(names)}",
                               **{k: s for k, s in zip(names, shape)})

        BK = 2048
        acc = ps[:, 0:4, :]

        def acc_rows(tb):
            return ps[:, 2 * tb:2 * tb + 2, :].rearrange("p a b -> p (a b)")

        def bank(s):
            return ps[:, 4 + s % 4, :]

        rows = SC[:, 2 * 1024:4 * 1024].rearrange("p (r n) -> p r n", r=2)
        onehot = SC[:, 0:2048].rearrange("p (w b t n) -> p w b t n", w=2, b=2, t=4)
        staged = SC[:, 0:2048].rearrange("p (s t) -> p s t", s=8)
        expert_tokens = big[:, :].rearrange("p (e t) -> p t e", t=T)
        TI = places[:, 0, :].bitcast(U32).rearrange("p (t c k) -> p t c k", t=TB, k=TOPK)
        TIf = places[:, 1, :].rearrange("p (t c k) -> p t c k", t=TB, k=TOPK)
        route_T = places[:, :, :].rearrange("p a b -> p (a b)")[:, 0:3 * T].rearrange("p (r t) -> p r t", r=3)
        TI_halves = [places[:, 0, k * T:(k + 1) * T].bitcast(U32) for k in range(2)]
        TV_routes = [TV[:].rearrange("p t c k -> p (t c k)")[:, k * T:(k + 1) * T]
                     .rearrange("p (t h k) -> p t h k", t=TB, h=H8) for k in range(2)]

        tile_landed = [sem(f"tile_landed{i}") for i in range(RING)]
        tiles_begun = sem("tiles_begun")
        slot_full = [sem(f"slot_full{i}") for i in range(4)]
        slot_moved = [sem(f"slot_moved{i}") for i in range(4)]
        acc_full = sem("acc_full")
        acc_moved = sem("acc_moved")
        turn_ready = sem("turn_ready")
        act_step = sem("act_step")
        dve_step = sem("dve_step")
        pool_step = sem("pool_step")
        sqrt_wanted = sem("sqrt_wanted")
        sqrt_done = sem("sqrt_done")
        xt_in = sem("xt_in")
        x_in = sem("x_in")
        gate_w_in = sem("gate_w_in")
        consts_in = sem("consts_in")
        rows_in = sem("rows_in")
        rows_used = sem("rows_used")
        p_in = sem("p_in")
        rope_in = sem("rope_in")
        mix_in = sem("mix_in")
        na_bias_in = sem("na_bias_in")
        zeros_set = sem("zeros_set")
        gates_split = sem("gates_split")
        gates_log = sem("gates_log")
        gates_scanned = sem("gates_scanned")
        floor_ready = sem("floor_ready")
        gate_cols_ready = sem("gate_cols_ready")
        decay_ready = sem("decay_ready")
        ones_set = sem("ones_set")
        sums_ready = sem("sums_ready")
        angles_ready = sem("angles_ready")
        sines_ready = sem("sines_ready")
        latents_ready = sem("latents_ready")
        rope_ready = sem("rope_ready")
        maxima_ready = sem("maxima_ready")
        exps_ready = sem("exps_ready")
        probs_ready = sem("probs_ready")
        probs_turned = sem("probs_turned")
        logits_wanted = sem("logits_wanted")
        logits_ready = sem("logits_ready")
        routes_ready = sem("routes_ready")
        softmax_wanted = sem("softmax_wanted")
        softmax_exps = sem("softmax_exps")
        gate_rows = sem("gate_rows")
        rows_staged = sem("rows_staged")
        silu_ready = sem("silu_ready")
        side_ready = sem("side_ready")
        decay_wanted = sem("decay_wanted")
        out_ready = sem("out_ready")
        stored = sem("stored")

        def tile_here(pe, i, turns=0):
            pe.wait_ge(tile_landed[i % RING], turns * 16 + 16 * (i // RING + 1))

        def tile(i):
            return ring[:, i % RING, :]

        def tall(i):
            return ring[:, i % RING, :].rearrange("p (k n) -> p k n", k=KC)

        def slot_free(pe, s, turns=0):
            if s >= 4:
                pe.wait_ge(slot_moved[s % 4], turns + s // 4)

        def slot_here(eng, s, turns=0):
            eng.wait_ge(slot_full[s % 4], turns + s // 4 + 1)

        def moved(eng, s, n=1):
            for k in range(max(s, s + n - 4), s + n):
                eng.wait_ge(slot_moved[k % 4], k // 4 + 1)

        def full(ins, s):
            return ins.then_inc(slot_full[s % 4], 1)

        def free(ins, s):
            return ins.then_inc(slot_moved[s % 4], 1)

        def acc_here(eng, name):
            eng.wait_ge(acc_full, ACC[name] + 1)

        def acc_gone(eng, name):
            eng.wait_ge(acc_moved, ACC[name] + 1)

        def head_rows(h):
            return slice(64 * (h % 2), 64 * (h % 2) + 64)

        class Steps:

            def __init__(self, eng, s):
                self.eng, self.sem, self.n = eng, s, 0

            def __call__(self, ins):
                ins.then_inc(self.sem, 1)
                self.n += 1

            def wait(self):
                self.eng.wait_ge(self.sem, self.n)

        ml_qk = buf(0, KC, T)
        ml_v = buf(BK, TB, H8, 129)
        ml_sig = buf(3 * BK, TB, D)
        ml_raw = buf(4 * BK, TB, H8, 129)
        ml_hn = buf(6 * BK, TB, D)
        ml_outT = buf(7 * BK, KC, T)
        ml_w = buf(8 * BK, 2, 384)
        ml_p = buf(8 * BK + 768, 2, 384)
        ml_rows = buf(9 * BK, 14, T)
        ml_sel = buf(11 * BK, H8, P)
        ml_gate_w = buf(12 * BK, KC, 16)
        ml_bias = buf(12 * BK + 128, 2)
        ml_mask = buf(12 * BK + 256, P)
        gate_cols = buf(13 * BK, 4, H8)
        ple_sig = buf(3 * BK, TB, D)
        ple_side = buf(4 * BK, TB, D)
        peer_q = big[:, 112 * T:128 * T].rearrange("p (j t) -> p j t", t=T)
        latent = buf(0, TB, 704)
        latT = buf(BK, 6, T)
        k_nope = buf(2 * BK, H8, T)
        mla_v = buf(3 * BK, TB, D)
        q_nope = buf(4 * BK, H8, T)
        q_rope = buf(5 * BK, TB, 2, H8, 32)
        q_rot = buf(5 * BK + 1024, TB, H8, 2, 32)
        q_ropeT = buf(6 * BK, 4, T)
        rope_k2 = buf(6 * BK + 1024, TB, 2, 2, 32)
        rope_tmp = buf(6 * BK + 1280, 2, 256)
        mla_oT = buf(7 * BK, H8, T)
        mla_p = buf(8 * BK, 2, 384)
        mla_pT = buf(8 * BK + 768, 2, 384)
        angle = buf(9 * BK, 2, TB, 32)
        turns_ = buf(9 * BK + 128, 2, TB, 32)
        sincos = buf(9 * BK + 256, 2, TB, 32)
        inv_freq = buf(9 * BK + 384, 32)
        pos_i = big[:, 9 * BK + 416:9 * BK + 418].bitcast(I32)
        pos_f = buf(9 * BK + 420, TB)
        mla_mask = buf(9 * BK + 512, P)
        sq_junk = buf(10 * BK, D)
        actT = buf(0, FF_TILES, T)
        silu_g = buf(3 * BK, 4, T)
        xn = buf(4 * BK, TB, D)
        na_bias = buf(5 * BK, TB, H8, 4, 64)
        post_tmp = buf(7 * BK, TB, D)
        rqk = buf(0, TB, 2 * RET_H, 2, 64)
        rqk_rot = buf(BK, TB, 2 * RET_H, 2, 64)
        rqkT = buf(2 * BK, 2 * RET_H, T)
        ret_v = buf(3 * BK, TB, D)
        ret_g = buf(4 * BK, TB, D)
        na_qk = buf(7 * BK, KC, T)
        na_v = buf(8 * BK, TB, 512)
        ret_cos = buf(8 * BK + 1024, TB, 64)
        ret_sin = buf(8 * BK + 1152, TB, 64)
        na_colmask = buf(8 * BK + 1280, 64)
        ret_logit = buf(8 * BK + 1344, 2 * RET_H)
        ret_lg = buf(8 * BK + 1352, 4, 2 * RET_H)
        sig_ret = buf(9 * BK, TB, D)
        sig_na = buf(10 * BK, TB, D)
        ret_y = buf(11 * BK, TB, RET_H, 256)
        ret_d = buf(12 * BK, 2, 512)
        ret_p = buf(12 * BK + 1024, 2, 512)
        na_s = buf(13 * BK, 2, 512)
        na_pT = buf(13 * BK + 1024, 2, 512)
        na_oT = buf(14 * BK, 4, T)
        ret_up = buf(14 * BK + 1024, 512)
        ret_down = buf(15 * BK, 512)
        rot_tmp = buf(15 * BK + 512, 2, 512)
        ret_junk = buf(13 * BK, 256)
        merged = buf(0, TB, D)
        merged_tmp = buf(BK, TB, D)
        ret_yT = buf(2 * BK, KC, T)
        mergedT = buf(3 * BK, KC, T)
        GAIN_ML, GAIN_KV, GAIN_Q, GAIN_FFN1, GAIN_MIX, GAIN_FFN2 = 0, 8, 10, 13, 21, 29

        CONSTS = [(ident[:], "ident"), (iota[:], "iota"), (ml_sel[0:H8], "ml_sel"), (ml_mask, "ml_mask"),
                  (cols[:], "cols")]
        CONST_LOADS = len(CONSTS)

        block = ctx.enter_context(nc.Block())

        @block.sync
        def _(sp):
            def stream(name, w):
                n, base, width = w.shape[0], TILE[name], w.shape[2]
                looped = n - n % RING if n >= 3 * RING else 0
                if looped:
                    with sp.Fori(0, looped // RING, 1) as turns:
                        for j in range(RING):
                            i = base + j
                            sp.wait_ge(tiles_begun, turns * RING + (i - RING + 2))
                            sp.dma_start(tile(i)[:, 0:width], w[ds(turns * RING + j, 1), :, :]
                                         .rearrange("a p n -> p (a n)")).then_inc(tile_landed[i % RING], 16)
                for j in range(looped, n):
                    i = base + j
                    if i >= RING:
                        sp.wait_ge(tiles_begun, i - RING + 2)
                    sp.dma_start(tile(i)[:, 0:width], w[j]).then_inc(tile_landed[i % RING], 16)

            for name, _n in STREAM:
                stream(name, a[name])
            sp.wait_ge(out_ready, 1)
            sp.dma_start(out, X[:]).then_inc(stored, 16)
            sp.wait_ge(stored, 16)

        @block.gpsimd
        def _(pool):
            step = Steps(pool, pool_step)
            nc.gpsimd.memset(zeros[:], 0.0).then_inc(zeros_set, 1)
            nc.gpsimd.memset(ml_v[:, :, :, 128:129], 1.0).then_inc(ones_set, 1)

            def load_rows(k, wait=None):
                if k:
                    pool.wait_ge(rows_used, k)
                if wait:
                    pool.wait_ge(*wait)
                for r in range(ROW_SETS[k]):
                    pool.dma_start(rows[:, r, :], a[f"rows{k}"][r:r + 1, :].to_broadcast([P, D])).then_inc(rows_in, 16)

            load_rows(0)
            pool.dma_start(pT[:], a["p0"]).then_inc(p_in, 16)
            load_rows(1, (routes_ready, 1))
            load_rows(2)
            pool.wait_ge(acc_full, ACC["ple_gate0"] + 1)
            pool.dma_start(pT[:], a["p1"]).then_inc(p_in, 16)
            load_rows(3, (routes_ready, 2))
            load_rows(4)
            pool.wait_ge(turn_ready, TURN["rms1"] + 1)
            for tb in range(TB):
                for r in range(2):
                    first = 3 - (2 * tb + r)
                    pool.dma_start(na_bias[64 * r:64 * r + 64, tb], a["na_bias"][:, :, first:first + 4, :]
                                   ).then_inc(na_bias_in, 16)
            for dst, name in ((ret_cos, "ret_cos"), (ret_sin, "ret_sin"), (na_colmask, "na_colmask"),
                              (ret_logit, "ret_logit"), (ret_up, "ret_up"), (ret_down, "ret_down")):
                src = a[name] if name != "ret_logit" else a[name].to_broadcast([P, 2 * RET_H])
                pool.dma_start(dst, src).then_inc(mix_in, 16)
            load_rows(5)
            load_rows(6)

        @block.tensor
        def _(pe):
            def begins_tile(mm):
                mm.then_inc(tiles_begun, 1)

            def to_acc(name, lhs, n, width=D, per_tile=1):
                if ACC[name]:
                    pe.wait_ge(acc_moved, ACC[name])
                halves = [(f, min(512, width - 512 * f)) for f in range((width + 511) // 512)]
                for k in range(n):
                    i = TILE[name] + k // per_tile
                    first = k % per_tile == 0
                    if first:
                        tile_here(pe, i)
                    w = tile(i)[:, (k % per_tile) * width:(k % per_tile + 1) * width]
                    for tb in range(TB):
                        for f, cnt in halves:
                            mm = nc.tensor.matmul(acc[:, 2 * tb + f, 0:cnt], lhs(k, tb),
                                                  w[:, 512 * f:512 * f + cnt],
                                                  start=(k == 0), stop=(k == n - 1))
                            if first:
                                begins_tile(mm)
                            first = False
                mm.then_inc(acc_full, 1)

            def from_tall(i, s, src, turns=0):
                tile_here(pe, i, turns)
                slot_free(pe, s, turns * 2 if not isinstance(turns, int) else 0)
                for k in range(KC):
                    mm = nc.tensor.matmul(bank(s)[:, 0:T], tall(i)[:, k, :], src[:, k, :],
                                          start=(k == 0), stop=(k == KC - 1))
                    if k == 0:
                        begins_tile(mm)
                full(mm, s)

            def turn_over(name, src, width=P):
                pe.wait_ge(turn_ready, TURN[name] + 1)
                for q in range(4):
                    s = SLOT[f"turn_{name}"] + q
                    slot_free(pe, s)
                    for c in range(2):
                        for tb in range(TB):
                            at = (2 * q + c) * P
                            mm = nc.tensor.transpose(bank(s)[:, (2 * c + tb) * P:(2 * c + tb + 1) * P],
                                                     src[:, tb, at:at + P], ident[:])
                    full(mm, s)

            def tokens(src):
                return lambda k, tb: src[:, k, tb * P:(tb + 1) * P]

            pe.wait_ge(consts_in, 16 * CONST_LOADS)
            pe.wait_ge(xt_in, 16)
            pe.wait_ge(gate_w_in, 32)
            pe.wait_ge(zeros_set, 1)
            s = SLOT["gates"]
            for g in range(2):
                for k in range(KC):
                    mm = nc.tensor.matmul(bank(s)[0:H8, g * T:(g + 1) * T], ml_gate_w[:, k, g * H8:(g + 1) * H8],
                                          XT[:, k, :], start=(k == 0), stop=(k == KC - 1))
            full(mm, s)
            for j in range(8):
                from_tall(TILE["a_qk"] + j, SLOT["a_qk"] + j, XT)
            to_acc("a_v", tokens(XT), KC)
            to_acc("a_og", tokens(XT), KC)
            pe.wait_ge(gates_scanned, 1)
            pe.wait_ge(floor_ready, 1)
            s = SLOT["gate_cols"]
            slot_free(pe, s)
            for c, row in ((0, 6), (2, 9)):
                for tb in range(TB):
                    mm = nc.tensor.matmul(bank(s)[:, (c + tb) * H8:(c + tb + 1) * H8],
                                          ml_rows[0:H8, row, tb * P:(tb + 1) * P], ident[0:H8, 0:H8],
                                          start=True, stop=True)
            full(mm, s)

            def ml_first(h):
                s = SLOT[("ml", "decay", h)]
                slot_free(pe, s)
                nc.tensor.matmul(bank(s)[:, 0:T], ml_sel[0:H8, h, :], ml_rows[0:H8, 7, :], start=True, stop=False)
                nc.tensor.matmul(bank(s)[:, 0:P], ident[:], ml_mask[:], start=False, stop=True)
                nc.tensor.matmul(bank(s)[:, T:T + P], ml_sel[0:H8, h, :], ml_rows[0:H8, 7, P:T],
                                 start=True, stop=False)
                full(nc.tensor.matmul(bank(s)[:, T:T + P], ident[:], ml_mask[:], start=False, stop=True), s)
                s = SLOT[("ml", "scores", h)]
                slot_free(pe, s)
                r, q, k = head_rows(h), h // 2, 4 + h // 2
                nc.tensor.matmul(bank(s)[:, 0:T], ml_qk[r, k, 0:P], ml_qk[r, q, :], start=True, stop=True)
                full(nc.tensor.matmul(bank(s)[:, T:T + P], ml_qk[r, k, P:T], ml_qk[r, q, P:T],
                                      start=True, stop=True), s)

            moved(pe, SLOT["a_qk"], 8)
            acc_gone(pe, "a_v")
            pe.wait_ge(ones_set, 1)
            ml_first(0)
            for h in range(H8):
                if h + 1 < H8:
                    ml_first(h + 1)
                moved(pe, SLOT[("ml", "scores", h)])
                s = SLOT[("ml", "out", h)]
                slot_free(pe, s)
                w = ml_p[:, h % 2]
                nc.tensor.matmul(bank(s)[:, 0:129], w[:, 0:P], ml_v[:, 0, h, :], start=True, stop=True)
                nc.tensor.matmul(bank(s)[:, T:T + 129], w[:, P:T], ml_v[:, 0, h, :], start=True, stop=False)
                full(nc.tensor.matmul(bank(s)[:, T:T + 129], w[:, T:T + P], ml_v[:, 1, h, :],
                                      start=False, stop=True), s)
            turn_over("ml_out", ml_hn)
            moved(pe, SLOT["turn_ml_out"], 4)
            to_acc("a_out", tokens(ml_outT), KC)

            def peer(layer):
                turn_over(f"ln{layer}_0", X)
                moved(pe, SLOT[f"turn_ln{layer}_0"], 4)
                for j in range(16):
                    from_tall(TILE[f"wq{layer}"] + j, SLOT[f"wq{layer}"] + j, XT)
                moved(pe, SLOT[f"wq{layer}"], 16)
                for half in range(2):
                    i = TILE[f"keys{layer}"] + half
                    tile_here(pe, i)
                    for tb in range(TB):
                        for g in range(2):
                            s = SLOT[f"scores{layer}"] + 4 * half + 2 * tb + g
                            slot_free(pe, s)
                            for j in range(4):
                                mm = nc.tensor.matmul(bank(s)[:, j * P:(j + 1) * P],
                                                      peer_q[:, 8 * half + 4 * g + j, tb * P:(tb + 1) * P],
                                                      tall(i)[:, 4 * g + j, :], start=True, stop=True)
                                if tb == 0 and g == 0 and j == 0:
                                    begins_tile(mm)
                            full(mm, s)
                base, sbase = TILE[f"u{layer}"], SLOT[f"u{layer}"]
                with pe.Fori(0, EXPERT_TILES // RING, 1) as turns:
                    for j in range(RING):
                        from_tall(base + j, sbase + j, XT, turns)
                pe.wait_ge(routes_ready, layer + 1)
                for q in range(2):
                    s = SLOT[f"routes{layer}"] + q
                    slot_free(pe, s)
                    for k, src in enumerate(((TV_routes[0], TV_routes[1]), (FV,))[q]):
                        for tb in range(TB):
                            mm = nc.tensor.transpose(bank(s)[:, (2 * k + tb) * P:(2 * k + tb + 1) * P],
                                                     src[:, tb].rearrange("p h k -> p (h k)"), ident[:])
                    full(mm, s)
                sbase = SLOT[f"gates{layer}"]
                with pe.Fori(0, T // 16, 1) as turns:
                    for k in range(4):
                        slot_free(pe, sbase + k, turns)
                        pe.wait_ge(gate_rows, turns * 4 + (64 * layer + k + 1))
                        for t in range(4):
                            mm = nc.tensor.matmul(bank(sbase + k)[:, t * P:(t + 1) * P], onehot[:, 1, k % 2, t],
                                                  onehot[:, 0, k % 2, t], start=True, stop=True)
                        full(mm, sbase + k)
                pe.wait_ge(acc_moved, ACC[f"v{layer}"])
                for b in range(4):
                    nc.tensor.matmul(acc[:, b, :], zeros[:, 0:P], zeros[:], start=True, stop=False)
                base = TILE[f"v{layer}"]
                with pe.Fori(0, EXPERT_TILES // RING, 1) as turns:
                    for j in range(RING):
                        tile_here(pe, base + j, turns)
                        pe.wait_ge(rows_staged, turns * RING + (EXPERT_TILES * layer + j + 1))
                        for tb in range(TB):
                            for f in range(2):
                                mm = nc.tensor.matmul(acc[:, 2 * tb + f, :], staged[:, j, tb * P:(tb + 1) * P],
                                                      tile(base + j)[:, 512 * f:512 * f + 512],
                                                      start=False, stop=False)
                                if tb == 0 and f == 0:
                                    begins_tile(mm)
                for b in range(4):
                    mm = nc.tensor.matmul(acc[:, b, :], zeros[:, 0:P], zeros[:], start=False, stop=True)
                mm.then_inc(acc_full, 1)
                pe.wait_ge(p_in, 16 * (layer + 1))
                to_acc(f"ple_proj{layer}", tokens(pT), 2)
                turn_over(f"ln{layer}_1", X)
                moved(pe, SLOT[f"turn_ln{layer}_1"], 4)
                to_acc(f"ple_gate{layer}", tokens(XT), KC)

            peer(0)

            turn_over("x1", X)
            moved(pe, SLOT["turn_x1"], 4)
            to_acc("kv_q_down", tokens(XT), KC, width=704)
            pe.wait_ge(latents_ready, 1)
            for q, parts in enumerate((((0, 0), (P, 1)), ((320, 0), (320 + P, 1)), ((320 + 2 * P, 0), (None, 1)))):
                s = SLOT["latents"] + q
                slot_free(pe, s)
                for at, c in parts:
                    for tb in range(TB):
                        src = latent[:, tb, at:at + P] if at is not None else \
                            rope_k2[:, tb].rearrange("p a b c -> p (a b c)")
                        mm = nc.tensor.transpose(bank(s)[:, (2 * c + tb) * P:(2 * c + tb + 1) * P], src, ident[:])
                full(mm, s)
            moved(pe, SLOT["latents"], 3)

            def up(name, lat, n):
                for k in range(n):
                    tile_here(pe, TILE[name] + k)
                for h in range(H8):
                    s = SLOT[name] + h
                    slot_free(pe, s)
                    for k in range(n):
                        if k == n - 1 and h == H8 - 1:
                            begins_tile(nc.tensor.matmul(bank(s)[:, 511:512], zeros[:, 0:P], zeros[:, 0:1],
                                                         start=False, stop=False, skip_group_check=True))
                        mm = nc.tensor.matmul(bank(s)[:, 0:T], tile(TILE[name] + k)[:, h * P:(h + 1) * P],
                                              latT[:, lat + k, :], start=(k == 0), stop=(k == n - 1))
                        if (k == 0 and h == 0) or (0 < k < n - 1 and h == H8 - 1):
                            begins_tile(mm)
                    full(mm, s)

            up("up_k", 0, 2)
            to_acc("up_v", lambda k, tb: latT[:, k, tb * P:(tb + 1) * P], 2)
            up("uq_nope", 2, 3)
            to_acc("uq_rope", lambda k, tb: latT[:, 2 + k, tb * P:(tb + 1) * P], 3, width=512)
            pe.wait_ge(rope_ready, 1)
            for q in range(2):
                s = SLOT["rope"] + q
                slot_free(pe, s)
                for c in range(2):
                    for tb in range(TB):
                        src = q_rot[:, tb].rearrange("p a b c -> p (a b c)")[:, (2 * q + c) * P:(2 * q + c + 1) * P]
                        mm = nc.tensor.transpose(bank(s)[:, (2 * c + tb) * P:(2 * c + tb + 1) * P], src, ident[:])
                full(mm, s)

            def mla_scores(h):
                s = SLOT[("mla", "scores", h)]
                slot_free(pe, s)
                r = head_rows(h)
                for tb in range(TB):
                    n, at = (tb + 1) * P, tb * P
                    o = bank(s)[:, at:at + n]
                    nc.tensor.matmul(o, q_nope[:, h, at:at + P], k_nope[:, h, 0:n], start=True, stop=False)
                    nc.tensor.matmul(o, q_ropeT[r, h // 2, at:at + P], latT[r, 5, 0:n], start=False, stop=False)
                    mm = nc.tensor.matmul(o[:, at:at + P], ident[:], mla_mask[:], start=False, stop=True)
                full(mm, s)

            moved(pe, SLOT["up_k"], 8)
            moved(pe, SLOT["uq_nope"], 8)
            moved(pe, SLOT["rope"], 2)
            acc_gone(pe, "up_v")
            pe.wait_ge(rope_in, 48)
            mla_scores(0)
            for h in range(H8):
                if h + 1 < H8:
                    mla_scores(h + 1)
                pe.wait_ge(probs_ready, h + 1)
                s = SLOT[("mla", "probs", h)]
                slot_free(pe, s)
                for k in range(3):
                    mm = nc.tensor.transpose(bank(s)[:, k * P:(k + 1) * P], mla_p[:, h % 2, k * P:(k + 1) * P],
                                             ident[:])
                full(mm, s)
                moved(pe, s)
                s = SLOT[("mla", "out", h)]
                slot_free(pe, s)
                nc.tensor.matmul(bank(s)[:, 0:T], mla_v[:, 0, h * P:(h + 1) * P], mla_pT[:, h % 2, 0:T],
                                 start=True, stop=False)
                full(nc.tensor.matmul(bank(s)[:, P:T], mla_v[:, 1, h * P:(h + 1) * P], mla_pT[:, h % 2, T:T + P],
                                      start=False, stop=True), s)
            moved(pe, SLOT[("mla", "out", H8 - 1)])
            to_acc("b_out", lambda k, tb: mla_oT[:, k, tb * P:(tb + 1) * P], KC)
            peer(1)

            def ffn(n):
                base, sbase = TILE[f"ffn{n}_in"], SLOT[f"ffn{n}"]
                looped = 2 * FF_TILES // RING
                with pe.Fori(0, looped, 1) as turns:
                    for j in range(RING):
                        from_tall(base + j, sbase + j, XT, turns)
                for j in range(looped * RING, 2 * FF_TILES):
                    from_tall(base + j, sbase + j, XT)
                moved(pe, sbase, 2 * FF_TILES)
                to_acc(f"ffn{n}_out", tokens(actT), FF_TILES)

            turn_over("rms1", xn)
            moved(pe, SLOT["turn_rms1"], 4)
            ffn(1)

            turn_over("rms2", xn)
            moved(pe, SLOT["turn_rms2"], 4)
            to_acc("rqk", tokens(XT), KC)
            to_acc("rv", tokens(XT), KC)
            to_acc("rg", tokens(XT), KC)
            for j in range(8):
                from_tall(TILE["nqk"] + j, SLOT["nqk"] + j, XT)
            to_acc("nv", tokens(XT), KC, width=512, per_tile=2)
            to_acc("g_ret", tokens(XT), KC)
            to_acc("g_na", tokens(XT), KC)
            turn_over("rqk", rqk_rot.rearrange("p t h a b -> p t (h a b)"))
            moved(pe, SLOT["turn_rqk"], 4)

            def ret_scores(h):
                s = SLOT[("ret", "scores", h)]
                slot_free(pe, s)
                for m in range(TB):
                    mm = nc.tensor.matmul(bank(s)[:, m * T:(m + 1) * T], rqkT[:, RET_H + h, m * P:(m + 1) * P],
                                          rqkT[:, h, :], start=True, stop=True)
                full(mm, s)

            acc_gone(pe, "rv")
            ret_scores(0)
            for h in range(RET_H):
                if h + 1 < RET_H:
                    ret_scores(h + 1)
                moved(pe, SLOT[("ret", "scores", h)])
                s = SLOT[("ret", "out", h)]
                slot_free(pe, s)
                for tb in range(TB):
                    for m in range(TB):
                        at = m * T + tb * P
                        mm = nc.tensor.matmul(bank(s)[:, tb * T:(tb + 1) * T], ret_p[:, h % 2, at:at + P],
                                              ret_v[:, m, h * T:(h + 1) * T], start=(m == 0), stop=(m == 1))
                full(mm, s)

            def na_scores(h):
                s = SLOT[("na", "scores", h)]
                slot_free(pe, s)
                r = head_rows(h)
                for tb in range(TB):
                    mm = nc.tensor.matmul(bank(s)[:, tb * T:(tb + 1) * T], na_qk[r, h // 2, tb * P:(tb + 1) * P],
                                          na_qk[r, 4 + h // 2, :], start=True, stop=True)
                full(mm, s)

            moved(pe, SLOT["nqk"], 8)
            acc_gone(pe, "nv")
            na_scores(0)
            for h in range(H8):
                if h + 1 < H8:
                    na_scores(h + 1)
                pe.wait_ge(probs_ready, H8 + h + 1)
                s = SLOT[("na", "probs", h)]
                slot_free(pe, s)
                for m in range(TB):
                    for tb in range(TB):
                        mm = nc.tensor.transpose(bank(s)[:, (2 * m + tb) * P:(2 * m + tb + 1) * P],
                                                 na_s[:, h % 2, tb * T + m * P:tb * T + (m + 1) * P], ident[:])
                full(mm, s)
                moved(pe, s)
                s = SLOT[("na", "out", h)]
                slot_free(pe, s)
                for m in range(TB):
                    mm = nc.tensor.matmul(bank(s)[head_rows(h), 0:T], na_v[:, m, h * 64:(h + 1) * 64],
                                          na_pT[:, h % 2, m * T:(m + 1) * T], start=(m == 0), stop=(m == 1))
                full(mm, s)
            turn_over("ret", ret_y.rearrange("p t h n -> p t (h n)"))
            moved(pe, SLOT["turn_ret"], 4)
            to_acc("ret_out", tokens(ret_yT), KC)
            moved(pe, SLOT[("na", "out", H8 - 1)])
            to_acc("na_out", tokens(na_oT), 4)
            turn_over("merged", merged)
            moved(pe, SLOT["turn_merged"], 4)
            to_acc("mix_out", tokens(mergedT), KC)
            turn_over("rms3", xn)
            moved(pe, SLOT["turn_rms3"], 4)
            ffn(2)

        @block.scalar
        def _(act):
            step = Steps(act, act_step)
            sqrts = [0]
            S = nc.scalar

            def square_roots(n):
                sqrts[0] += 1
                act.wait_ge(sqrt_wanted, sqrts[0])
                S.activation(col[:, 1, 0:n], col[:, 0, 0:n], ACT.Sqrt).then_inc(sqrt_done, 1)

            def turned(name, dst, gain=None):
                for q in range(2):
                    s = SLOT[f"turn_{name}"] + q
                    slot_here(act, s)
                    if gain is None:
                        free(S.copy(dst[:, 2 * q:2 * q + 2, :].rearrange("p a b -> p (a b)"), bank(s)), s)
                    else:
                        for c in range(2):
                            k = 2 * q + c
                            ins = S.mul(dst[:, k, :], bank(s)[:, c * T:(c + 1) * T], cols[:, gain + k:gain + k + 1])
                            if c == 0:
                                step(ins)
                        free(ins, s)

            def from_slots(name, dst, n):
                for j in range(n):
                    s = SLOT[name] + j
                    slot_here(act, s)
                    free(S.copy(dst[:, j, :], bank(s)[:, 0:T]), s)

            def from_acc(name, dst, func, width=D):
                acc_here(act, name)
                for tb in range(TB):
                    ins = S.activation(dst(tb), acc_rows(tb)[:, 0:width], func)
                    if tb == 0:
                        step(ins)
                step.wait()
                ins.then_inc(acc_moved, 1)

            act.dma_start(XT[:], a["xT"]).then_inc(xt_in, 16)
            act.dma_start(ml_gate_w, a["ml_gate_w"]).then_inc(gate_w_in, 16)
            act.dma_start(ml_bias[0:H8, :], a["ml_bias"]).then_inc(gate_w_in, 16)
            for dst, name in CONSTS:
                act.dma_start(dst, a[name]).then_inc(consts_in, 16)
            act.dma_start(X[:], a["x"]).then_inc(x_in, 16)

            def log_sigmoid_part(dst, src, tmp):
                step(S.activation(tmp, src, ACT.Abs))
                step.wait()
                step(S.activation(tmp, tmp, ACT.Exp, scale=-1.0))
                step.wait()
                return S.activation(dst, tmp, ACT.Ln, bias=1.0)

            act.wait_ge(gates_split, 1)
            log_sigmoid_part(ml_rows[0:H8, 2, :], ml_rows[0:H8, 1, :], ml_rows[0:H8, 3, :]).then_inc(gates_log, 1)
            from_slots("a_qk", ml_qk, 8)
            acc_here(act, "a_v")
            for tb in range(TB):
                ins = S.copy(ml_v[:, tb, :, 0:P], acc_rows(tb).rearrange("p (h n) -> p h n", h=H8))
                if tb == 0:
                    step(ins)
            step.wait()
            ins.then_inc(acc_moved, 1)
            act.wait_ge(gates_scanned, 1)
            S.activation(ml_rows[0:H8, 9, :], ml_rows[0:H8, 8, :], ACT.Exp, scale=-1.0).then_inc(floor_ready, 1)
            from_acc("a_og", lambda tb: ml_sig[:, tb, :], ACT.Sigmoid)
            act.wait_ge(gate_cols_ready, 1)

            def ml_decay(h):
                s = SLOT[("ml", "decay", h)]
                slot_here(act, s)
                if h >= 2:
                    moved(act, SLOT[("ml", "scores", h - 2)])
                step(S.activation(ml_w[:, h % 2, 0:T], bank(s)[:, 0:T], ACT.Exp, scale=-1.0,
                                  bias=gate_cols[:, 0, h:h + 1]))
                step.wait()
                ins = S.activation(ml_w[:, h % 2, T:T + P], bank(s)[:, T:T + P], ACT.Exp, scale=-1.0,
                                   bias=gate_cols[:, 1, h:h + 1])
                free(ins, s)

            ml_decay(0)
            for h in range(H8):
                if h + 1 < H8:
                    ml_decay(h + 1)
                s = SLOT[("ml", "out", h)]
                slot_here(act, s)
                free(S.copy(ml_raw[:, :, h, :], bank(s).rearrange("p (t n) -> p t n", t=TB)[:, :, 0:129]), s)
            square_roots(16)
            turned("ml_out", ml_outT, GAIN_ML)
            square_roots(2)

            def peer(layer):
                turned(f"ln{layer}_0", XT)
                from_slots(f"wq{layer}", peer_q, 16)
                for half in range(2):
                    for tb in range(TB):
                        for g in range(2):
                            s = SLOT[f"scores{layer}"] + 4 * half + 2 * tb + g
                            slot_here(act, s)
                            at = tb * 2048 + (8 * half + 4 * g) * P
                            free(S.copy(SC[:, at:at + 512], bank(s)), s)
                base = SLOT[f"u{layer}"]
                with act.Fori(0, EXPERT_TILES // RING, 1) as turns:
                    for j in range(RING):
                        slot_here(act, base + j, turns * 2)
                        free(S.activation(big[:, ds(turns * (RING * T) + j * T, T)], bank(base + j)[:, 0:T],
                                          ACT.Gelu), base + j)
                act.wait_ge(softmax_wanted, layer + 1)
                S.activation(FV[:], FV[:], ACT.Exp).then_inc(softmax_exps, 1)
                square_roots(2)
                acc_here(act, f"ple_proj{layer}")
                for tb in range(TB):
                    ins = S.copy(ple_side[:, tb, :], acc_rows(tb))
                    if tb == 0:
                        step(ins)
                step.wait()
                ins.then_inc(acc_moved, 1)
                turned(f"ln{layer}_1", XT)
                from_acc(f"ple_gate{layer}", lambda tb: ple_sig[:, tb, :], ACT.Sigmoid)

            peer(0)

            act.wait_ge(turn_ready, TURN["x1"] + 1)
            act.dma_start(inv_freq, a["inv_freq"]).then_inc(rope_in, 16)
            act.dma_start(pos_i, a["positions"]).then_inc(rope_in, 16)
            act.dma_start(mla_mask, a["mla_mask"]).then_inc(rope_in, 16)
            turned("x1", XT)
            act.wait_ge(angles_ready, 1)
            S.activation(sincos.rearrange("p a b c -> p (a b c)"), angle.rearrange("p a b c -> p (a b c)"),
                         ACT.Sin).then_inc(sines_ready, 1)
            acc_here(act, "kv_q_down")
            for tb in range(TB):
                step(S.copy(latent[:, tb, :], acc_rows(tb)[:, 0:704]))
            for tb in range(TB):
                for k, (lo, hi) in enumerate(((0, KV_RANK), (KV_RANK + ROPE, 704))):
                    step.wait()
                    step(S.activation(sq_junk[:, 0:hi - lo], acc_rows(tb)[:, lo:hi], ACT.Square,
                                      accum_out=col[:, 2, 2 * tb + k:2 * tb + k + 1]))
            step.wait()
            act.sem_inc(sums_ready, 1)
            act.sem_inc(acc_moved, 1)
            square_roots(4)
            for q, parts in enumerate((((0, GAIN_KV), (1, GAIN_KV + 1)), ((2, GAIN_Q), (3, GAIN_Q + 1)),
                                       ((4, GAIN_Q + 2), (5, None)))):
                s = SLOT["latents"] + q
                slot_here(act, s)
                for c, (k, gain) in enumerate(parts):
                    src = bank(s)[:, c * T:(c + 1) * T]
                    ins = S.copy(latT[:, k, :], src) if gain is None else \
                        S.mul(latT[:, k, :], src, cols[:, gain:gain + 1])
                    if c == 0:
                        step(ins)
                free(ins, s)
            from_slots("up_k", k_nope, 8)
            from_acc("up_v", lambda tb: mla_v[:, tb, :], ACT.Copy)
            from_slots("uq_nope", q_nope, 8)
            acc_here(act, "uq_rope")
            for tb in range(TB):
                ins = S.copy(q_rope[:, tb].rearrange("p a h c -> p h a c"),
                             acc_rows(tb)[:, 0:512].rearrange("p (h a c) -> p h a c", h=H8, a=2))
                if tb == 0:
                    step(ins)
            step.wait()
            ins.then_inc(acc_moved, 1)
            for q in range(2):
                s = SLOT["rope"] + q
                slot_here(act, s)
                free(S.copy(q_ropeT[:, 2 * q:2 * q + 2, :].rearrange("p a b -> p (a b)"), bank(s)), s)

            def exponents(name, n, h, dst, parts, scale):
                act.wait_ge(maxima_ready, n + h + 1)
                for tb, (lo, hi) in enumerate(parts):
                    src = bank(SLOT[(name, "scores", h)]) if name == "mla" else na_s[:, h % 2]
                    step(S.activation(dst[:, h % 2, lo:hi], src[:, lo:hi], ACT.Exp, scale=scale,
                                      bias=col[:, 2 + h % 2, 8 + tb:9 + tb],
                                      accum_out=col[:, 4 + h % 2, tb:tb + 1]))
                step.wait()
                act.sem_inc(exps_ready, 1)

            def probs_over(name, h, dst, width):
                s = SLOT[(name, "probs", h)]
                slot_here(act, s)
                free(S.copy(dst[:, h % 2, :], bank(s)[:, 0:width]), s)

            exponents("mla", 0, 0, mla_p, ((0, P), (P, P + T)), MLA_SCALE)
            for h in range(H8):
                if h + 1 < H8:
                    exponents("mla", 0, h + 1, mla_p, ((0, P), (P, P + T)), MLA_SCALE)
                probs_over("mla", h, mla_pT, 384)
            square_roots(2)
            peer(1)

            def rms_of(src_ready, src, n=TB):
                act.wait_ge(*src_ready)
                for tb in range(n):
                    step.wait()
                    step(S.activation(sq_junk, src(tb), ACT.Square, accum_out=col[:, 2, tb:tb + 1]))
                step.wait()
                act.sem_inc(sums_ready, 1)

            def ffn(n):
                base, looped = SLOT[f"ffn{n}"], 2 * FF_TILES // RING

                def gate(j, turns=0):
                    s = base + 2 * j
                    slot_here(act, s, turns * 2 if not isinstance(turns, int) else 0)
                    before = s + 1 - 8
                    if not isinstance(turns, int):
                        act.wait_ge(slot_moved[before % 4], turns * 2 + (before // 4 + 1))
                    else:
                        act.wait_ge(slot_moved[before % 4], before // 4 + 1)
                    free(S.activation(silu_g[:, j % 4, :], bank(s)[:, 0:T], ACT.Silu), s)

                with act.Fori(0, looped, 1) as turns:
                    for j in range(4):
                        gate(j, turns)
                for j in range(4 * looped, FF_TILES):
                    gate(j)

            def post_norm(name):
                rms_of((acc_full, ACC[name] + 1), acc_rows)
                square_roots(2)

            rms_of((turn_ready, TURN["x2"] + 1), lambda tb: X[:, tb, :])
            square_roots(2)
            turned("rms1", XT, GAIN_FFN1)
            ffn(1)
            post_norm("ffn1_out")
            rms_of((rows_used, 5), lambda tb: X[:, tb, :])
            square_roots(2)
            turned("rms2", XT, GAIN_MIX)
            act.wait_ge(mix_in, 16 * 6)
            log_sigmoid_part(ret_lg[:, 1, :], ret_logit, ret_lg[:, 0, :]).then_inc(logits_ready, 1)
            from_acc("rqk", lambda tb: rqk[:, tb].rearrange("p h a b -> p (h a b)"), ACT.Copy)
            from_acc("rv", lambda tb: ret_v[:, tb, :], ACT.Copy)
            from_acc("rg", lambda tb: ret_g[:, tb, :], ACT.Silu)
            from_slots("nqk", na_qk, 8)
            from_acc("nv", lambda tb: na_v[:, tb, :], ACT.Copy, width=512)
            from_acc("g_ret", lambda tb: sig_ret[:, tb, :], ACT.Sigmoid)
            from_acc("g_na", lambda tb: sig_na[:, tb, :], ACT.Sigmoid)
            turned("rqk", rqkT)

            def ret_decay(h):
                act.wait_ge(decay_wanted, h + 1)
                S.activation(ret_d[:, h % 2, :], ret_d[:, h % 2, :], ACT.Exp).then_inc(decay_ready, 1)

            ret_decay(0)
            for h in range(RET_H):
                if h + 1 < RET_H:
                    ret_decay(h + 1)
                s = SLOT[("ret", "out", h)]
                slot_here(act, s)
                step(S.copy(ret_y[:, :, h, :], bank(s).rearrange("p (t n) -> p t n", t=TB)))
                for tb in range(TB):
                    step.wait()
                    step(S.activation(ret_junk, bank(s)[:, tb * T:(tb + 1) * T], ACT.Square,
                                      accum_out=col[:, 3, RET_H * tb + h:RET_H * tb + h + 1]))
                step.wait()
                act.sem_inc(slot_moved[s % 4], 1)
            act.sem_inc(sums_ready, 1)
            square_roots(8)
            exponents("na", H8, 0, na_s, ((0, T), (T, 2 * T)), 1.0)
            for h in range(H8):
                if h + 1 < H8:
                    exponents("na", H8, h + 1, na_s, ((0, T), (T, 2 * T)), 1.0)
                probs_over("na", h, na_pT, 512)
                s = SLOT[("na", "out", h)]
                slot_here(act, s)
                free(S.copy(na_oT[head_rows(h), h // 2, :], bank(s)[head_rows(h), 0:T]), s)
            turned("ret", ret_yT)
            turned("merged", mergedT)
            post_norm("mix_out")
            rms_of((rows_used, 6), lambda tb: X[:, tb, :])
            square_roots(2)
            turned("rms3", XT, GAIN_FFN2)
            ffn(2)
            post_norm("ffn2_out")

        @block.vector
        def _(dve):
            step = Steps(dve, dve_step)
            counts = {"sqrt": 0, "rows": 0, "sums": 0}
            V = nc.vector

            def tt(out, x, y, op):
                step(V.tensor_tensor(out, x, y, op))

            def ts(out, x, s1, s2, op0, op1=None):
                step(V.tensor_scalar(out, x, s1, s2, op0, op1) if op1 is not None
                     else V.tensor_scalar(out, x, s1, None, op0))

            def stt(out, x, s, y, op0, op1):
                step(V.scalar_tensor_tensor(out=out, in0=x, scalar=s, in1=y, op0=op0, op1=op1))

            def wait():
                step.wait()

            def inverse_roots(n):
                wait()
                dve.sem_inc(sqrt_wanted, 1)
                counts["sqrt"] += 1
                dve.wait_ge(sqrt_done, counts["sqrt"])
                step(V.reciprocal(col[:, 1, 0:n], col[:, 1, 0:n]))
                wait()

            def turned(name, dst, gain=None):
                for q in range(2, 4):
                    s = SLOT[f"turn_{name}"] + q
                    slot_here(dve, s)
                    if gain is None:
                        free(V.tensor_copy(dst[:, 2 * q:2 * q + 2, :].rearrange("p a b -> p (a b)"), bank(s)), s)
                    else:
                        for c in range(2):
                            k = 2 * q + c
                            ins = V.tensor_scalar(dst[:, k, :], bank(s)[:, c * T:(c + 1) * T],
                                                  cols[:, gain + k:gain + k + 1], None, ALU.mult)
                            if c == 0:
                                step(ins)
                        free(ins, s)

            def rows_here():
                counts["rows"] += 1
                dve.wait_ge(rows_in, 16 * sum(ROW_SETS[:counts["rows"]]))

            def layer_norm(name):
                acc_here(dve, name)
                for tb in range(TB):
                    stt(X[:, tb, :], X[:, tb, :], DN_ALPHA, acc_rows(tb), ALU.mult, ALU.add)
                wait()
                dve.sem_inc(acc_moved, 1)
                for tb in range(TB):
                    for f in range(2):
                        step(V.bn_stats(stats[:, 2 * tb + f, :], X[:, tb, 512 * f:512 * f + 512]))
                wait()
                for tb in range(TB):
                    step(V.bn_aggr(mv[:, tb, :], stats[:, 2 * tb:2 * tb + 2, :]))
                wait()
                ts(col[:, 0, 0:TB], mv[:, 0:TB, 1], NORM_EPS, None, ALU.add)
                inverse_roots(TB)
                rows_here()
                for tb in range(TB):
                    ts(X[:, tb, :], X[:, tb, :], mv[:, tb, 0:1], col[:, 1, tb:tb + 1], ALU.subtract, ALU.mult)
                wait()
                for tb in range(TB):
                    tt(X[:, tb, :], X[:, tb, :], rows[:, 0, :], ALU.mult)
                wait()
                for tb in range(TB):
                    tt(X[:, tb, :], X[:, tb, :], rows[:, 1, :], ALU.add)
                wait()
                dve.sem_inc(turn_ready, 1)
                dve.sem_inc(rows_used, 1)

            def mean_square_roots(n, width, eps, src=2):
                counts["sums"] += 1
                dve.wait_ge(sums_ready, counts["sums"])
                ts(col[:, 0, 0:n], col[:, src, 0:n], 1.0 / width, eps, ALU.mult, ALU.add)
                inverse_roots(n)

            def pre_norm():
                mean_square_roots(TB, D, RMS_EPS)
                for tb in range(TB):
                    ts(xn[:, tb, :], X[:, tb, :], col[:, 1, tb:tb + 1], None, ALU.mult)
                wait()
                dve.sem_inc(turn_ready, 1)

            def post_norm(name, weight):
                mean_square_roots(TB, D, RMS_EPS)
                rows_here()
                for tb in range(TB):
                    stt(post_tmp[:, tb, :], acc_rows(tb), col[:, 1, tb:tb + 1], rows[:, 0, :], ALU.mult, ALU.mult)
                wait()
                dve.sem_inc(acc_moved, 1)
                for tb in range(TB):
                    stt(X[:, tb, :], post_tmp[:, tb, :], weight, X[:, tb, :], ALU.mult, ALU.add)
                wait()
                dve.sem_inc(rows_used, 1)

            dve.wait_ge(gate_w_in, 32)
            dve.wait_ge(consts_in, 16 * CONST_LOADS)
            s = SLOT["gates"]
            slot_here(dve, s)
            R = lambda k: ml_rows[0:H8, k, :]
            step(V.memset(R(10), 1.0))
            step(V.memset(R(11), 0.0))
            ts(R(0), bank(s)[0:H8, 0:T], ml_bias[0:H8, 0:1], None, ALU.add)
            ts(R(1), bank(s)[0:H8, T:2 * T], ml_bias[0:H8, 1:2], None, ALU.add)
            wait()
            dve.sem_inc(slot_moved[s % 4], 1)
            dve.sem_inc(gates_split, 1)
            ts(R(4), R(1), 0.0, None, ALU.min)
            wait()
            dve.wait_ge(gates_log, 1)
            tt(R(4), R(4), R(2), ALU.subtract)
            wait()
            step(V.tensor_tensor_scan(R(5), R(10), R(4), 0.0, ALU.mult, ALU.add))
            wait()
            tt(R(6), R(0), R(5), ALU.subtract)
            wait()
            step(V.tensor_tensor_scan(R(7), R(6), R(11), 0.0, ALU.max, ALU.add))
            wait()
            tt(R(8), R(5), R(7), ALU.add)
            wait()
            dve.sem_inc(gates_scanned, 1)
            s = SLOT["gate_cols"]
            slot_here(dve, s)
            step(V.tensor_copy(gate_cols.rearrange("p a b -> p (a b)"), bank(s)[:, 0:32]))
            wait()
            dve.sem_inc(slot_moved[s % 4], 1)
            dve.sem_inc(gate_cols_ready, 1)
            for h in range(H8):
                s = SLOT[("ml", "scores", h)]
                slot_here(dve, s)
                moved(dve, SLOT[("ml", "decay", h)])
                if h >= 2:
                    slot_here(dve, SLOT[("ml", "out", h - 2)])
                free(V.scalar_tensor_tensor(out=ml_p[:, h % 2, :], in0=bank(s)[:, 0:384], scalar=ML_SCALE,
                                            in1=ml_w[:, h % 2, :], op0=ALU.mult, op1=ALU.mult), s)
            for h in range(H8):
                moved(dve, SLOT[("ml", "out", h)])
            for tb in range(TB):
                for h in range(H8):
                    step(V.bn_stats(stats[:, H8 * tb + h, :], ml_raw[:, tb, h, 0:P]))
            c16 = lambda k: col[:, k, 0:16].rearrange("p (t h) -> p t h", t=TB)
            stt(c16(2), ml_raw[:, :, :, 128], -1.0, ml_raw[:, :, :, 128], ALU.mult, ALU.max)
            wait()
            for k in range(16):
                step(V.bn_aggr(mv[:, k, :], stats[:, k:k + 1, :]))
            tt(c16(3), c16(2), gate_cols[:, 2:4, :], ALU.max)
            wait()
            step(V.reciprocal(col[:, 2, :], col[:, 3, :]))
            wait()
            tt(col[:, 3, :], col[:, 2, :], col[:, 2, :], ALU.mult)
            wait()
            tt(col[:, 4, :], col[:, 3, :], mv[:, :, 1], ALU.mult)
            wait()
            ts(col[:, 0, :], col[:, 4, :], NORM_EPS, None, ALU.add)
            inverse_roots(16)
            tt(col[:, 5, :], col[:, 1, :], col[:, 2, :], ALU.mult)
            wait()
            for tb in range(TB):
                for h in range(H8):
                    k = H8 * tb + h
                    ts(ml_hn[:, tb, h * P:(h + 1) * P], ml_raw[:, tb, h, 0:P], mv[:, k, 0:1], col[:, 5, k:k + 1],
                       ALU.subtract, ALU.mult)
            acc_gone(dve, "a_og")
            wait()
            for tb in range(TB):
                tt(ml_hn[:, tb, :], ml_hn[:, tb, :], ml_sig[:, tb, :], ALU.mult)
            wait()
            dve.sem_inc(turn_ready, 1)
            turned("ml_out", ml_outT, GAIN_ML)
            dve.wait_ge(x_in, 16)
            layer_norm("a_out")

            def top16(lists, values, where):
                n = len(lists)
                for r in range(2):
                    for k in range(n):
                        step(V.max(values(k)[:, 8 * r:8 * r + 8], lists[k]))
                    wait()
                    for k in range(n):
                        step(V.max_index(where(k)[:, 8 * r:8 * r + 8], values(k)[:, 8 * r:8 * r + 8], lists[k]))
                    if r == 0:
                        wait()
                        for k in range(n):
                            step(V.match_replace(lists[k], values(k)[:, 0:8], lists[k], LOWEST))
                        wait()

            def routing(layer):
                moved(dve, SLOT[f"scores{layer}"], 8)
                for tb in range(TB):
                    top16([SC[:, tb * 2048 + j * P:tb * 2048 + (j + 1) * P] for j in range(16)],
                          lambda k: TV[:, tb, k, :], lambda k: TI[:, tb, k, :])
                wait()
                step(V.tensor_copy(TIf, TI))
                sums = []
                for tb in range(TB):
                    c = SC[:, tb * 2048:(tb + 1) * 2048].rearrange("p (h a b) -> p h a b", h=H8, a=TOPK)
                    v = TV[:, tb].rearrange("p (h c) k -> p h c k", c=2)
                    tt(c, v[:, :, 0, :, None].to_broadcast([P, H8, TOPK, TOPK]),
                       v[:, :, 1, None, :].to_broadcast([P, H8, TOPK, TOPK]), ALU.add)
                    sums += [c[:, h].rearrange("p a b -> p (a b)") for h in range(H8)]
                wait()
                for tb in range(TB):
                    top16(sums[H8 * tb:H8 * tb + H8], lambda k: FV[:, tb, k, :], lambda k: FI[:, tb, k, :])
                wait()
                tops = col[:, 2, 0:16]
                fv = FV[:].rearrange("p t h k -> p (t h) k")
                step(V.tensor_copy(tops, fv[:, :, 0]))
                step(V.tensor_scalar(TI_halves[0], FI[:].rearrange("p t h k -> p (t h k)"), 4, None,
                                     ALU.logical_shift_right))
                step(V.tensor_scalar(TI_halves[1], FI[:].rearrange("p t h k -> p (t h k)"), 15, None,
                                     ALU.bitwise_and))
                wait()
                tt(fv, fv, tops[:, :, None].to_broadcast([P, 16, TOPK]), ALU.subtract)
                for k in range(2):
                    step(V.tensor_copy(HL[:, k].rearrange("p t h k -> p (t h k)"), TI_halves[k]))
                wait()
                dve.sem_inc(softmax_wanted, 1)
                for tb in range(TB):
                    for k in range(2):
                        eq = SC[:, k * 2048:(k + 1) * 2048].rearrange("p (h a b) -> p h a b", h=H8, a=TOPK)
                        tt(eq, HL[:, k, tb, :, :, None].to_broadcast([P, H8, TOPK, TOPK]),
                           iota[:, None, None, 0:TOPK].to_broadcast([P, H8, TOPK, TOPK]), ALU.is_equal)
                    wait()
                    for k in range(2):
                        eq = SC[:, k * 2048:(k + 1) * 2048].rearrange("p (h a b) -> p h a b", h=H8, a=TOPK)
                        lists = TIf[:, tb].rearrange("p (h c) k -> p h c k", c=2)
                        tt(eq, eq, lists[:, :, k, None, :].to_broadcast([P, H8, TOPK, TOPK]), ALU.mult)
                    wait()
                    for k in range(2):
                        eq = SC[:, k * 2048:(k + 1) * 2048].rearrange("p (n b) -> p n b", b=TOPK)
                        step(V.tensor_reduce(TV_routes[k][:, tb].rearrange("p h k -> p (h k)"), eq, AX, ALU.add))
                    wait()
                dve.wait_ge(softmax_exps, layer + 1)
                step(V.tensor_reduce(col[:, 2, 0:16], fv, AX, ALU.add))
                wait()
                step(V.reciprocal(col[:, 3, 0:16], col[:, 2, 0:16]))
                wait()
                tt(fv, fv, col[:, 3, 0:16, None].to_broadcast([P, 16, TOPK]), ALU.mult)
                wait()
                dve.sem_inc(routes_ready, 1)

            def peer(layer):
                turned(f"ln{layer}_0", XT)
                routing(layer)
                for q in range(2):
                    s = SLOT[f"routes{layer}"] + q
                    slot_here(dve, s)
                    n = 2 - q
                    step(V.tensor_copy(route_T[:, 2 * q:2 * q + n, :].rearrange("p a b -> p (a b)"),
                                       bank(s)[:, 0:n * T]))
                    wait()
                    dve.sem_inc(slot_moved[s % 4], 1)
                moved(dve, SLOT[f"u{layer}"], EXPERT_TILES)
                base = SLOT[f"gates{layer}"]

                def gate_group(k, turns):
                    for t in range(4):
                        at = turns * 16 + (4 * k + t)
                        V.tensor_scalar(onehot[:, 1, k % 2, t], iota[:], route_T[:, 1, ds(at, 1)], None,
                                        ALU.is_equal)
                        ins = V.tensor_scalar(onehot[:, 0, k % 2, t], iota[:], route_T[:, 0, ds(at, 1)],
                                              route_T[:, 2, ds(at, 1)], ALU.is_equal, ALU.mult)
                    ins.then_inc(gate_rows, 1)

                def apply_gates(k, turns):
                    slot_here(dve, base + k, turns)
                    h = expert_tokens[:, ds(turns * 16 + 4 * k, 4), :]
                    free(V.tensor_tensor(h, h, bank(base + k).rearrange("p (t e) -> p t e", t=4), ALU.mult),
                         base + k)

                with dve.Fori(0, T // 16, 1) as turns:
                    gate_group(0, turns)
                    gate_group(1, turns)
                    apply_gates(0, turns)
                    gate_group(2, turns)
                    apply_gates(1, turns)
                    gate_group(3, turns)
                    apply_gates(2, turns)
                    apply_gates(3, turns)
                moved(dve, base, T // 4)
                with dve.Fori(0, EXPERT_TILES // RING, 1) as turns:
                    for j in range(RING):
                        dve.wait_ge(tiles_begun, turns * RING + (TILE[f"v{layer}"] - RING + j + 2))
                        V.tensor_copy(staged[:, j, :], big[:, ds(turns * (RING * T) + j * T, T)]
                                      ).then_inc(rows_staged, 1)
                layer_norm(f"v{layer}")
                turned(f"ln{layer}_1", XT)
                acc_gone(dve, f"ple_gate{layer}")
                for tb in range(TB):
                    tt(ple_sig[:, tb, :], ple_sig[:, tb, :], ple_side[:, tb, :], ALU.mult)
                wait()
                for tb in range(TB):
                    tt(X[:, tb, :], X[:, tb, :], ple_sig[:, tb, :], ALU.add)
                wait()
                dve.sem_inc(turn_ready, 1)

            peer(0)
            dve.wait_ge(rope_in, 48)
            step(V.tensor_copy(pos_f, pos_i))
            wait()
            for tb in range(TB):
                ts(angle[:, 0, tb, :], inv_freq, pos_f[:, tb:tb + 1], None, ALU.mult)
            wait()
            ts(turns_[:, 0], angle[:, 0], 1.0 / (2 * np.pi), ROUND, ALU.mult, ALU.add)
            ts(turns_[:, 1], angle[:, 0], 1.0 / (2 * np.pi), 0.25, ALU.mult, ALU.add)
            wait()
            ts(turns_[:, 1], turns_[:, 1], ROUND, None, ALU.add)
            wait()
            ts(turns_[:], turns_[:], ROUND, None, ALU.subtract)
            wait()
            stt(angle[:, 1], turns_[:, 1], -TWO_PI_A, angle[:, 0], ALU.mult, ALU.add)
            wait()
            stt(angle[:, 0], turns_[:, 0], -TWO_PI_A, angle[:, 0], ALU.mult, ALU.add)
            wait()
            flat = lambda v: v.rearrange("p a b c -> p (a b c)")
            stt(flat(angle), flat(turns_), -TWO_PI_B, flat(angle), ALU.mult, ALU.add)
            wait()
            ts(angle[:, 1], angle[:, 1], float(np.pi / 2), None, ALU.add)
            wait()
            ts(flat(angle), flat(angle), -PI_BELOW, PI_BELOW, ALU.max, ALU.min)
            wait()
            dve.sem_inc(angles_ready, 1)
            turned("x1", XT)
            counts["sums"] += 1
            dve.wait_ge(sums_ready, counts["sums"])
            for k, width in ((0, KV_RANK), (1, Q_RANK)):
                ts(col[:, 0, k:4:2], col[:, 2, k:4:2], 1.0 / width, NORM_EPS, ALU.mult, ALU.add)
            inverse_roots(4)
            for tb in range(TB):
                ts(latent[:, tb, 0:KV_RANK], latent[:, tb, 0:KV_RANK], col[:, 1, 2 * tb:2 * tb + 1], None, ALU.mult)
                ts(latent[:, tb, 320:704], latent[:, tb, 320:704], col[:, 1, 2 * tb + 1:2 * tb + 2], None, ALU.mult)
            dve.wait_ge(sines_ready, 1)

            def rotate(o1, o2, x1, x2, cos, sin, tmp):
                wait()
                tt(o1, x1, cos, ALU.mult)
                tt(tmp, x2, sin, ALU.mult)
                tt(o2, x1, sin, ALU.mult)
                wait()
                tt(o1, o1, tmp, ALU.subtract)
                wait()
                tt(tmp, x2, cos, ALU.mult)
                wait()
                tt(o2, o2, tmp, ALU.add)

            for tb in range(TB):
                x1, x2 = latent[:, tb, 256:288], latent[:, tb, 288:320]
                rotate(rope_k2[:, tb, 0, 0], rope_k2[:, tb, 0, 1], x1, x2, sincos[:, 1, tb], sincos[:, 0, tb],
                       rope_tmp[:, 0, 0:32])
            wait()
            step(V.tensor_copy(rope_k2[:, :, 1], rope_k2[:, :, 0]))
            wait()
            dve.sem_inc(latents_ready, 1)
            acc_gone(dve, "uq_rope")
            for tb in range(TB):
                bc = lambda v: v[:, None, :].to_broadcast([P, H8, 32])
                rotate(q_rot[:, tb, :, 0, :], q_rot[:, tb, :, 1, :], q_rope[:, tb, 0], q_rope[:, tb, 1],
                       bc(sincos[:, 1, tb]), bc(sincos[:, 0, tb]),
                       rope_tmp[:, 0, :].rearrange("p (h c) -> p h c", h=H8))
            wait()
            dve.sem_inc(rope_ready, 1)

            def maxima(h, src, parts, scale):
                for tb, (lo, hi) in enumerate(parts):
                    step(V.tensor_reduce(col[:, 2 + h % 2, 10 + tb:11 + tb], src[:, lo:hi], AX, ALU.max))
                wait()
                ts(col[:, 2 + h % 2, 8:10], col[:, 2 + h % 2, 10:12], -scale, None, ALU.mult)
                wait()
                dve.sem_inc(maxima_ready, 1)

            def normalise(n, h, p, parts):
                dve.wait_ge(exps_ready, n + h + 1)
                step(V.reciprocal(col[:, 4 + h % 2, 2:4], col[:, 4 + h % 2, 0:2]))
                wait()
                for tb, (lo, hi) in enumerate(parts):
                    ts(p[:, h % 2, lo:hi], p[:, h % 2, lo:hi], col[:, 4 + h % 2, 2 + tb:3 + tb], None, ALU.mult)
                wait()
                dve.sem_inc(probs_ready, 1)

            def mla_max(h):
                s = SLOT[("mla", "scores", h)]
                slot_here(dve, s)
                if h >= 2:
                    slot_here(dve, SLOT[("mla", "probs", h - 2)])
                maxima(h, bank(s), parts, MLA_SCALE)

            parts = ((0, P), (P, P + T))
            mla_max(0)
            for h in range(H8):
                if h + 1 < H8:
                    mla_max(h + 1)
                normalise(0, h, mla_p, parts)
                dve.sem_inc(slot_moved[SLOT[("mla", "scores", h)] % 4], 1)
                s = SLOT[("mla", "out", h)]
                slot_here(dve, s)
                free(V.tensor_copy(mla_oT[:, h, :], bank(s)[:, 0:T]), s)
            layer_norm("b_out")
            peer(1)

            def ffn(n):
                base, looped = SLOT[f"ffn{n}"], 2 * FF_TILES // RING

                def product(j, turns=0):
                    s = base + 2 * j + 1
                    t = turns * 2 if not isinstance(turns, int) else 0
                    slot_here(dve, s, t)
                    dve.wait_ge(slot_moved[(s - 1) % 4], t + ((s - 1) // 4 + 1))
                    dst = actT[:, ds(turns * 4 + j, 1), :] if not isinstance(turns, int) else actT[:, j:j + 1, :]
                    free(V.tensor_tensor(dst, silu_g[:, j % 4:j % 4 + 1, :], bank(s)[:, None, 0:T], ALU.mult), s)

                with dve.Fori(0, looped, 1) as turns:
                    for j in range(4):
                        product(j, turns)
                for j in range(4 * looped, FF_TILES):
                    product(j)

            pre_norm()
            turned("rms1", XT, GAIN_FFN1)
            ffn(1)
            post_norm("ffn1_out", 0.5)
            pre_norm()
            turned("rms2", XT, GAIN_MIX)
            dve.wait_ge(mix_in, 16 * 6)
            dve.wait_ge(logits_ready, 1)
            ts(ret_lg[:, 2, :], ret_logit, 0.0, None, ALU.min)
            dve.wait_ge(na_bias_in, 64)
            for tb in range(TB):
                v = na_bias[:, tb].rearrange("p h r c -> p (h r) c")
                tt(v, v, na_colmask[:, None, :].to_broadcast([P, 32, 64]), ALU.add)
            wait()
            tt(ret_lg[:, 3, :], ret_lg[:, 2, :], ret_lg[:, 1, :], ALU.subtract)
            acc_gone(dve, "rqk")
            for tb in range(TB):
                bc = lambda v: v[:, None, :].to_broadcast([P, 2 * RET_H, 64])
                rotate(rqk_rot[:, tb, :, 0, :], rqk_rot[:, tb, :, 1, :], rqk[:, tb, :, 0, :], rqk[:, tb, :, 1, :],
                       bc(ret_cos[:, tb]), bc(ret_sin[:, tb]),
                       rot_tmp[:, 0, :].rearrange("p (h c) -> p h c", c=64))
            wait()
            dve.sem_inc(turn_ready, 1)
            turned("rqk", rqkT)

            def ret_exponent(h):
                tt_ = ret_d[:, h % 2, :]
                ts(tt_, ret_down, ret_lg[:, 3, RET_H + h:RET_H + h + 1], None, ALU.mult)
                wait()
                stt(tt_, ret_up, ret_lg[:, 3, h:h + 1], tt_, ALU.mult, ALU.add)
                wait()
                dve.sem_inc(decay_wanted, 1)

            wait()
            ret_exponent(0)
            for h in range(RET_H):
                if h + 1 < RET_H:
                    ret_exponent(h + 1)
                s = SLOT[("ret", "scores", h)]
                slot_here(dve, s)
                dve.wait_ge(decay_ready, h + 1)
                if h >= 2:
                    slot_here(dve, SLOT[("ret", "out", h - 2)])
                step(V.scalar_tensor_tensor(out=ret_p[:, h % 2, :], in0=bank(s), scalar=RET_SCALE,
                                            in1=ret_d[:, h % 2, :], op0=ALU.mult, op1=ALU.mult))
                wait()
                dve.sem_inc(slot_moved[s % 4], 1)
            mean_square_roots(2 * RET_H, T, RMS_EPS, src=3)
            acc_gone(dve, "rg")
            for tb in range(TB):
                for h in range(RET_H):
                    k = RET_H * tb + h
                    stt(ret_y[:, tb, h, :], ret_y[:, tb, h, :], col[:, 1, k:k + 1],
                        ret_g[:, tb, h * T:(h + 1) * T], ALU.mult, ALU.mult)
            wait()
            dve.sem_inc(turn_ready, 1)
            nparts = ((0, T), (T, 2 * T))

            def na_max(h):
                s = SLOT[("na", "scores", h)]
                slot_here(dve, s)
                if h >= 2:
                    slot_here(dve, SLOT[("na", "probs", h - 2)])
                for tb in range(TB):
                    stt(na_s[:, h % 2, tb * T:(tb + 1) * T], bank(s)[:, tb * T:(tb + 1) * T], NA_SCALE,
                        na_bias[:, tb, h].rearrange("p r c -> p (r c)"), ALU.mult, ALU.add)
                wait()
                dve.sem_inc(slot_moved[s % 4], 1)
                maxima(h, na_s[:, h % 2], nparts, 1.0)

            na_max(0)
            for h in range(H8):
                if h + 1 < H8:
                    na_max(h + 1)
                normalise(H8, h, na_s, nparts)
            turned("ret", ret_yT)
            acc_here(dve, "ret_out")
            for tb in range(TB):
                tt(merged_tmp[:, tb, :], sig_ret[:, tb, :], acc_rows(tb), ALU.mult)
            wait()
            dve.sem_inc(acc_moved, 1)
            acc_here(dve, "na_out")
            for tb in range(TB):
                tt(merged[:, tb, :], sig_na[:, tb, :], acc_rows(tb), ALU.mult)
            wait()
            dve.sem_inc(acc_moved, 1)
            for tb in range(TB):
                tt(merged[:, tb, :], merged[:, tb, :], merged_tmp[:, tb, :], ALU.add)
            wait()
            dve.sem_inc(turn_ready, 1)
            turned("merged", mergedT)
            post_norm("mix_out", 1.0)
            pre_norm()
            turned("rms3", XT, GAIN_FFN2)
            ffn(2)
            post_norm("ffn2_out", 0.5)
            dve.sem_inc(out_ready, 1)





def tall(w):
    n = w.shape[1] // P
    return np.ascontiguousarray(w.reshape(KC, P, n, P).transpose(2, 1, 0, 3)).reshape(n, P, D)


def wide(w):
    return np.ascontiguousarray(w.reshape(-1, P, w.shape[1]))


def by_feature(v):
    return np.ascontiguousarray(v.T.reshape(-1, P, v.shape[0]).transpose(1, 0, 2))


def by_token(v):
    return np.ascontiguousarray(np.swapaxes(v.reshape(TB, P, *v.shape[1:]), 0, 1))


def columns(v):
    return v.reshape(-1, P).T


def constants():
    f = np.float32
    q, k = np.arange(P)[None, :], np.arange(P)[:, None]
    pos = np.arange(T, dtype=f)
    ang = pos[:, None] * (f(1.0) / (f(10000.0) ** np.linspace(0.0, 1.0, 64, dtype=f)))[None, :]
    diff = (np.arange(T)[None, None, :] - (np.arange(P)[:, None, None] + P * np.arange(TB)[None, :, None]))
    c = np.arange(P) % 64
    first = np.clip(c - 8, 0, 48)[:, None]
    cc = np.arange(64)[None, :]
    sel = np.zeros((H8, H8, P), f)
    sel[np.arange(H8), np.arange(H8)] = 1.0
    return {
        "ident": np.eye(P, dtype=f),
        "iota": np.tile(np.arange(P, dtype=f), (P, 1)),
        "ml_sel": sel,
        "ml_mask": np.where(q < k, f(BIG), f(0.0)),
        "mla_mask": np.where(q > k, f(-BIG), f(0.0)),
        "inv_freq": np.tile(f(10000.0) ** (-np.arange(0, ROPE, 2, dtype=f) / f(ROPE)), (P, 1)),
        "ret_cos": by_token(np.cos(ang)), "ret_sin": by_token(np.sin(ang)),
        "ret_up": np.maximum(diff, 0).astype(f).reshape(P, TB * T),
        "ret_down": np.maximum(-diff, 0).astype(f).reshape(P, TB * T),
        "na_colmask": np.where((cc >= first) & (cc < first + 16), f(0.0), f(-BIG)),
    }


def layout(i):
    w, wmix = i["a_w_in"][0], i["w_mix_in_2"][0]
    kv_up, uq = i["kv_w_up"].reshape(KV_RANK, H8, 2 * P), i["b_w_uq"][0].reshape(Q_RANK, H8, P + ROPE)
    at = np.clip(np.arange(64)[None, :] - np.arange(64)[:, None] + 15, 0, 30)
    m = {
        "x": by_token(i["x"][0]), "xT": by_feature(i["x"][0]),
        "positions": by_token(i["positions"][0]),
        "ml_gate_w": np.ascontiguousarray(w[:, 2048:2064].reshape(KC, P, 16).transpose(1, 0, 2)),
        "ml_bias": np.ascontiguousarray(i["a_b_if"][0].T),
        "cols": np.ascontiguousarray(np.concatenate(
            [columns(v) for v in (i["a_hn_g"][0], i["kv_norm_g"], i["b_q_norm_g"][0], i["ffn1_pre_norm_2"][0],
                                  i["mix_pre_norm_2"][0], i["ffn2_pre_norm_2"][0])], axis=1)),
        "a_qk": tall(w[:, 0:1024]), "a_v": wide(w[:, 1024:2048]), "a_og": wide(w[:, 2064:3088]),
        "a_out": wide(i["a_w_out"][0]),
        "kv_q_down": wide(np.concatenate([i["kv_w_down"], i["b_w_dq"][0]], axis=1)),
        "up_k": wide(kv_up[:, :, 0:P].reshape(KV_RANK, D)), "up_v": wide(kv_up[:, :, P:].reshape(KV_RANK, D)),
        "uq_nope": wide(uq[:, :, 0:P].reshape(Q_RANK, D)), "uq_rope": wide(uq[:, :, P:].reshape(Q_RANK, 512)),
        "b_out": wide(i["b_w_out"][0]),
        "rqk": wide(wmix[:, 0:1024]), "rv": wide(wmix[:, 1024:2048]), "rg": wide(wmix[:, 2048:3072]),
        "nqk": tall(wmix[:, 3072:4096]),
        "nv": np.ascontiguousarray(wmix[:, 4096:4608].reshape(4, 2, P, 512).transpose(0, 2, 1, 3)).reshape(4, P, D),
        "g_ret": wide(wmix[:, 4608:5632]), "g_na": wide(wmix[:, 5632:6656]),
        "ret_out": wide(i["w_ret_out_2"][0]), "na_out": wide(i["w_na_out_2"][0]),
        "mix_out": wide(i["w_mix_out_2"][0]),
        "ret_logit": np.concatenate([i["ret_decay_fwd_2"], i["ret_decay_bwd_2"]], axis=1),
        "na_bias": np.ascontiguousarray(i["na_rel_bias_2"][0][:, 4:11, :][:, :, at].transpose(2, 0, 1, 3)),
    }
    for n in (1, 2):
        t = tall(i[f"ffn{n}_w_in_2"][0])
        m[f"ffn{n}_in"] = np.stack([t[:FF_TILES], t[FF_TILES:]], axis=1).reshape(2 * FF_TILES, P, D)
        m[f"ffn{n}_out"] = wide(i[f"ffn{n}_w_out_2"][0])
    for l in range(LAYERS):
        m[f"p{l}"] = by_feature(i["p"][l, 0])
        m[f"wq{l}"] = tall(i["peer_w_q"][l])
        m[f"keys{l}"] = np.ascontiguousarray(
            i["peer_sub_keys"][l].reshape(2, KC, P, P).transpose(0, 3, 1, 2)).reshape(2, P, D)
        m[f"u{l}"] = np.ascontiguousarray(
            i["peer_u"][l].reshape(EXPERT_TILES, P, KC, P).transpose(0, 3, 2, 1)).reshape(EXPERT_TILES, P, D)
        m[f"v{l}"] = i["peer_v"][l].reshape(EXPERT_TILES, P, D)
        m[f"ple_proj{l}"] = wide(i["ple_w_proj"][l])
        m[f"ple_gate{l}"] = wide(i["ple_w_gate"][l])
    rows = [(i["ln_g"][l, k], i["ln_b"][l, k]) for l in range(LAYERS) for k in range(2)]
    rows += [(i[n][0],) for n in ("ffn1_post_norm_2", "mix_post_norm_2", "ffn2_post_norm_2")]
    for k, r in enumerate(rows):
        m[f"rows{k}"] = np.stack(r)
    return m


def kernel(**inputs):
    import concourse.bacc as bacc
    from concourse.bass_utils import run_bass_kernel_spmd

    laid = {**layout({k: np.asarray(v) for k, v in inputs.items()}), **constants()}
    nc = bacc.Bacc("TRN2", target_bir_lowering=False, num_devices=1)
    aps = {n: nc.dram_tensor(f"in_{n}", v.shape, mybir.dt.from_np(v.dtype), kind="ExternalInput").ap()
           for n, v in laid.items()}
    out = nc.dram_tensor("out", (1, T, D), F32, kind="ExternalOutput").ap()
    program(nc, aps, out.rearrange("a (t p) d -> p (a t) d", p=P))
    r = run_bass_kernel_spmd(nc, [{f"in_{n}": v for n, v in laid.items()}], core_ids=[0])
    return r.results[0]["out"]
```

```python
from contextlib import ExitStack

import numpy as np

import concourse.bass as bass
from concourse import mybir

P = 128
D = 1024
T = 256
TB = T // P
KC = D // P
RING = 4
BODY = 8
F32 = mybir.dt.float32
BF16 = mybir.dt.bfloat16
F32R = mybir.dt.float32r
U32 = mybir.dt.uint32
I32 = mybir.dt.int32
ALU = mybir.AluOpType
ACT = mybir.ActivationFunctionType
AX = mybir.AxisListType.X
ds = bass.ds

LAYERS = 2
DN_ALPHA = (2.0 * LAYERS) ** 0.25
NORM_EPS = 1e-5
RMS_EPS = 1e-6
BIG = 1e30
LOWEST = -3.0e38
ROUND = 12582912.0
TWO_PI_A = 6.28125
TWO_PI_B = float(np.float32(2 * np.pi - 6.28125))
PI_BELOW = 3.1415925

H8 = 8
ML_SCALE = 64 ** -0.5
KV_RANK, ROPE, Q_RANK = 256, 64, 384
LATENTS = KV_RANK + ROPE + Q_RANK
MLA_SCALE = (128 + 64) ** -0.5
TOPK = 16
EXPERT_TILES = 128
RET_H = 4
RET_SCALE = 128 ** -0.5
NA_SCALE = 64 ** -0.5
FF_TILES = 2816 // P

PEER_TILES = [("wq", 16), ("keys", 2), ("u", EXPERT_TILES), ("v", EXPERT_TILES), ("ple_proj", 2), ("ple_gate", 8)]
STREAM = (
    [("a_qk", 8), ("a_v", 8), ("a_og", 8), ("a_out", 8)]
    + [(f"{n}0", k) for n, k in PEER_TILES]
    + [("kv_q_down", 8), ("up_k", 2), ("up_v", 2), ("uq_nope", 3), ("uq_rope", 3), ("b_out", 8)]
    + [(f"{n}1", k) for n, k in PEER_TILES]
    + [("ffn1_in", 2 * FF_TILES), ("ffn1_out", FF_TILES)]
    + [("rqk", 8), ("rv", 8), ("rg", 8), ("nqk", 8), ("nv", 4), ("g_ret", 8), ("g_na", 8)]
    + [("ret_out", 8), ("na_out", 4), ("mix_out", 8)]
    + [("ffn2_in", 2 * FF_TILES), ("ffn2_out", FF_TILES)]
)

ACC_ORDER = ["a_v", "a_og", "a_out", "v0", "ple_proj0", "ple_gate0", "kv_q_down", "up_v", "uq_rope", "b_out",
             "v1", "ple_proj1", "ple_gate1", "ffn1_out", "rqk", "rv", "rg", "nv", "g_ret", "g_na",
             "ret_out", "na_out", "mix_out", "ffn2_out"]

TURN_ORDER = ["ml_out", "ln0_0", "ln0_1", "x1", "ln1_0", "ln1_1", "x2", "rms1", "rms2", "rqk", "ret", "merged", "rms3"]


def starts(items):
    out, at = {}, 0
    for name, n in items:
        out[name] = at
        at += n
    return out


def attention_order(name, first, last):
    heads = H8 if name != "ret" else RET_H
    out = [((name, s, 0), 1) for s in first]
    for h in range(heads):
        if h + 1 < heads:
            out += [((name, s, h + 1), 1) for s in first]
        out += [((name, s, h), 1) for s in last]
    return out


def peer_slots(layer):
    return [(f"wq{layer}", 16), (f"scores{layer}", 8), (f"u{layer}", EXPERT_TILES), (f"routes{layer}", 2),
            (f"gates{layer}", T // 4)]


def turn(name):
    return [(f"turn_{name}", 4)]


SLOT_ORDER = (
    [("gates", 1), ("a_qk", 8), ("gate_cols", 1)]
    + attention_order("ml", ["decay", "scores"], ["out"])
    + turn("ml_out") + turn("ln0_0") + peer_slots(0) + turn("ln0_1") + turn("x1")
    + [("latents", 3), ("up_k", 8), ("uq_nope", 8), ("rope", 2)]
    + attention_order("mla", ["scores"], ["probs", "out"])
    + turn("ln1_0") + peer_slots(1) + turn("ln1_1")
    + turn("rms1") + [("ffn1", 2 * FF_TILES)] + turn("rms2") + [("nqk", 8)] + turn("rqk")
    + attention_order("ret", ["scores"], ["out"])
    + attention_order("na", ["scores"], ["probs", "out"])
    + turn("ret") + turn("merged") + turn("rms3") + [("ffn2", 2 * FF_TILES)]
)
TILE = starts(STREAM)
SPLIT_STAGES = {"wq0", "u0", "v0", "ple_gate0", "kv_q_down", "wq1", "u1", "v1", "ple_gate1", "ffn1_in", "ffn1_out",
                "rqk", "rv", "rg", "nqk", "nv", "g_ret", "g_na", "ret_out", "mix_out", "ffn2_in", "ffn2_out"}
PART_TURNS = ["ln0_0", "ln0_1", "x1", "ln1_0", "ln1_1", "rms1", "rms2", "ret", "merged", "rms3"]
SPLIT = starts([(name, n if name in SPLIT_STAGES else 0) for name, n in STREAM])
TILE_NAMES = [name for name, n in STREAM for _ in range(n)]
SLOT = starts(SLOT_ORDER)
ACC = {name: n for n, name in enumerate(ACC_ORDER)}
TURN = {name: n for n, name in enumerate(TURN_ORDER)}

ROW_SETS = [2, 2, 2, 2, 1, 1, 1]


def program(nc, a, out):
    with ExitStack() as ctx:
        def sbuf(name, shape, dt=F32):
            return ctx.enter_context(nc.sbuf_tensor(name, shape, dt))

        def sem(name):
            return ctx.enter_context(nc.semaphore(name))

        ps = ctx.enter_context(nc.psum_tensor("ps", [P, 8, 512], F32))
        ring = sbuf("ring", [P, RING, D])
        big_at = nc.sbuf_base
        big = sbuf("big", [P, EXPERT_TILES * T])
        X = sbuf("X", [P, TB, D])
        w_hi = sbuf("w_hi", [P, 2, D], F32R)
        w_lo = sbuf("w_lo", [P, 2, D], F32R)
        x_hi_at = nc.sbuf_base
        x_hi = sbuf("x_hi", [P, KC, T], F32R)
        x_lo_at = nc.sbuf_base
        x_lo = sbuf("x_lo", [P, KC, T], F32R)
        SC = sbuf("SC", [P, 4096])
        tops = sbuf("tops", [P, 1024])
        ident = sbuf("ident", [P, P])
        iota = sbuf("iota", [P, P])
        zeros = sbuf("zeros", [P, 512], BF16)
        cols = sbuf("cols", [P, 37])
        col = sbuf("col", [P, 6, 16])
        stats = sbuf("stats", [P, 16, 6])
        mv = sbuf("mv", [P, 16, 2])

        def shaped(v, *shape):
            if len(shape) == 1:
                return v
            names = "abcd"[:len(shape)]
            return v.rearrange(f"p ({' '.join(names)}) -> p {' '.join(names)}",
                               **{k: s for k, s in zip(names, shape)})

        def buf(at, *shape):
            return shaped(big[:, at:at + int(np.prod(shape))], *shape)

        BK = 2048
        acc = ps[:, 0:4, :]

        def acc_rows(tb):
            return ps[:, 2 * tb:2 * tb + 2, :].rearrange("p a b -> p (a b)")

        def bank(s):
            return ps[:, 4 + s % 4, :]

        rows = SC[:, 2 * 1024:4 * 1024].rearrange("p (r n) -> p r n", r=2)
        gated_rows = shaped(SC[:, 0:2048], 4, 4, P)
        pT = shaped(SC[:, 0:512], 2, T)
        place = nc.alloc_sbuf_tensor_at("place", [P, 4, 4, P], F32, offset=x_hi_at)
        distance = nc.alloc_sbuf_tensor_at("distance", [P, 4, 4, P], F32, offset=x_lo_at)
        expert_tokens = big[:, :].rearrange("p (e t) -> p t e", t=T)
        TV = shaped(tops[:, 0:512], TB, 2 * H8, TOPK)
        TI = shaped(tops[:, 512:1024].bitcast(U32), TB, 2 * H8, TOPK)
        TIf = shaped(tops[:, 512:1024], TB, 2 * H8, TOPK)
        FI = shaped(SC[:, 2048:2304].bitcast(U32), TB, H8, TOPK)
        halves = [SC[:, 2304 + k * T:2304 + (k + 1) * T].bitcast(U32) for k in range(2)]
        HL = shaped(SC[:, 2816:3328], 2, TB, H8, TOPK)
        FV = shaped(SC[:, 3328:3584], TB, H8, TOPK)
        route_index = [shaped(tops[:, k * T:(k + 1) * T], TB, H8, TOPK) for k in range(2)]
        route_T = shaped(tops[:, 0:3 * T], 3, T)

        def expert_rows(j, turns):
            at = turns * (BODY * T) + j * T
            return big[:, at:at + T] if isinstance(turns, int) else big[:, ds(at, T)]

        tiles_hi = sem("tiles_hi")
        tiles_split = sem("tiles_split")
        staged_hi = sem("staged_hi")
        staged = sem("staged")
        x_hi_ready = sem("x_hi_ready")
        routes_turned = sem("routes_turned")
        tile_landed = [sem(f"tile_landed{i}") for i in range(RING)]
        tiles_begun = sem("tiles_begun")
        slot_full = [sem(f"slot_full{i}") for i in range(4)]
        slot_moved = [sem(f"slot_moved{i}") for i in range(4)]
        acc_full = sem("acc_full")
        acc_moved = sem("acc_moved")
        turn_ready = sem("turn_ready")
        act_step = sem("act_step")
        dve_step = sem("dve_step")
        pool_step = sem("pool_step")
        sqrt_wanted = sem("sqrt_wanted")
        sqrt_done = sem("sqrt_done")
        xt_in = sem("xt_in")
        x_in = sem("x_in")
        gate_w_in = sem("gate_w_in")
        consts_in = sem("consts_in")
        rows_in = sem("rows_in")
        rows_used = sem("rows_used")
        p_in = sem("p_in")
        rope_in = sem("rope_in")
        mix_in = sem("mix_in")
        na_bias_in = sem("na_bias_in")
        zeros_set = sem("zeros_set")
        gates_split = sem("gates_split")
        gates_log = sem("gates_log")
        gates_scanned = sem("gates_scanned")
        floor_ready = sem("floor_ready")
        gate_cols_ready = sem("gate_cols_ready")
        decay_ready = sem("decay_ready")
        ones_set = sem("ones_set")
        sums_ready = sem("sums_ready")
        angles_ready = sem("angles_ready")
        sines_ready = sem("sines_ready")
        latents_ready = sem("latents_ready")
        rope_ready = sem("rope_ready")
        maxima_ready = sem("maxima_ready")
        exps_ready = sem("exps_ready")
        probs_ready = sem("probs_ready")
        probs_turned = sem("probs_turned")
        logits_wanted = sem("logits_wanted")
        logits_ready = sem("logits_ready")
        routes_ready = sem("routes_ready")
        softmax_wanted = sem("softmax_wanted")
        softmax_exps = sem("softmax_exps")
        gate_rows = sem("gate_rows")
        place_rows = sem("place_rows")
        distances = sem("distances")
        inner_step = sem("inner_step")
        decay_wanted = sem("decay_wanted")
        out_ready = sem("out_ready")
        stored = sem("stored")

        def tile_here(pe, i, turns=0):
            pe.wait_ge(tile_landed[i % RING], turns * 16 + 16 * (i // RING + 1))

        def tile(i):
            return ring[:, i % RING, :]

        def tall(i):
            return ring[:, i % RING, :].rearrange("p (k n) -> p k n", k=KC)

        def part(t, i):
            return t[:, i % 2, :]

        def split_from(name):
            return SPLIT[name]

        def part_free(eng, i, turns=0):
            if not isinstance(turns, int) or (i >= 2 and TILE_NAMES[i - 2] in SPLIT_STAGES):
                eng.wait_ge(tiles_begun, turns * BODY + i)

        def used(name):
            return slice(0, LATENTS if name == "kv_q_down" else D)

        def take_high(act, name, j, turns=0):
            i = TILE[name] + j
            tile_here(act, i, turns * (BODY // RING))
            part_free(act, i, turns)
            nc.scalar.copy(part(w_hi, i)[:, used(name)], tile(i)[:, used(name)]).then_inc(tiles_hi, 1)

        def take_low(dve, name, j, turns=0):
            i = TILE[name] + j
            dve.wait_ge(tiles_hi, turns * BODY + SPLIT[name] + j + 1)
            at = used(name)
            nc.vector.tensor_tensor(part(w_lo, i)[:, at], tile(i)[:, at], part(w_hi, i)[:, at], ALU.subtract
                                    ).then_inc(tiles_split, 1)

        def slot_free(pe, s, turns=0):
            if s >= 4:
                pe.wait_ge(slot_moved[s % 4], turns + s // 4)

        def slot_here(eng, s, turns=0):
            eng.wait_ge(slot_full[s % 4], turns + s // 4 + 1)

        def moved(eng, s, n=1):
            for k in range(max(s, s + n - 4), s + n):
                eng.wait_ge(slot_moved[k % 4], k // 4 + 1)

        def full(ins, s):
            return ins.then_inc(slot_full[s % 4], 1)

        def free(ins, s):
            return ins.then_inc(slot_moved[s % 4], 1)

        def acc_here(eng, name):
            eng.wait_ge(acc_full, ACC[name] + 1)

        def acc_gone(eng, name):
            eng.wait_ge(acc_moved, ACC[name] + 1)

        def head_rows(h):
            return slice(64 * (h % 2), 64 * (h % 2) + 64)

        class Steps:

            def __init__(self, eng, s):
                self.eng, self.sem, self.n = eng, s, 0

            def __call__(self, ins):
                ins.then_inc(self.sem, 1)
                self.n += 1

            def wait(self):
                self.eng.wait_ge(self.sem, self.n)

        AFTER_PEER = ["kv_q_down", "ffn1_in"]

        XT = buf(11 * BK, KC, T)
        ml_qk = buf(0, KC, T)
        ml_v = buf(BK, TB, H8, 129)
        ml_sig = buf(3 * BK, TB, D)
        ml_raw = buf(4 * BK, TB, H8, 129)
        ml_hn = buf(6 * BK, TB, D)
        ml_outT = buf(7 * BK, KC, T)
        ml_w = buf(8 * BK, 2, 384)
        ml_p = buf(8 * BK + 768, 2, 384)
        ml_rows = buf(9 * BK, 14, T)
        ml_sel = buf(15 * BK, H8, P)
        ml_gate_w = buf(12 * BK, KC, 16)
        ml_bias = buf(12 * BK + 128, 2)
        ml_mask = buf(12 * BK + 256, P)
        gate_cols = buf(13 * BK, 4, H8)
        ple_sig = buf(3 * BK, TB, D)
        ple_side = buf(4 * BK, TB, D)
        peer_q = big[:, 112 * T:128 * T].rearrange("p (j t) -> p j t", t=T)
        latent = buf(0, TB, LATENTS)
        latT = buf(BK, 6, T)
        k_nope = buf(2 * BK, H8, T)
        mla_v = buf(3 * BK, TB, D)
        q_nope = buf(4 * BK, H8, T)
        q_rope = buf(5 * BK, TB, 2, H8, 32)
        q_rot = buf(5 * BK + 1024, TB, H8, 2, 32)
        q_ropeT = buf(6 * BK, 4, T)
        rope_k2 = buf(6 * BK + 1024, TB, 2, 2, 32)
        rope_tmp = buf(6 * BK + 1280, 2, 256)
        mla_oT = buf(7 * BK, H8, T)
        mla_p = buf(8 * BK, 2, 384)
        mla_pT = buf(8 * BK + 768, 2, 384)
        angle = buf(9 * BK, 2, TB, 32)
        turns_ = buf(9 * BK + 128, 2, TB, 32)
        sincos = buf(9 * BK + 256, 2, TB, 32)
        inv_freq = buf(9 * BK + 384, 32)
        pos_i = big[:, 9 * BK + 416:9 * BK + 418].bitcast(I32)
        pos_f = buf(9 * BK + 420, TB)
        mla_mask = buf(9 * BK + 512, P)
        sq_junk = buf(10 * BK, D)
        act_hi = nc.alloc_sbuf_tensor_at("act_hi", [P, FF_TILES, T], F32R, offset=big_at)
        act_lo = nc.alloc_sbuf_tensor_at("act_lo", [P, FF_TILES, T], F32R, offset=big_at + 9 * BK * 4)
        act_f = buf(3 * BK + 1024, T)
        silu_g = buf(3 * BK, 4, T)
        xn = buf(4 * BK, TB, D)
        na_bias = buf(5 * BK, TB, H8, 4, 64)
        post_tmp = buf(7 * BK, TB, D)
        rqk = buf(0, TB, 2 * RET_H, 2, 64)
        rqk_rot = buf(BK, TB, 2 * RET_H, 2, 64)
        rqkT = buf(2 * BK, 2 * RET_H, T)
        ret_v = buf(3 * BK, TB, D)
        ret_g = buf(4 * BK, TB, D)
        na_qk = buf(7 * BK, KC, T)
        na_v = buf(8 * BK, TB, 512)
        ret_cos = buf(8 * BK + 1024, TB, 64)
        ret_sin = buf(8 * BK + 1152, TB, 64)
        na_colmask = buf(8 * BK + 1280, 64)
        ret_logit = buf(8 * BK + 1344, 2 * RET_H)
        ret_lg = buf(8 * BK + 1352, 4, 2 * RET_H)
        sig_ret = buf(9 * BK, TB, D)
        sig_na = buf(10 * BK, TB, D)
        ret_y = buf(11 * BK, TB, RET_H, 256)
        ret_d = buf(12 * BK, 2, 512)
        ret_p = buf(12 * BK + 1024, 2, 512)
        na_s = buf(13 * BK, 2, 512)
        na_pT = buf(13 * BK + 1024, 2, 512)
        na_oT = buf(14 * BK, 4, T)
        ret_up = buf(14 * BK + 1024, 512)
        ret_down = buf(15 * BK, 512)
        rot_tmp = buf(15 * BK + 512, 2, 512)
        ret_junk = buf(13 * BK, 256)
        merged = buf(0, TB, D)
        merged_tmp = buf(BK, TB, D)
        ret_yT = buf(2 * BK, KC, T)
        mergedT = buf(3 * BK, KC, T)
        GAIN_ML, GAIN_KV, GAIN_Q, GAIN_FFN1, GAIN_MIX, GAIN_FFN2 = 0, 8, 10, 13, 21, 29

        CONSTS = [(ident[:], "ident"), (iota[:], "iota"), (ml_sel[0:H8], "ml_sel"), (ml_mask, "ml_mask"),
                  (cols[:], "cols")]
        CONST_LOADS = len(CONSTS)

        block = ctx.enter_context(nc.Block())

        @block.sync
        def _(sp):
            def load(name, w, j):
                i = TILE[name] + j
                if i >= RING:
                    before = TILE_NAMES[i - RING]
                    if before in SPLIT_STAGES:
                        sp.wait_ge(tiles_split, SPLIT[before] + i - RING - TILE[before] + 1)
                    else:
                        sp.wait_ge(tiles_begun, i - RING + 2)
                sp.dma_start(tile(i)[:, 0:w.shape[2]], w[j]).then_inc(tile_landed[i % RING], 16)

            def stream(name, w):
                n, j = w.shape[0], 0
                if n >= 3 * BODY:
                    for j in range(BODY):
                        load(name, w, j)
                    with sp.Fori(1, n // BODY, 1) as turns:
                        for j in range(BODY):
                            i = TILE[name] + j
                            sp.wait_ge(tiles_split, turns * BODY + (SPLIT[name] + j - RING + 1))
                            sp.dma_start(tile(i), w[ds(turns * BODY + j, 1), :, :].rearrange("a p n -> p (a n)")
                                         ).then_inc(tile_landed[i % RING], 16)
                    j = n - n % BODY
                for j in range(j, n):
                    load(name, w, j)

            for name, _n in STREAM:
                stream(name, a[name])
            sp.wait_ge(out_ready, 1)
            sp.dma_start(out, X[:]).then_inc(stored, 16)
            sp.wait_ge(stored, 16)

        @block.gpsimd
        def _(pool):
            step = Steps(pool, pool_step)
            nc.gpsimd.memset(zeros[:], 0.0).then_inc(zeros_set, 1)
            nc.gpsimd.memset(ml_v[:, :, :, 128:129], 1.0).then_inc(ones_set, 1)

            def load_rows(k, wait=None):
                if k:
                    pool.wait_ge(rows_used, k)
                if wait:
                    pool.wait_ge(*wait)
                for r in range(ROW_SETS[k]):
                    pool.dma_start(rows[:, r, :], a[f"rows{k}"][r:r + 1, :].to_broadcast([P, D])).then_inc(rows_in, 16)

            def load_p(layer):
                moved(pool, SLOT[f"gates{layer}"], T // 4)
                pool.dma_start(pT, a[f"p{layer}"]).then_inc(p_in, 16)

            load_rows(0)
            load_rows(1, (routes_turned, 1))
            load_p(0)
            load_rows(2)
            load_rows(3, (routes_turned, 2))
            load_p(1)
            load_rows(4)
            pool.wait_ge(turn_ready, TURN["rms1"] + 1)
            for tb in range(TB):
                for r in range(2):
                    first = 3 - (2 * tb + r)
                    pool.dma_start(na_bias[64 * r:64 * r + 64, tb], a["na_bias"][:, :, first:first + 4, :]
                                   ).then_inc(na_bias_in, 16)
            for dst, name in ((ret_cos, "ret_cos"), (ret_sin, "ret_sin"), (na_colmask, "na_colmask"),
                              (ret_logit, "ret_logit"), (ret_up, "ret_up"), (ret_down, "ret_down")):
                src = a[name] if name != "ret_logit" else a[name].to_broadcast([P, 2 * RET_H])
                pool.dma_start(dst, src).then_inc(mix_in, 16)
            load_rows(5)
            load_rows(6)

        @block.tensor
        def _(pe):
            def begins_tile(mm):
                mm.then_inc(tiles_begun, 1)

            def to_acc(name, lhs, n, width=D):
                if ACC[name]:
                    pe.wait_ge(acc_moved, ACC[name])
                halves = [(f, min(512, width - 512 * f)) for f in range((width + 511) // 512)]
                for k in range(n):
                    i = TILE[name] + k
                    tile_here(pe, i)
                    for tb in range(TB):
                        for f, cnt in halves:
                            mm = nc.tensor.matmul(acc[:, 2 * tb + f, 0:cnt], lhs(k, tb),
                                                  tile(i)[:, 512 * f:512 * f + cnt],
                                                  start=(k == 0), stop=(k == n - 1))
                            if tb == f == 0:
                                begins_tile(mm)
                mm.then_inc(acc_full, 1)

            def from_tall(i, s, src, turns=0):
                tile_here(pe, i, turns)
                slot_free(pe, s, turns * 2 if not isinstance(turns, int) else 0)
                for k in range(KC):
                    mm = nc.tensor.matmul(bank(s)[:, 0:T], tall(i)[:, k, :], src[:, k, :],
                                          start=(k == 0), stop=(k == KC - 1))
                    if k == 0:
                        begins_tile(mm)
                full(mm, s)

            def hi_here(name, j, turns=0):
                pe.wait_ge(tiles_hi, turns * BODY + (SPLIT[name] + j + 1))

            def lo_here(name, j, turns=0):
                pe.wait_ge(tiles_split, turns * BODY + (SPLIT[name] + j + 1))

            def split_tall(name, j, s, turns=0):
                i = TILE[name] + j
                hi_here(name, j, turns)
                slot_free(pe, s, turns * 2)
                hi, lo = (part(t, i).rearrange("p (k n) -> p k n", k=KC) for t in (w_hi, w_lo))
                for k in range(KC):
                    mm = nc.tensor.matmul(bank(s)[:, 0:T], hi[:, k, :], x_hi[:, k, :], start=(k == 0), stop=False)
                    if k == 0:
                        begins_tile(mm)
                    nc.tensor.matmul(bank(s)[:, 0:T], hi[:, k, :], x_lo[:, k, :], start=False, stop=False)
                lo_here(name, j, turns)
                for k in range(KC):
                    mm = nc.tensor.matmul(bank(s)[:, 0:T], lo[:, k, :], x_hi[:, k, :],
                                          start=False, stop=(k == KC - 1))
                full(mm, s)

            def split_wide(name, j, xs, k, first, last, turns=0, width=D, per_tile=1):
                halves = [(f, min(512, width - 512 * f)) for f in range((width + 511) // 512)]
                i = TILE[name] + j
                hi_here(name, j, turns)
                passes = ((xs[0], w_hi), (xs[1], w_hi), (xs[0], w_lo))
                for n, (x, w) in enumerate(passes):
                    if w is w_lo:
                        lo_here(name, j, turns)
                    for c in range(per_tile):
                        for tb in range(TB):
                            for f, cnt in halves:
                                at = c * width + 512 * f
                                mm = nc.tensor.matmul(acc[:, 2 * tb + f, 0:cnt], x[:, k + c, tb * P:(tb + 1) * P],
                                                      part(w, i)[:, at:at + cnt],
                                                      start=(first and n == 0 and c == 0),
                                                      stop=(last and n == 2 and c == per_tile - 1))
                                if n == c == tb == f == 0:
                                    begins_tile(mm)
                return mm

            def split_to_acc(name, width=D, per_tile=1):
                pe.wait_ge(acc_moved, ACC[name])
                for k in range(0, KC, per_tile):
                    mm = split_wide(name, k // per_tile, (x_hi, x_lo), k, k == 0, k == KC - per_tile,
                                    width=width, per_tile=per_tile)
                mm.then_inc(acc_full, 1)

            def turn_over(name, src, width=P):
                pe.wait_ge(turn_ready, TURN[name] + 1)
                for q in range(4):
                    s = SLOT[f"turn_{name}"] + q
                    slot_free(pe, s)
                    for c in range(2):
                        for tb in range(TB):
                            at = (2 * q + c) * P
                            mm = nc.tensor.transpose(bank(s)[:, (2 * c + tb) * P:(2 * c + tb + 1) * P],
                                                     src[:, tb, at:at + P], ident[:])
                    full(mm, s)

            def tokens(src):
                return lambda k, tb: src[:, k, tb * P:(tb + 1) * P]

            pe.wait_ge(consts_in, 16 * CONST_LOADS)
            pe.wait_ge(xt_in, 16)
            pe.wait_ge(gate_w_in, 32)
            pe.wait_ge(zeros_set, 1)
            s = SLOT["gates"]
            for g in range(2):
                for k in range(KC):
                    mm = nc.tensor.matmul(bank(s)[0:H8, g * T:(g + 1) * T], ml_gate_w[:, k, g * H8:(g + 1) * H8],
                                          XT[:, k, :], start=(k == 0), stop=(k == KC - 1))
            full(mm, s)
            for j in range(8):
                from_tall(TILE["a_qk"] + j, SLOT["a_qk"] + j, XT)
            to_acc("a_v", tokens(XT), KC)
            to_acc("a_og", tokens(XT), KC)
            pe.wait_ge(gates_scanned, 1)
            pe.wait_ge(floor_ready, 1)
            s = SLOT["gate_cols"]
            slot_free(pe, s)
            for c, row in ((0, 6), (2, 9)):
                for tb in range(TB):
                    mm = nc.tensor.matmul(bank(s)[:, (c + tb) * H8:(c + tb + 1) * H8],
                                          ml_rows[0:H8, row, tb * P:(tb + 1) * P], ident[0:H8, 0:H8],
                                          start=True, stop=True)
            full(mm, s)

            def ml_first(h):
                s = SLOT[("ml", "decay", h)]
                slot_free(pe, s)
                nc.tensor.matmul(bank(s)[:, 0:T], ml_sel[0:H8, h, :], ml_rows[0:H8, 7, :], start=True, stop=False)
                nc.tensor.matmul(bank(s)[:, 0:P], ident[:], ml_mask[:], start=False, stop=True)
                nc.tensor.matmul(bank(s)[:, T:T + P], ml_sel[0:H8, h, :], ml_rows[0:H8, 7, P:T],
                                 start=True, stop=False)
                full(nc.tensor.matmul(bank(s)[:, T:T + P], ident[:], ml_mask[:], start=False, stop=True), s)
                s = SLOT[("ml", "scores", h)]
                slot_free(pe, s)
                r, q, k = head_rows(h), h // 2, 4 + h // 2
                nc.tensor.matmul(bank(s)[:, 0:T], ml_qk[r, k, 0:P], ml_qk[r, q, :], start=True, stop=True)
                full(nc.tensor.matmul(bank(s)[:, T:T + P], ml_qk[r, k, P:T], ml_qk[r, q, P:T],
                                      start=True, stop=True), s)

            moved(pe, SLOT["a_qk"], 8)
            acc_gone(pe, "a_v")
            pe.wait_ge(ones_set, 1)
            ml_first(0)
            for h in range(H8):
                if h + 1 < H8:
                    ml_first(h + 1)
                moved(pe, SLOT[("ml", "scores", h)])
                s = SLOT[("ml", "out", h)]
                slot_free(pe, s)
                w = ml_p[:, h % 2]
                nc.tensor.matmul(bank(s)[:, 0:129], w[:, 0:P], ml_v[:, 0, h, :], start=True, stop=True)
                nc.tensor.matmul(bank(s)[:, T:T + 129], w[:, P:T], ml_v[:, 0, h, :], start=True, stop=False)
                full(nc.tensor.matmul(bank(s)[:, T:T + 129], w[:, T:T + P], ml_v[:, 1, h, :],
                                      start=False, stop=True), s)
            turn_over("ml_out", ml_hn)
            moved(pe, SLOT["turn_ml_out"], 4)
            to_acc("a_out", tokens(ml_outT), KC)

            def peer(layer):
                turn_over(f"ln{layer}_0", X)
                moved(pe, SLOT[f"turn_ln{layer}_0"], 4)
                for j in range(16):
                    split_tall(f"wq{layer}", j, SLOT[f"wq{layer}"] + j)
                moved(pe, SLOT[f"wq{layer}"], 16)
                for half in range(2):
                    i = TILE[f"keys{layer}"] + half
                    tile_here(pe, i)
                    for tb in range(TB):
                        for g in range(2):
                            s = SLOT[f"scores{layer}"] + 4 * half + 2 * tb + g
                            slot_free(pe, s)
                            for j in range(4):
                                mm = nc.tensor.matmul(bank(s)[:, j * P:(j + 1) * P],
                                                      peer_q[:, 8 * half + 4 * g + j, tb * P:(tb + 1) * P],
                                                      tall(i)[:, 4 * g + j, :], start=True, stop=True)
                                if tb == 0 and g == 0 and j == 0:
                                    begins_tile(mm)
                            full(mm, s)
                with pe.Fori(0, EXPERT_TILES // BODY, 1) as turns:
                    for j in range(BODY):
                        split_tall(f"u{layer}", j, SLOT[f"u{layer}"] + j, turns)
                pe.wait_ge(routes_ready, layer + 1)
                for q in range(2):
                    s = SLOT[f"routes{layer}"] + q
                    slot_free(pe, s)
                    for k, src in enumerate(((route_index[0], route_index[1]), (FV,))[q]):
                        for tb in range(TB):
                            mm = nc.tensor.transpose(bank(s)[:, (2 * k + tb) * P:(2 * k + tb + 1) * P],
                                                     src[:, tb].rearrange("p h k -> p (h k)"), ident[:])
                    full(mm, s)
                sbase = SLOT[f"gates{layer}"]
                with pe.Fori(0, T // 16, 1) as turns:
                    for k in range(4):
                        slot_free(pe, sbase + k, turns)
                        pe.wait_ge(gate_rows, turns * 4 + (T // 4 * layer + k + 1))
                        pe.wait_ge(place_rows, turns * 4 + (T // 4 * layer + k + 1))
                        for t in range(4):
                            mm = nc.tensor.matmul(bank(sbase + k)[:, t * P:(t + 1) * P], place[:, k, t],
                                                  gated_rows[:, k, t], start=True, stop=True)
                        full(mm, sbase + k)
                pe.wait_ge(acc_moved, ACC[f"v{layer}"])
                for b in range(4):
                    nc.tensor.matmul(acc[:, b, :], zeros[:, 0:P], zeros[:], start=True, stop=False)
                with pe.Fori(0, EXPERT_TILES // BODY, 1) as turns:
                    for j in range(BODY):
                        pe.wait_ge(staged, turns * BODY + (EXPERT_TILES * layer + j + 1))
                        split_wide(f"v{layer}", j, (x_hi, x_lo), j, False, False, turns)
                for b in range(4):
                    mm = nc.tensor.matmul(acc[:, b, :], zeros[:, 0:P], zeros[:], start=False, stop=True)
                mm.then_inc(acc_full, 1)
                pe.wait_ge(p_in, 16 * (layer + 1))
                to_acc(f"ple_proj{layer}", tokens(pT), 2)
                turn_over(f"ln{layer}_1", X)
                moved(pe, SLOT[f"turn_ln{layer}_1"], 4)
                split_to_acc(f"ple_gate{layer}")

            peer(0)

            turn_over("x1", X)
            moved(pe, SLOT["turn_x1"], 4)
            split_to_acc("kv_q_down", width=LATENTS)
            pe.wait_ge(latents_ready, 1)
            for q, parts in enumerate((((0, 0), (P, 1)), ((320, 0), (320 + P, 1)), ((320 + 2 * P, 0), (None, 1)))):
                s = SLOT["latents"] + q
                slot_free(pe, s)
                for at, c in parts:
                    for tb in range(TB):
                        src = latent[:, tb, at:at + P] if at is not None else \
                            rope_k2[:, tb].rearrange("p a b c -> p (a b c)")
                        mm = nc.tensor.transpose(bank(s)[:, (2 * c + tb) * P:(2 * c + tb + 1) * P], src, ident[:])
                full(mm, s)
            moved(pe, SLOT["latents"], 3)

            def up(name, lat, n):
                for k in range(n):
                    tile_here(pe, TILE[name] + k)
                for h in range(H8):
                    s = SLOT[name] + h
                    slot_free(pe, s)
                    for k in range(n):
                        if k == n - 1 and h == H8 - 1:
                            begins_tile(nc.tensor.matmul(bank(s)[:, 511:512], zeros[:, 0:P], zeros[:, 0:1],
                                                         start=False, stop=False, skip_group_check=True))
                        mm = nc.tensor.matmul(bank(s)[:, 0:T], tile(TILE[name] + k)[:, h * P:(h + 1) * P],
                                              latT[:, lat + k, :], start=(k == 0), stop=(k == n - 1))
                        if (k == 0 and h == 0) or (0 < k < n - 1 and h == H8 - 1):
                            begins_tile(mm)
                    full(mm, s)

            up("up_k", 0, 2)
            to_acc("up_v", lambda k, tb: latT[:, k, tb * P:(tb + 1) * P], 2)
            up("uq_nope", 2, 3)
            to_acc("uq_rope", lambda k, tb: latT[:, 2 + k, tb * P:(tb + 1) * P], 3, width=512)
            pe.wait_ge(rope_ready, 1)
            for q in range(2):
                s = SLOT["rope"] + q
                slot_free(pe, s)
                for c in range(2):
                    for tb in range(TB):
                        src = q_rot[:, tb].rearrange("p a b c -> p (a b c)")[:, (2 * q + c) * P:(2 * q + c + 1) * P]
                        mm = nc.tensor.transpose(bank(s)[:, (2 * c + tb) * P:(2 * c + tb + 1) * P], src, ident[:])
                full(mm, s)

            def mla_scores(h):
                s = SLOT[("mla", "scores", h)]
                slot_free(pe, s)
                r = head_rows(h)
                for tb in range(TB):
                    n, at = (tb + 1) * P, tb * P
                    o = bank(s)[:, at:at + n]
                    nc.tensor.matmul(o, q_nope[:, h, at:at + P], k_nope[:, h, 0:n], start=True, stop=False)
                    nc.tensor.matmul(o, q_ropeT[r, h // 2, at:at + P], latT[r, 5, 0:n], start=False, stop=False)
                    mm = nc.tensor.matmul(o[:, at:at + P], ident[:], mla_mask[:], start=False, stop=True)
                full(mm, s)

            moved(pe, SLOT["up_k"], 8)
            moved(pe, SLOT["uq_nope"], 8)
            moved(pe, SLOT["rope"], 2)
            acc_gone(pe, "up_v")
            pe.wait_ge(rope_in, 48)
            mla_scores(0)
            for h in range(H8):
                if h + 1 < H8:
                    mla_scores(h + 1)
                pe.wait_ge(probs_ready, h + 1)
                s = SLOT[("mla", "probs", h)]
                slot_free(pe, s)
                for k in range(3):
                    mm = nc.tensor.transpose(bank(s)[:, k * P:(k + 1) * P], mla_p[:, h % 2, k * P:(k + 1) * P],
                                             ident[:])
                full(mm, s)
                moved(pe, s)
                s = SLOT[("mla", "out", h)]
                slot_free(pe, s)
                nc.tensor.matmul(bank(s)[:, 0:T], mla_v[:, 0, h * P:(h + 1) * P], mla_pT[:, h % 2, 0:T],
                                 start=True, stop=False)
                full(nc.tensor.matmul(bank(s)[:, P:T], mla_v[:, 1, h * P:(h + 1) * P], mla_pT[:, h % 2, T:T + P],
                                      start=False, stop=True), s)
            moved(pe, SLOT[("mla", "out", H8 - 1)])
            to_acc("b_out", lambda k, tb: mla_oT[:, k, tb * P:(tb + 1) * P], KC)
            peer(1)

            def ffn(n):
                sbase = SLOT[f"ffn{n}"]
                with pe.Fori(0, 2 * FF_TILES // BODY, 1) as turns:
                    for j in range(BODY):
                        split_tall(f"ffn{n}_in", j, sbase + j, turns)
                for j in range(2 * FF_TILES - 2 * FF_TILES % BODY, 2 * FF_TILES):
                    split_tall(f"ffn{n}_in", j, sbase + j)
                pe.wait_ge(acc_moved, ACC[f"ffn{n}_out"])
                for j in range(FF_TILES):
                    moved(pe, sbase + 2 * j + 1)
                    mm = split_wide(f"ffn{n}_out", j, (act_hi, act_lo), j, j == 0, j == FF_TILES - 1)
                mm.then_inc(acc_full, 1)

            turn_over("rms1", xn)
            moved(pe, SLOT["turn_rms1"], 4)
            ffn(1)

            turn_over("rms2", xn)
            moved(pe, SLOT["turn_rms2"], 4)
            split_to_acc("rqk")
            split_to_acc("rv")
            split_to_acc("rg")
            for j in range(8):
                split_tall("nqk", j, SLOT["nqk"] + j)
            split_to_acc("nv", width=512, per_tile=2)
            split_to_acc("g_ret")
            split_to_acc("g_na")
            turn_over("rqk", rqk_rot.rearrange("p t h a b -> p t (h a b)"))
            moved(pe, SLOT["turn_rqk"], 4)

            def ret_scores(h):
                s = SLOT[("ret", "scores", h)]
                slot_free(pe, s)
                for m in range(TB):
                    mm = nc.tensor.matmul(bank(s)[:, m * T:(m + 1) * T], rqkT[:, RET_H + h, m * P:(m + 1) * P],
                                          rqkT[:, h, :], start=True, stop=True)
                full(mm, s)

            acc_gone(pe, "rv")
            ret_scores(0)
            for h in range(RET_H):
                if h + 1 < RET_H:
                    ret_scores(h + 1)
                moved(pe, SLOT[("ret", "scores", h)])
                s = SLOT[("ret", "out", h)]
                slot_free(pe, s)
                for tb in range(TB):
                    for m in range(TB):
                        at = m * T + tb * P
                        mm = nc.tensor.matmul(bank(s)[:, tb * T:(tb + 1) * T], ret_p[:, h % 2, at:at + P],
                                              ret_v[:, m, h * T:(h + 1) * T], start=(m == 0), stop=(m == 1))
                full(mm, s)

            def na_scores(h):
                s = SLOT[("na", "scores", h)]
                slot_free(pe, s)
                r = head_rows(h)
                for tb in range(TB):
                    mm = nc.tensor.matmul(bank(s)[:, tb * T:(tb + 1) * T], na_qk[r, h // 2, tb * P:(tb + 1) * P],
                                          na_qk[r, 4 + h // 2, :], start=True, stop=True)
                full(mm, s)

            moved(pe, SLOT["nqk"], 8)
            acc_gone(pe, "nv")
            na_scores(0)
            for h in range(H8):
                if h + 1 < H8:
                    na_scores(h + 1)
                pe.wait_ge(probs_ready, H8 + h + 1)
                s = SLOT[("na", "probs", h)]
                slot_free(pe, s)
                for m in range(TB):
                    for tb in range(TB):
                        mm = nc.tensor.transpose(bank(s)[:, (2 * m + tb) * P:(2 * m + tb + 1) * P],
                                                 na_s[:, h % 2, tb * T + m * P:tb * T + (m + 1) * P], ident[:])
                full(mm, s)
                moved(pe, s)
                s = SLOT[("na", "out", h)]
                slot_free(pe, s)
                for m in range(TB):
                    mm = nc.tensor.matmul(bank(s)[head_rows(h), 0:T], na_v[:, m, h * 64:(h + 1) * 64],
                                          na_pT[:, h % 2, m * T:(m + 1) * T], start=(m == 0), stop=(m == 1))
                full(mm, s)
            turn_over("ret", ret_y.rearrange("p t h n -> p t (h n)"))
            moved(pe, SLOT["turn_ret"], 4)
            split_to_acc("ret_out")
            moved(pe, SLOT[("na", "out", H8 - 1)])
            to_acc("na_out", tokens(na_oT), 4)
            turn_over("merged", merged)
            moved(pe, SLOT["turn_merged"], 4)
            split_to_acc("mix_out")
            turn_over("rms3", xn)
            moved(pe, SLOT["turn_rms3"], 4)
            ffn(2)

        @block.scalar
        def _(act):
            step = Steps(act, act_step)
            sqrts = [0]
            S = nc.scalar

            def square_roots(n):
                sqrts[0] += 1
                act.wait_ge(sqrt_wanted, sqrts[0])
                S.activation(col[:, 1, 0:n], col[:, 0, 0:n], ACT.Sqrt).then_inc(sqrt_done, 1)

            def turned(name, dst, gain=None):
                for q in range(2):
                    s = SLOT[f"turn_{name}"] + q
                    slot_here(act, s)
                    if gain is None:
                        free(S.copy(dst[:, 2 * q:2 * q + 2, :].rearrange("p a b -> p (a b)"), bank(s)), s)
                    else:
                        for c in range(2):
                            k = 2 * q + c
                            ins = S.mul(dst[:, k, :], bank(s)[:, c * T:(c + 1) * T], cols[:, gain + k:gain + k + 1])
                            if c == 0:
                                step(ins)
                        free(ins, s)

            def turned_parts(name, gain=None):
                for q in range(4):
                    s = SLOT[f"turn_{name}"] + q
                    slot_here(act, s)
                    if gain is None:
                        ins = S.copy(x_hi[:, 2 * q:2 * q + 2, :].rearrange("p a b -> p (a b)"), bank(s))
                    else:
                        for c in range(2):
                            k = 2 * q + c
                            ins = S.mul(x_hi[:, k, :], bank(s)[:, c * T:(c + 1) * T], cols[:, gain + k:gain + k + 1])
                    ins.then_inc(x_hi_ready, 1)

            def highs(name, first, last, following=None):
                for j in range(first, last):
                    take_high(act, name, j)
                if following:
                    take_high(act, following, 0)

            def split_from_slots(name, dst, n, following=None):
                for j in range(1, n + 2):
                    if j < n:
                        take_high(act, name, j)
                    elif j == n and following:
                        take_high(act, following, 0)
                    if j >= 2:
                        s = SLOT[name] + j - 2
                        slot_here(act, s)
                        free(S.copy(dst[:, j - 2, :], bank(s)[:, 0:T]), s)

            def from_slots(name, dst, n):
                for j in range(n):
                    s = SLOT[name] + j
                    slot_here(act, s)
                    free(S.copy(dst[:, j, :], bank(s)[:, 0:T]), s)

            def from_acc(name, dst, func, width=D):
                acc_here(act, name)
                for tb in range(TB):
                    ins = S.activation(dst(tb), acc_rows(tb)[:, 0:width], func)
                    if tb == 0:
                        step(ins)
                step.wait()
                ins.then_inc(acc_moved, 1)

            act.dma_start(XT[:], a["xT"]).then_inc(xt_in, 16)
            act.dma_start(ml_gate_w, a["ml_gate_w"]).then_inc(gate_w_in, 16)
            act.dma_start(ml_bias[0:H8, :], a["ml_bias"]).then_inc(gate_w_in, 16)
            for dst, name in CONSTS:
                act.dma_start(dst, a[name]).then_inc(consts_in, 16)
            act.dma_start(X[:], a["x"]).then_inc(x_in, 16)

            def log_sigmoid_part(dst, src, tmp):
                step(S.activation(tmp, src, ACT.Abs))
                step.wait()
                step(S.activation(tmp, tmp, ACT.Exp, scale=-1.0))
                step.wait()
                return S.activation(dst, tmp, ACT.Ln, bias=1.0)

            act.wait_ge(gates_split, 1)
            log_sigmoid_part(ml_rows[0:H8, 2, :], ml_rows[0:H8, 1, :], ml_rows[0:H8, 3, :]).then_inc(gates_log, 1)
            from_slots("a_qk", ml_qk, 8)
            acc_here(act, "a_v")
            for tb in range(TB):
                ins = S.copy(ml_v[:, tb, :, 0:P], acc_rows(tb).rearrange("p (h n) -> p h n", h=H8))
                if tb == 0:
                    step(ins)
            step.wait()
            ins.then_inc(acc_moved, 1)
            act.wait_ge(gates_scanned, 1)
            S.activation(ml_rows[0:H8, 9, :], ml_rows[0:H8, 8, :], ACT.Exp, scale=-1.0).then_inc(floor_ready, 1)
            from_acc("a_og", lambda tb: ml_sig[:, tb, :], ACT.Sigmoid)
            act.wait_ge(gate_cols_ready, 1)

            def ml_decay(h):
                s = SLOT[("ml", "decay", h)]
                slot_here(act, s)
                if h >= 2:
                    moved(act, SLOT[("ml", "scores", h - 2)])
                step(S.activation(ml_w[:, h % 2, 0:T], bank(s)[:, 0:T], ACT.Exp, scale=-1.0,
                                  bias=gate_cols[:, 0, h:h + 1]))
                step.wait()
                ins = S.activation(ml_w[:, h % 2, T:T + P], bank(s)[:, T:T + P], ACT.Exp, scale=-1.0,
                                   bias=gate_cols[:, 1, h:h + 1])
                free(ins, s)

            ml_decay(0)
            for h in range(H8):
                if h + 1 < H8:
                    ml_decay(h + 1)
                s = SLOT[("ml", "out", h)]
                slot_here(act, s)
                free(S.copy(ml_raw[:, :, h, :], bank(s).rearrange("p (t n) -> p t n", t=TB)[:, :, 0:129]), s)
            square_roots(16)
            turned("ml_out", ml_outT, GAIN_ML)
            square_roots(2)

            def peer(layer):
                take_high(act, f"wq{layer}", 0)
                turned_parts(f"ln{layer}_0")
                split_from_slots(f"wq{layer}", peer_q, 16)
                highs(f"u{layer}", 0, 2)
                for half in range(2):
                    for tb in range(TB):
                        for g in range(2):
                            s = SLOT[f"scores{layer}"] + 4 * half + 2 * tb + g
                            slot_here(act, s)
                            at = tb * 2048 + (8 * half + 4 * g) * P
                            free(S.copy(SC[:, at:at + 512], bank(s)), s)
                base = SLOT[f"u{layer}"]

                def experts(j, turns=0):
                    slot_here(act, base + j, turns * 2)
                    free(S.activation(expert_rows(j, turns), bank(base + j)[:, 0:T], ACT.Gelu), base + j)

                for j in range(2, BODY):
                    take_high(act, f"u{layer}", j)
                    experts(j - 2)
                with act.Fori(1, EXPERT_TILES // BODY, 1) as turns:
                    for j in range(BODY):
                        take_high(act, f"u{layer}", j, turns)
                        experts(j - 2, turns)
                for j in range(EXPERT_TILES - 2, EXPERT_TILES):
                    experts(j)
                act.wait_ge(softmax_wanted, layer + 1)
                S.activation(FV[:], FV[:], ACT.Exp).then_inc(softmax_exps, 1)
                gates = SLOT[f"gates{layer}"]

                def place_distances(k, turns):
                    slot_here(act, gates + k - 4, turns)
                    for t in range(4):
                        ins = S.activation(distance[:, k, t], iota[:], ACT.Abs,
                                           bias=route_T[:, 1, ds(turns * 16 + (4 * k + t), 1)])
                    ins.then_inc(distances, 1)

                def places(k, turns):
                    act.wait_ge(distances, turns * 4 + (T // 4 * layer + k + 1))
                    S.activation(place[:, k], distance[:, k], ACT.Relu, scale=-1.0, bias=1.0
                                 ).then_inc(place_rows, 1)

                act.wait_ge(routes_turned, layer + 1)
                with act.Fori(0, T // 16, 1) as turns:
                    place_distances(0, turns)
                    for k in range(4):
                        if k + 1 < 4:
                            place_distances(k + 1, turns)
                        places(k, turns)
                moved(act, gates, T // 4)

                def stage(j, turns=0):
                    act.wait_ge(tiles_begun, turns * BODY + (TILE[f"v{layer}"] + j - BODY + 2))
                    S.copy(x_hi[:, j % BODY, :], expert_rows(j, turns)).then_inc(staged_hi, 1)

                stage(0)
                with act.Fori(0, EXPERT_TILES // BODY - 1, 1) as turns:
                    for j in range(BODY):
                        take_high(act, f"v{layer}", j, turns)
                        stage(j + 1, turns)
                for j in range(EXPERT_TILES - BODY, EXPERT_TILES):
                    take_high(act, f"v{layer}", j)
                    if j + 1 < EXPERT_TILES:
                        stage(j + 1)
                square_roots(2)
                take_high(act, f"ple_gate{layer}", 0)
                acc_here(act, f"ple_proj{layer}")
                for tb in range(TB):
                    ins = S.copy(ple_side[:, tb, :], acc_rows(tb))
                    if tb == 0:
                        step(ins)
                step.wait()
                ins.then_inc(acc_moved, 1)
                turned_parts(f"ln{layer}_1")
                highs(f"ple_gate{layer}", 1, 8, following=AFTER_PEER[layer])
                from_acc(f"ple_gate{layer}", lambda tb: ple_sig[:, tb, :], ACT.Sigmoid)

            peer(0)

            act.wait_ge(turn_ready, TURN["x1"] + 1)
            act.dma_start(inv_freq, a["inv_freq"]).then_inc(rope_in, 16)
            act.dma_start(pos_i, a["positions"]).then_inc(rope_in, 16)
            act.dma_start(mla_mask, a["mla_mask"]).then_inc(rope_in, 16)
            turned_parts("x1")
            highs("kv_q_down", 1, 8)
            act.wait_ge(angles_ready, 1)
            S.activation(sincos.rearrange("p a b c -> p (a b c)"), angle.rearrange("p a b c -> p (a b c)"),
                         ACT.Sin).then_inc(sines_ready, 1)
            acc_here(act, "kv_q_down")
            for tb in range(TB):
                step(S.copy(latent[:, tb, :], acc_rows(tb)[:, 0:LATENTS]))
            for tb in range(TB):
                for k, (lo, hi) in enumerate(((0, KV_RANK), (KV_RANK + ROPE, LATENTS))):
                    step.wait()
                    step(S.activation(sq_junk[:, 0:hi - lo], acc_rows(tb)[:, lo:hi], ACT.Square,
                                      accum_out=col[:, 2, 2 * tb + k:2 * tb + k + 1]))
            step.wait()
            act.sem_inc(sums_ready, 1)
            act.sem_inc(acc_moved, 1)
            square_roots(4)
            for q, parts in enumerate((((0, GAIN_KV), (1, GAIN_KV + 1)), ((2, GAIN_Q), (3, GAIN_Q + 1)),
                                       ((4, GAIN_Q + 2), (5, None)))):
                s = SLOT["latents"] + q
                slot_here(act, s)
                for c, (k, gain) in enumerate(parts):
                    src = bank(s)[:, c * T:(c + 1) * T]
                    ins = S.copy(latT[:, k, :], src) if gain is None else \
                        S.mul(latT[:, k, :], src, cols[:, gain:gain + 1])
                    if c == 0:
                        step(ins)
                free(ins, s)
            from_slots("up_k", k_nope, 8)
            from_acc("up_v", lambda tb: mla_v[:, tb, :], ACT.Copy)
            from_slots("uq_nope", q_nope, 8)
            acc_here(act, "uq_rope")
            for tb in range(TB):
                ins = S.copy(q_rope[:, tb].rearrange("p a h c -> p h a c"),
                             acc_rows(tb)[:, 0:512].rearrange("p (h a c) -> p h a c", h=H8, a=2))
                if tb == 0:
                    step(ins)
            step.wait()
            ins.then_inc(acc_moved, 1)
            for q in range(2):
                s = SLOT["rope"] + q
                slot_here(act, s)
                free(S.copy(q_ropeT[:, 2 * q:2 * q + 2, :].rearrange("p a b -> p (a b)"), bank(s)), s)

            def exponents(name, n, h, dst, parts, scale):
                act.wait_ge(maxima_ready, n + h + 1)
                for tb, (lo, hi) in enumerate(parts):
                    src = bank(SLOT[(name, "scores", h)]) if name == "mla" else na_s[:, h % 2]
                    step(S.activation(dst[:, h % 2, lo:hi], src[:, lo:hi], ACT.Exp, scale=scale,
                                      bias=col[:, 2 + h % 2, 8 + tb:9 + tb],
                                      accum_out=col[:, 4 + h % 2, tb:tb + 1]))
                step.wait()
                act.sem_inc(exps_ready, 1)

            def probs_over(name, h, dst, width):
                s = SLOT[(name, "probs", h)]
                slot_here(act, s)
                free(S.copy(dst[:, h % 2, :], bank(s)[:, 0:width]), s)

            exponents("mla", 0, 0, mla_p, ((0, P), (P, P + T)), MLA_SCALE)
            for h in range(H8):
                if h + 1 < H8:
                    exponents("mla", 0, h + 1, mla_p, ((0, P), (P, P + T)), MLA_SCALE)
                probs_over("mla", h, mla_pT, 384)
            square_roots(2)
            peer(1)

            def rms_of(src_ready, src, n=TB):
                act.wait_ge(*src_ready)
                for tb in range(n):
                    step.wait()
                    step(S.activation(sq_junk, src(tb), ACT.Square, accum_out=col[:, 2, tb:tb + 1]))
                step.wait()
                act.sem_inc(sums_ready, 1)

            def ffn(n):
                base, looped = SLOT[f"ffn{n}"], 2 * FF_TILES // BODY

                def gate(j, turns=0):
                    s = base + 2 * j
                    slot_here(act, s, turns * 2)
                    before = s + 1 - 8
                    act.wait_ge(slot_moved[before % 4], turns * 2 + (before // 4 + 1))
                    free(S.activation(silu_g[:, j % 4, :], bank(s)[:, 0:T], ACT.Silu), s)

                def pair(j, turns=0):
                    take_high(act, f"ffn{n}_in", 2 * j + 1, turns)
                    gate(j, turns)
                    take_high(act, f"ffn{n}_in", 2 * j + 2, turns)

                with act.Fori(0, looped, 1) as turns:
                    for j in range(4):
                        pair(j, turns)
                for j in range(4 * looped, FF_TILES):
                    pair(j)
                highs(f"ffn{n}_out", 1, FF_TILES, following="rqk" if n == 1 else None)

            def post_norm(name):
                rms_of((acc_full, ACC[name] + 1), acc_rows)
                square_roots(2)

            rms_of((turn_ready, TURN["x2"] + 1), lambda tb: X[:, tb, :])
            square_roots(2)
            turned_parts("rms1", GAIN_FFN1)
            ffn(1)
            post_norm("ffn1_out")
            rms_of((rows_used, 5), lambda tb: X[:, tb, :])
            square_roots(2)
            turned_parts("rms2", GAIN_MIX)
            act.wait_ge(mix_in, 16 * 6)
            highs("rqk", 1, 4)
            log_sigmoid_part(ret_lg[:, 1, :], ret_logit, ret_lg[:, 0, :]).then_inc(logits_ready, 1)
            highs("rqk", 4, 8, following="rv")
            from_acc("rqk", lambda tb: rqk[:, tb].rearrange("p h a b -> p (h a b)"), ACT.Copy)
            highs("rv", 1, 8, following="rg")
            from_acc("rv", lambda tb: ret_v[:, tb, :], ACT.Copy)
            highs("rg", 1, 8, following="nqk")
            from_acc("rg", lambda tb: ret_g[:, tb, :], ACT.Silu)
            split_from_slots("nqk", na_qk, 8, following="nv")
            highs("nv", 1, 4, following="g_ret")
            from_acc("nv", lambda tb: na_v[:, tb, :], ACT.Copy, width=512)
            highs("g_ret", 1, 8, following="g_na")
            from_acc("g_ret", lambda tb: sig_ret[:, tb, :], ACT.Sigmoid)
            highs("g_na", 1, 8, following="ret_out")
            from_acc("g_na", lambda tb: sig_na[:, tb, :], ACT.Sigmoid)
            turned("rqk", rqkT)

            def ret_decay(h):
                act.wait_ge(decay_wanted, h + 1)
                S.activation(ret_d[:, h % 2, :], ret_d[:, h % 2, :], ACT.Exp).then_inc(decay_ready, 1)

            ret_decay(0)
            for h in range(RET_H):
                if h + 1 < RET_H:
                    ret_decay(h + 1)
                s = SLOT[("ret", "out", h)]
                slot_here(act, s)
                step(S.copy(ret_y[:, :, h, :], bank(s).rearrange("p (t n) -> p t n", t=TB)))
                for tb in range(TB):
                    step.wait()
                    step(S.activation(ret_junk, bank(s)[:, tb * T:(tb + 1) * T], ACT.Square,
                                      accum_out=col[:, 3, RET_H * tb + h:RET_H * tb + h + 1]))
                step.wait()
                act.sem_inc(slot_moved[s % 4], 1)
            act.sem_inc(sums_ready, 1)
            square_roots(8)
            exponents("na", H8, 0, na_s, ((0, T), (T, 2 * T)), 1.0)
            for h in range(H8):
                if h + 1 < H8:
                    exponents("na", H8, h + 1, na_s, ((0, T), (T, 2 * T)), 1.0)
                probs_over("na", h, na_pT, 512)
                s = SLOT[("na", "out", h)]
                slot_here(act, s)
                free(S.copy(na_oT[head_rows(h), h // 2, :], bank(s)[head_rows(h), 0:T]), s)
            turned_parts("ret")
            highs("ret_out", 1, 8)
            acc_here(act, "na_out")
            take_high(act, "mix_out", 0)
            turned_parts("merged")
            highs("mix_out", 1, 8, following="ffn2_in")
            post_norm("mix_out")
            rms_of((rows_used, 6), lambda tb: X[:, tb, :])
            square_roots(2)
            turned_parts("rms3", GAIN_FFN2)
            ffn(2)
            post_norm("ffn2_out")

        @block.vector
        def _(dve):
            step = Steps(dve, dve_step)
            counts = {"sqrt": 0, "rows": 0, "sums": 0}
            V = nc.vector

            def tt(out, x, y, op):
                step(V.tensor_tensor(out, x, y, op))

            def ts(out, x, s1, s2, op0, op1=None):
                step(V.tensor_scalar(out, x, s1, s2, op0, op1) if op1 is not None
                     else V.tensor_scalar(out, x, s1, None, op0))

            def stt(out, x, s, y, op0, op1):
                step(V.scalar_tensor_tensor(out=out, in0=x, scalar=s, in1=y, op0=op0, op1=op1))

            def wait():
                step.wait()

            def inverse_roots(n):
                wait()
                dve.sem_inc(sqrt_wanted, 1)
                counts["sqrt"] += 1
                dve.wait_ge(sqrt_done, counts["sqrt"])
                step(V.reciprocal(col[:, 1, 0:n], col[:, 1, 0:n]))
                wait()

            def turned(name, dst, gain=None):
                for q in range(2, 4):
                    s = SLOT[f"turn_{name}"] + q
                    slot_here(dve, s)
                    if gain is None:
                        free(V.tensor_copy(dst[:, 2 * q:2 * q + 2, :].rearrange("p a b -> p (a b)"), bank(s)), s)
                    else:
                        for c in range(2):
                            k = 2 * q + c
                            ins = V.tensor_scalar(dst[:, k, :], bank(s)[:, c * T:(c + 1) * T],
                                                  cols[:, gain + k:gain + k + 1], None, ALU.mult)
                            if c == 0:
                                step(ins)
                        free(ins, s)

            def turned_parts(name, gain=None):
                for q in range(4):
                    s = SLOT[f"turn_{name}"] + q
                    dve.wait_ge(x_hi_ready, 4 * PART_TURNS.index(name) + q + 1)
                    if gain is None:
                        c = slice(2 * q, 2 * q + 2)
                        ins = V.tensor_tensor(x_lo[:, c, :], bank(s).rearrange("p (a b) -> p a b", a=2),
                                              x_hi[:, c, :], ALU.subtract)
                    else:
                        for c in range(2):
                            k = 2 * q + c
                            ins = V.scalar_tensor_tensor(out=x_lo[:, k, :], in0=bank(s)[:, c * T:(c + 1) * T],
                                                         scalar=cols[:, gain + k:gain + k + 1], in1=x_hi[:, k, :],
                                                         op0=ALU.mult, op1=ALU.subtract)
                    free(ins, s)

            def lows(name, first, last, following=None):
                for j in range(first, last):
                    take_low(dve, name, j)
                if following:
                    take_low(dve, following, 0)

            def rows_here():
                counts["rows"] += 1
                dve.wait_ge(rows_in, 16 * sum(ROW_SETS[:counts["rows"]]))

            def layer_norm(name):
                acc_here(dve, name)
                for tb in range(TB):
                    stt(X[:, tb, :], X[:, tb, :], DN_ALPHA, acc_rows(tb), ALU.mult, ALU.add)
                wait()
                dve.sem_inc(acc_moved, 1)
                for tb in range(TB):
                    for f in range(2):
                        step(V.bn_stats(stats[:, 2 * tb + f, :], X[:, tb, 512 * f:512 * f + 512]))
                wait()
                for tb in range(TB):
                    step(V.bn_aggr(mv[:, tb, :], stats[:, 2 * tb:2 * tb + 2, :]))
                wait()
                ts(col[:, 0, 0:TB], mv[:, 0:TB, 1], NORM_EPS, None, ALU.add)
                inverse_roots(TB)
                rows_here()
                for tb in range(TB):
                    ts(X[:, tb, :], X[:, tb, :], mv[:, tb, 0:1], col[:, 1, tb:tb + 1], ALU.subtract, ALU.mult)
                wait()
                for tb in range(TB):
                    tt(X[:, tb, :], X[:, tb, :], rows[:, 0, :], ALU.mult)
                wait()
                for tb in range(TB):
                    tt(X[:, tb, :], X[:, tb, :], rows[:, 1, :], ALU.add)
                wait()
                dve.sem_inc(turn_ready, 1)
                dve.sem_inc(rows_used, 1)

            def mean_square_roots(n, width, eps, src=2):
                counts["sums"] += 1
                dve.wait_ge(sums_ready, counts["sums"])
                ts(col[:, 0, 0:n], col[:, src, 0:n], 1.0 / width, eps, ALU.mult, ALU.add)
                inverse_roots(n)

            def pre_norm():
                mean_square_roots(TB, D, RMS_EPS)
                for tb in range(TB):
                    ts(xn[:, tb, :], X[:, tb, :], col[:, 1, tb:tb + 1], None, ALU.mult)
                wait()
                dve.sem_inc(turn_ready, 1)

            def post_norm(name, weight):
                mean_square_roots(TB, D, RMS_EPS)
                rows_here()
                for tb in range(TB):
                    stt(post_tmp[:, tb, :], acc_rows(tb), col[:, 1, tb:tb + 1], rows[:, 0, :], ALU.mult, ALU.mult)
                wait()
                dve.sem_inc(acc_moved, 1)
                for tb in range(TB):
                    stt(X[:, tb, :], post_tmp[:, tb, :], weight, X[:, tb, :], ALU.mult, ALU.add)
                wait()
                dve.sem_inc(rows_used, 1)

            dve.wait_ge(gate_w_in, 32)
            dve.wait_ge(consts_in, 16 * CONST_LOADS)
            s = SLOT["gates"]
            slot_here(dve, s)
            R = lambda k: ml_rows[0:H8, k, :]
            step(V.memset(R(10), 1.0))
            step(V.memset(R(11), 0.0))
            ts(R(0), bank(s)[0:H8, 0:T], ml_bias[0:H8, 0:1], None, ALU.add)
            ts(R(1), bank(s)[0:H8, T:2 * T], ml_bias[0:H8, 1:2], None, ALU.add)
            wait()
            dve.sem_inc(slot_moved[s % 4], 1)
            dve.sem_inc(gates_split, 1)
            ts(R(4), R(1), 0.0, None, ALU.min)
            wait()
            dve.wait_ge(gates_log, 1)
            tt(R(4), R(4), R(2), ALU.subtract)
            wait()
            step(V.tensor_tensor_scan(R(5), R(10), R(4), 0.0, ALU.mult, ALU.add))
            wait()
            tt(R(6), R(0), R(5), ALU.subtract)
            wait()
            step(V.tensor_tensor_scan(R(7), R(6), R(11), 0.0, ALU.max, ALU.add))
            wait()
            tt(R(8), R(5), R(7), ALU.add)
            wait()
            dve.sem_inc(gates_scanned, 1)
            s = SLOT["gate_cols"]
            slot_here(dve, s)
            step(V.tensor_copy(gate_cols.rearrange("p a b -> p (a b)"), bank(s)[:, 0:32]))
            wait()
            dve.sem_inc(slot_moved[s % 4], 1)
            dve.sem_inc(gate_cols_ready, 1)
            for h in range(H8):
                s = SLOT[("ml", "scores", h)]
                slot_here(dve, s)
                moved(dve, SLOT[("ml", "decay", h)])
                if h >= 2:
                    slot_here(dve, SLOT[("ml", "out", h - 2)])
                free(V.scalar_tensor_tensor(out=ml_p[:, h % 2, :], in0=bank(s)[:, 0:384], scalar=ML_SCALE,
                                            in1=ml_w[:, h % 2, :], op0=ALU.mult, op1=ALU.mult), s)
            for h in range(H8):
                moved(dve, SLOT[("ml", "out", h)])
            for tb in range(TB):
                for h in range(H8):
                    step(V.bn_stats(stats[:, H8 * tb + h, :], ml_raw[:, tb, h, 0:P]))
            c16 = lambda k: col[:, k, 0:16].rearrange("p (t h) -> p t h", t=TB)
            stt(c16(2), ml_raw[:, :, :, 128], -1.0, ml_raw[:, :, :, 128], ALU.mult, ALU.max)
            wait()
            for k in range(16):
                step(V.bn_aggr(mv[:, k, :], stats[:, k:k + 1, :]))
            tt(c16(3), c16(2), gate_cols[:, 2:4, :], ALU.max)
            wait()
            step(V.reciprocal(col[:, 2, :], col[:, 3, :]))
            wait()
            tt(col[:, 3, :], col[:, 2, :], col[:, 2, :], ALU.mult)
            wait()
            tt(col[:, 4, :], col[:, 3, :], mv[:, :, 1], ALU.mult)
            wait()
            ts(col[:, 0, :], col[:, 4, :], NORM_EPS, None, ALU.add)
            inverse_roots(16)
            tt(col[:, 5, :], col[:, 1, :], col[:, 2, :], ALU.mult)
            wait()
            for tb in range(TB):
                for h in range(H8):
                    k = H8 * tb + h
                    ts(ml_hn[:, tb, h * P:(h + 1) * P], ml_raw[:, tb, h, 0:P], mv[:, k, 0:1], col[:, 5, k:k + 1],
                       ALU.subtract, ALU.mult)
            acc_gone(dve, "a_og")
            wait()
            for tb in range(TB):
                tt(ml_hn[:, tb, :], ml_hn[:, tb, :], ml_sig[:, tb, :], ALU.mult)
            wait()
            dve.sem_inc(turn_ready, 1)
            turned("ml_out", ml_outT, GAIN_ML)
            dve.wait_ge(x_in, 16)
            layer_norm("a_out")

            def top16(lists, values, where, between):
                n = len(lists)
                every = 5 if n == 16 else 3
                for r in range(2):
                    for k in range(n):
                        step(V.max(values(k)[:, 8 * r:8 * r + 8], lists[k]))
                        between(k % every == 0)
                    wait()
                    for k in range(n):
                        step(V.max_index(where(k)[:, 8 * r:8 * r + 8], values(k)[:, 8 * r:8 * r + 8], lists[k]))
                        between(k % every == 0)
                    if r == 0:
                        wait()
                        for k in range(n):
                            step(V.match_replace(lists[k], values(k)[:, 0:8], lists[k], LOWEST))
                            between(k % every == 0)
                        wait()

            def routing(layer, between):
                for tb in range(TB):
                    top16([SC[:, tb * 2048 + j * P:tb * 2048 + (j + 1) * P] for j in range(16)],
                          lambda k: TV[:, tb, k, :], lambda k: TI[:, tb, k, :], between)
                wait()
                step(V.tensor_copy(TIf, TI))
                wait()
                v = lambda tb: TV[:, tb].rearrange("p (h c) k -> p h c k", c=2)
                c = shaped(SC[:, 0:2048], H8, TOPK, TOPK)
                for tb in range(TB):
                    tt(c, v(tb)[:, :, 0, :, None].to_broadcast([P, H8, TOPK, TOPK]),
                       v(tb)[:, :, 1, None, :].to_broadcast([P, H8, TOPK, TOPK]), ALU.add)
                    between()
                    wait()
                    top16([c[:, h].rearrange("p a b -> p (a b)") for h in range(H8)],
                          lambda k: FV[:, tb, k, :], lambda k: FI[:, tb, k, :], between)
                    wait()
                top = col[:, 2, 0:16]
                fv = FV.rearrange("p t h k -> p (t h) k")
                step(V.tensor_copy(top, fv[:, :, 0]))
                fi = FI.rearrange("p t h k -> p (t h k)")
                step(V.tensor_scalar(halves[0], fi, 4, None, ALU.logical_shift_right))
                step(V.tensor_scalar(halves[1], fi, 15, None, ALU.bitwise_and))
                wait()
                tt(fv, fv, top[:, :, None].to_broadcast([P, 16, TOPK]), ALU.subtract)
                for k in range(2):
                    step(V.tensor_copy(HL[:, k].rearrange("p t h k -> p (t h k)"), halves[k]))
                wait()
                dve.sem_inc(softmax_wanted, 1)
                for tb in range(TB):
                    for k in range(2):
                        lists = TIf[:, tb].rearrange("p (h c) k -> p h c k", c=2)
                        between()
                        tt(c, HL[:, k, tb, :, :, None].to_broadcast([P, H8, TOPK, TOPK]),
                           iota[:, None, None, 0:TOPK].to_broadcast([P, H8, TOPK, TOPK]), ALU.is_equal)
                        between()
                        wait()
                        tt(c, c, lists[:, :, k, None, :].to_broadcast([P, H8, TOPK, TOPK]), ALU.mult)
                        between()
                        wait()
                        step(V.tensor_reduce(route_index[k][:, tb].rearrange("p h k -> p (h k)"),
                                             c.rearrange("p h a b -> p (h a) b"), AX, ALU.add))
                        wait()

            def gates_from_exps(layer):
                fv = FV.rearrange("p t h k -> p (t h) k")
                dve.wait_ge(softmax_exps, layer + 1)
                step(V.tensor_reduce(col[:, 2, 0:16], fv, AX, ALU.add))
                wait()
                step(V.reciprocal(col[:, 3, 0:16], col[:, 2, 0:16]))
                wait()
                tt(fv, fv, col[:, 3, 0:16, None].to_broadcast([P, 16, TOPK]), ALU.mult)
                wait()
                dve.sem_inc(routes_ready, 1)

            def peer(layer):
                take_low(dve, f"wq{layer}", 0)
                turned_parts(f"ln{layer}_0")
                lows(f"wq{layer}", 1, 16)
                lows(f"u{layer}", 0, 2)
                moved(dve, SLOT[f"scores{layer}"], 8)
                done = [2]

                def between(now=True):
                    if now and done[0] < EXPERT_TILES - BODY:
                        take_low(dve, f"u{layer}", done[0])
                        done[0] += 1

                routing(layer, between)
                while done[0] % BODY:
                    between()
                with dve.Fori(done[0] // BODY, EXPERT_TILES // BODY, 1) as turns:
                    for j in range(BODY):
                        take_low(dve, f"u{layer}", j, turns)
                gates_from_exps(layer)
                for q in range(2):
                    s = SLOT[f"routes{layer}"] + q
                    slot_here(dve, s)
                    step(V.tensor_copy(route_T[:, 2 * q, :], bank(s)[:, 0:T]))
                    if q == 0:
                        ts(route_T[:, 1, :], bank(s)[:, T:2 * T], -1.0, None, ALU.mult)
                    wait()
                    dve.sem_inc(slot_moved[s % 4], 1)
                dve.sem_inc(routes_turned, 1)
                moved(dve, SLOT[f"u{layer}"], EXPERT_TILES)
                base = SLOT[f"gates{layer}"]

                def gate_group(k, turns=0):
                    for t in range(4):
                        at = turns * 16 + (4 * k + t)
                        ins = V.tensor_scalar(gated_rows[:, k % 4, t], iota[:], route_T[:, 0, ds(at, 1)],
                                              route_T[:, 2, ds(at, 1)], ALU.is_equal, ALU.mult)
                    ins.then_inc(gate_rows, 1)

                def apply_gates(k, turns=0):
                    slot_here(dve, base + k, turns)
                    h = expert_tokens[:, ds(turns * 16 + 4 * k, 4), :]
                    free(V.tensor_tensor(h, h, bank(base + k).rearrange("p (t e) -> p t e", t=4), ALU.mult),
                         base + k)

                for k in range(4):
                    gate_group(k)
                    if k >= 2:
                        apply_gates(k - 2)
                with dve.Fori(1, T // 16, 1) as turns:
                    for k in range(4):
                        gate_group(k, turns)
                        apply_gates(k - 2, turns)
                for k in range(T // 4 - 2, T // 4):
                    apply_gates(k)
                moved(dve, base, T // 4)

                def stage(j, turns=0):
                    dve.wait_ge(staged_hi, turns * BODY + (EXPERT_TILES * layer + j + 1))
                    V.tensor_tensor(x_lo[:, j % BODY, :], expert_rows(j, turns), x_hi[:, j % BODY, :],
                                    ALU.subtract).then_inc(staged, 1)

                stage(0)
                with dve.Fori(0, EXPERT_TILES // BODY - 1, 1) as turns:
                    for j in range(BODY):
                        take_low(dve, f"v{layer}", j, turns)
                        stage(j + 1, turns)
                for j in range(EXPERT_TILES - BODY, EXPERT_TILES):
                    take_low(dve, f"v{layer}", j)
                    if j + 1 < EXPERT_TILES:
                        stage(j + 1)
                layer_norm(f"v{layer}")
                take_low(dve, f"ple_gate{layer}", 0)
                turned_parts(f"ln{layer}_1")
                lows(f"ple_gate{layer}", 1, 8, following=AFTER_PEER[layer])
                acc_gone(dve, f"ple_gate{layer}")
                for tb in range(TB):
                    tt(ple_sig[:, tb, :], ple_sig[:, tb, :], ple_side[:, tb, :], ALU.mult)
                wait()
                for tb in range(TB):
                    tt(X[:, tb, :], X[:, tb, :], ple_sig[:, tb, :], ALU.add)
                wait()
                dve.sem_inc(turn_ready, 1)

            peer(0)
            dve.wait_ge(rope_in, 48)
            step(V.tensor_copy(pos_f, pos_i))
            wait()
            for tb in range(TB):
                ts(angle[:, 0, tb, :], inv_freq, pos_f[:, tb:tb + 1], None, ALU.mult)
            wait()
            ts(turns_[:, 0], angle[:, 0], 1.0 / (2 * np.pi), ROUND, ALU.mult, ALU.add)
            ts(turns_[:, 1], angle[:, 0], 1.0 / (2 * np.pi), 0.25, ALU.mult, ALU.add)
            wait()
            ts(turns_[:, 1], turns_[:, 1], ROUND, None, ALU.add)
            wait()
            ts(turns_[:], turns_[:], ROUND, None, ALU.subtract)
            wait()
            stt(angle[:, 1], turns_[:, 1], -TWO_PI_A, angle[:, 0], ALU.mult, ALU.add)
            wait()
            stt(angle[:, 0], turns_[:, 0], -TWO_PI_A, angle[:, 0], ALU.mult, ALU.add)
            wait()
            flat = lambda v: v.rearrange("p a b c -> p (a b c)")
            stt(flat(angle), flat(turns_), -TWO_PI_B, flat(angle), ALU.mult, ALU.add)
            wait()
            ts(angle[:, 1], angle[:, 1], float(np.pi / 2), None, ALU.add)
            wait()
            ts(flat(angle), flat(angle), -PI_BELOW, PI_BELOW, ALU.max, ALU.min)
            wait()
            dve.sem_inc(angles_ready, 1)
            turned_parts("x1")
            lows("kv_q_down", 1, 8)
            counts["sums"] += 1
            dve.wait_ge(sums_ready, counts["sums"])
            for k, width in ((0, KV_RANK), (1, Q_RANK)):
                ts(col[:, 0, k:4:2], col[:, 2, k:4:2], 1.0 / width, NORM_EPS, ALU.mult, ALU.add)
            inverse_roots(4)
            for tb in range(TB):
                ts(latent[:, tb, 0:KV_RANK], latent[:, tb, 0:KV_RANK], col[:, 1, 2 * tb:2 * tb + 1], None, ALU.mult)
                ts(latent[:, tb, 320:LATENTS], latent[:, tb, 320:LATENTS], col[:, 1, 2 * tb + 1:2 * tb + 2], None, ALU.mult)
            dve.wait_ge(sines_ready, 1)

            def rotate(o1, o2, x1, x2, cos, sin, tmp, pause=lambda n: None):
                wait()
                tt(o1, x1, cos, ALU.mult)
                tt(tmp, x2, sin, ALU.mult)
                tt(o2, x1, sin, ALU.mult)
                pause(0)
                wait()
                tt(o1, o1, tmp, ALU.subtract)
                pause(1)
                wait()
                tt(tmp, x2, cos, ALU.mult)
                pause(2)
                wait()
                tt(o2, o2, tmp, ALU.add)

            for tb in range(TB):
                x1, x2 = latent[:, tb, 256:288], latent[:, tb, 288:320]
                rotate(rope_k2[:, tb, 0, 0], rope_k2[:, tb, 0, 1], x1, x2, sincos[:, 1, tb], sincos[:, 0, tb],
                       rope_tmp[:, 0, 0:32])
            wait()
            step(V.tensor_copy(rope_k2[:, :, 1], rope_k2[:, :, 0]))
            wait()
            dve.sem_inc(latents_ready, 1)
            acc_gone(dve, "uq_rope")
            for tb in range(TB):
                bc = lambda v: v[:, None, :].to_broadcast([P, H8, 32])
                rotate(q_rot[:, tb, :, 0, :], q_rot[:, tb, :, 1, :], q_rope[:, tb, 0], q_rope[:, tb, 1],
                       bc(sincos[:, 1, tb]), bc(sincos[:, 0, tb]),
                       rope_tmp[:, 0, :].rearrange("p (h c) -> p h c", h=H8))
            wait()
            dve.sem_inc(rope_ready, 1)

            def maxima(h, src, parts, scale):
                for tb, (lo, hi) in enumerate(parts):
                    step(V.tensor_reduce(col[:, 2 + h % 2, 10 + tb:11 + tb], src[:, lo:hi], AX, ALU.max))
                wait()
                ts(col[:, 2 + h % 2, 8:10], col[:, 2 + h % 2, 10:12], -scale, None, ALU.mult)
                wait()
                dve.sem_inc(maxima_ready, 1)

            def normalise(n, h, p, parts):
                dve.wait_ge(exps_ready, n + h + 1)
                step(V.reciprocal(col[:, 4 + h % 2, 2:4], col[:, 4 + h % 2, 0:2]))
                wait()
                for tb, (lo, hi) in enumerate(parts):
                    ts(p[:, h % 2, lo:hi], p[:, h % 2, lo:hi], col[:, 4 + h % 2, 2 + tb:3 + tb], None, ALU.mult)
                wait()
                dve.sem_inc(probs_ready, 1)

            def mla_max(h):
                s = SLOT[("mla", "scores", h)]
                slot_here(dve, s)
                if h >= 2:
                    slot_here(dve, SLOT[("mla", "probs", h - 2)])
                maxima(h, bank(s), parts, MLA_SCALE)

            parts = ((0, P), (P, P + T))
            mla_max(0)
            for h in range(H8):
                if h + 1 < H8:
                    mla_max(h + 1)
                normalise(0, h, mla_p, parts)
                dve.sem_inc(slot_moved[SLOT[("mla", "scores", h)] % 4], 1)
                s = SLOT[("mla", "out", h)]
                slot_here(dve, s)
                free(V.tensor_copy(mla_oT[:, h, :], bank(s)[:, 0:T]), s)
            layer_norm("b_out")
            peer(1)

            def ffn(n):
                base, looped = SLOT[f"ffn{n}"], 2 * FF_TILES // BODY

                def product(j, turns=0):
                    s = base + 2 * j + 1
                    slot_here(dve, s, turns * 2)
                    dve.wait_ge(slot_moved[(s - 1) % 4], turns * 2 + ((s - 1) // 4 + 1))
                    at = slice(j, j + 1) if isinstance(turns, int) else ds(turns * 4 + j, 1)
                    inner = act_f[:, None, :]
                    k = turns * 8 + 2 * (FF_TILES * (n - 1) + j)
                    V.tensor_tensor(inner, silu_g[:, j % 4:j % 4 + 1, :], bank(s)[:, None, 0:T], ALU.mult
                                    ).then_inc(inner_step, 1)
                    dve.wait_ge(inner_step, k + 1)
                    V.tensor_copy(act_hi[:, at, :], inner).then_inc(inner_step, 1)
                    dve.wait_ge(inner_step, k + 2)
                    free(V.tensor_tensor(act_lo[:, at, :], inner, act_hi[:, at, :], ALU.subtract), s)
                    dve.wait_ge(slot_moved[s % 4], turns * 2 + (s // 4 + 1))

                def pair(j, turns=0):
                    take_low(dve, f"ffn{n}_in", 2 * j + 1, turns)
                    take_low(dve, f"ffn{n}_in", 2 * j + 2, turns)
                    product(j, turns)

                with dve.Fori(0, looped, 1) as turns:
                    for j in range(4):
                        pair(j, turns)
                for j in range(4 * looped, FF_TILES):
                    pair(j)
                lows(f"ffn{n}_out", 1, FF_TILES, following="rqk" if n == 1 else None)

            pre_norm()
            turned_parts("rms1", GAIN_FFN1)
            ffn(1)
            post_norm("ffn1_out", 0.5)
            pre_norm()
            turned_parts("rms2", GAIN_MIX)
            lows("rqk", 1, 5)
            dve.wait_ge(mix_in, 16 * 6)
            dve.wait_ge(logits_ready, 1)
            ts(ret_lg[:, 2, :], ret_logit, 0.0, None, ALU.min)
            dve.wait_ge(na_bias_in, 64)
            for tb in range(TB):
                v = na_bias[:, tb].rearrange("p h r c -> p (h r) c")
                tt(v, v, na_colmask[:, None, :].to_broadcast([P, 32, 64]), ALU.add)
                lows("rqk", 5 + 2 * tb, min(7 + 2 * tb, 8))
            wait()
            tt(ret_lg[:, 3, :], ret_lg[:, 2, :], ret_lg[:, 1, :], ALU.subtract)
            lows("rv", 0, 2)
            acc_gone(dve, "rqk")
            for tb in range(TB):
                bc = lambda v: v[:, None, :].to_broadcast([P, 2 * RET_H, 64])
                rotate(rqk_rot[:, tb, :, 0, :], rqk_rot[:, tb, :, 1, :], rqk[:, tb, :, 0, :], rqk[:, tb, :, 1, :],
                       bc(ret_cos[:, tb]), bc(ret_sin[:, tb]),
                       rot_tmp[:, 0, :].rearrange("p (h c) -> p h c", c=64),
                       pause=lambda n: take_low(dve, "rv", 2 + 3 * tb + n))
            wait()
            dve.sem_inc(turn_ready, 1)
            lows("rg", 0, 8)
            lows("nqk", 0, 8)
            lows("nv", 0, 4)
            lows("g_ret", 0, 8)
            lows("g_na", 0, 8, following="ret_out")
            turned("rqk", rqkT)

            def ret_exponent(h):
                tt_ = ret_d[:, h % 2, :]
                ts(tt_, ret_down, ret_lg[:, 3, RET_H + h:RET_H + h + 1], None, ALU.mult)
                wait()
                stt(tt_, ret_up, ret_lg[:, 3, h:h + 1], tt_, ALU.mult, ALU.add)
                wait()
                dve.sem_inc(decay_wanted, 1)

            wait()
            ret_exponent(0)
            for h in range(RET_H):
                if h + 1 < RET_H:
                    ret_exponent(h + 1)
                s = SLOT[("ret", "scores", h)]
                slot_here(dve, s)
                dve.wait_ge(decay_ready, h + 1)
                if h >= 2:
                    slot_here(dve, SLOT[("ret", "out", h - 2)])
                step(V.scalar_tensor_tensor(out=ret_p[:, h % 2, :], in0=bank(s), scalar=RET_SCALE,
                                            in1=ret_d[:, h % 2, :], op0=ALU.mult, op1=ALU.mult))
                wait()
                dve.sem_inc(slot_moved[s % 4], 1)
            mean_square_roots(2 * RET_H, T, RMS_EPS, src=3)
            acc_gone(dve, "rg")
            for tb in range(TB):
                for h in range(RET_H):
                    k = RET_H * tb + h
                    stt(ret_y[:, tb, h, :], ret_y[:, tb, h, :], col[:, 1, k:k + 1],
                        ret_g[:, tb, h * T:(h + 1) * T], ALU.mult, ALU.mult)
            wait()
            dve.sem_inc(turn_ready, 1)
            nparts = ((0, T), (T, 2 * T))

            def na_max(h):
                s = SLOT[("na", "scores", h)]
                slot_here(dve, s)
                if h >= 2:
                    slot_here(dve, SLOT[("na", "probs", h - 2)])
                for tb in range(TB):
                    stt(na_s[:, h % 2, tb * T:(tb + 1) * T], bank(s)[:, tb * T:(tb + 1) * T], NA_SCALE,
                        na_bias[:, tb, h].rearrange("p r c -> p (r c)"), ALU.mult, ALU.add)
                wait()
                dve.sem_inc(slot_moved[s % 4], 1)
                maxima(h, na_s[:, h % 2], nparts, 1.0)

            na_max(0)
            for h in range(H8):
                if h + 1 < H8:
                    na_max(h + 1)
                normalise(H8, h, na_s, nparts)
            turned_parts("ret")
            lows("ret_out", 1, 8)
            acc_here(dve, "ret_out")
            for tb in range(TB):
                tt(merged_tmp[:, tb, :], sig_ret[:, tb, :], acc_rows(tb), ALU.mult)
            wait()
            dve.sem_inc(acc_moved, 1)
            acc_here(dve, "na_out")
            for tb in range(TB):
                tt(merged[:, tb, :], sig_na[:, tb, :], acc_rows(tb), ALU.mult)
            wait()
            dve.sem_inc(acc_moved, 1)
            for tb in range(TB):
                tt(merged[:, tb, :], merged[:, tb, :], merged_tmp[:, tb, :], ALU.add)
            wait()
            dve.sem_inc(turn_ready, 1)
            take_low(dve, "mix_out", 0)
            turned_parts("merged")
            lows("mix_out", 1, 8, following="ffn2_in")
            post_norm("mix_out", 1.0)
            pre_norm()
            turned_parts("rms3", GAIN_FFN2)
            ffn(2)
            post_norm("ffn2_out", 0.5)
            dve.sem_inc(out_ready, 1)





def tall(w):
    n = w.shape[1] // P
    return np.ascontiguousarray(w.reshape(KC, P, n, P).transpose(2, 1, 0, 3)).reshape(n, P, D)


def wide(w):
    return np.ascontiguousarray(w.reshape(-1, P, w.shape[1]))


def by_feature(v):
    return np.ascontiguousarray(v.T.reshape(-1, P, v.shape[0]).transpose(1, 0, 2))


def by_token(v):
    return np.ascontiguousarray(np.swapaxes(v.reshape(TB, P, *v.shape[1:]), 0, 1))


def columns(v):
    return v.reshape(-1, P).T


def constants():
    f = np.float32
    q, k = np.arange(P)[None, :], np.arange(P)[:, None]
    pos = np.arange(T, dtype=f)
    ang = pos[:, None] * (f(1.0) / (f(10000.0) ** np.linspace(0.0, 1.0, 64, dtype=f)))[None, :]
    diff = (np.arange(T)[None, None, :] - (np.arange(P)[:, None, None] + P * np.arange(TB)[None, :, None]))
    c = np.arange(P) % 64
    first = np.clip(c - 8, 0, 48)[:, None]
    cc = np.arange(64)[None, :]
    sel = np.zeros((H8, H8, P), f)
    sel[np.arange(H8), np.arange(H8)] = 1.0
    return {
        "ident": np.eye(P, dtype=f),
        "iota": np.tile(np.arange(P, dtype=f), (P, 1)),
        "ml_sel": sel,
        "ml_mask": np.where(q < k, f(BIG), f(0.0)),
        "mla_mask": np.where(q > k, f(-BIG), f(0.0)),
        "inv_freq": np.tile(f(10000.0) ** (-np.arange(0, ROPE, 2, dtype=f) / f(ROPE)), (P, 1)),
        "ret_cos": by_token(np.cos(ang)), "ret_sin": by_token(np.sin(ang)),
        "ret_up": np.maximum(diff, 0).astype(f).reshape(P, TB * T),
        "ret_down": np.maximum(-diff, 0).astype(f).reshape(P, TB * T),
        "na_colmask": np.where((cc >= first) & (cc < first + 16), f(0.0), f(-BIG)),
    }


def layout(i):
    w, wmix = i["a_w_in"][0], i["w_mix_in_2"][0]
    kv_up, uq = i["kv_w_up"].reshape(KV_RANK, H8, 2 * P), i["b_w_uq"][0].reshape(Q_RANK, H8, P + ROPE)
    at = np.clip(np.arange(64)[None, :] - np.arange(64)[:, None] + 15, 0, 30)
    m = {
        "x": by_token(i["x"][0]), "xT": by_feature(i["x"][0]),
        "positions": by_token(i["positions"][0]),
        "ml_gate_w": np.ascontiguousarray(w[:, 2048:2064].reshape(KC, P, 16).transpose(1, 0, 2)),
        "ml_bias": np.ascontiguousarray(i["a_b_if"][0].T),
        "cols": np.ascontiguousarray(np.concatenate(
            [columns(v) for v in (i["a_hn_g"][0], i["kv_norm_g"], i["b_q_norm_g"][0], i["ffn1_pre_norm_2"][0],
                                  i["mix_pre_norm_2"][0], i["ffn2_pre_norm_2"][0])], axis=1)),
        "a_qk": tall(w[:, 0:1024]), "a_v": wide(w[:, 1024:2048]), "a_og": wide(w[:, 2064:3088]),
        "a_out": wide(i["a_w_out"][0]),
        "kv_q_down": wide(np.concatenate([i["kv_w_down"], i["b_w_dq"][0]], axis=1)),
        "up_k": wide(kv_up[:, :, 0:P].reshape(KV_RANK, D)), "up_v": wide(kv_up[:, :, P:].reshape(KV_RANK, D)),
        "uq_nope": wide(uq[:, :, 0:P].reshape(Q_RANK, D)), "uq_rope": wide(uq[:, :, P:].reshape(Q_RANK, 512)),
        "b_out": wide(i["b_w_out"][0]),
        "rqk": wide(wmix[:, 0:1024]), "rv": wide(wmix[:, 1024:2048]), "rg": wide(wmix[:, 2048:3072]),
        "nqk": tall(wmix[:, 3072:4096]),
        "nv": np.ascontiguousarray(wmix[:, 4096:4608].reshape(4, 2, P, 512).transpose(0, 2, 1, 3)).reshape(4, P, D),
        "g_ret": wide(wmix[:, 4608:5632]), "g_na": wide(wmix[:, 5632:6656]),
        "ret_out": wide(i["w_ret_out_2"][0]), "na_out": wide(i["w_na_out_2"][0]),
        "mix_out": wide(i["w_mix_out_2"][0]),
        "ret_logit": np.concatenate([i["ret_decay_fwd_2"], i["ret_decay_bwd_2"]], axis=1),
        "na_bias": np.ascontiguousarray(i["na_rel_bias_2"][0][:, 4:11, :][:, :, at].transpose(2, 0, 1, 3)),
    }
    for n in (1, 2):
        t = tall(i[f"ffn{n}_w_in_2"][0])
        m[f"ffn{n}_in"] = np.stack([t[:FF_TILES], t[FF_TILES:]], axis=1).reshape(2 * FF_TILES, P, D)
        m[f"ffn{n}_out"] = wide(i[f"ffn{n}_w_out_2"][0])
    for l in range(LAYERS):
        m[f"p{l}"] = by_feature(i["p"][l, 0])
        m[f"wq{l}"] = tall(i["peer_w_q"][l])
        m[f"keys{l}"] = np.ascontiguousarray(
            i["peer_sub_keys"][l].reshape(2, KC, P, P).transpose(0, 3, 1, 2)).reshape(2, P, D)
        m[f"u{l}"] = np.ascontiguousarray(
            i["peer_u"][l].reshape(EXPERT_TILES, P, KC, P).transpose(0, 3, 2, 1)).reshape(EXPERT_TILES, P, D)
        m[f"v{l}"] = i["peer_v"][l].reshape(EXPERT_TILES, P, D)
        m[f"ple_proj{l}"] = wide(i["ple_w_proj"][l])
        m[f"ple_gate{l}"] = wide(i["ple_w_gate"][l])
    rows = [(i["ln_g"][l, k], i["ln_b"][l, k]) for l in range(LAYERS) for k in range(2)]
    rows += [(i[n][0],) for n in ("ffn1_post_norm_2", "mix_post_norm_2", "ffn2_post_norm_2")]
    for k, r in enumerate(rows):
        m[f"rows{k}"] = np.stack(r)
    return m


def kernel(**inputs):
    import concourse.bacc as bacc
    from concourse.bass_utils import run_bass_kernel_spmd

    laid = {**layout({k: np.asarray(v) for k, v in inputs.items()}), **constants()}
    nc = bacc.Bacc("TRN2", target_bir_lowering=False, num_devices=1)
    aps = {n: nc.dram_tensor(f"in_{n}", v.shape, mybir.dt.from_np(v.dtype), kind="ExternalInput").ap()
           for n, v in laid.items()}
    out = nc.dram_tensor("out", (1, T, D), F32, kind="ExternalOutput").ap()
    program(nc, aps, out.rearrange("a (t p) d -> p (a t) d", p=P))
    r = run_bass_kernel_spmd(nc, [{f"in_{n}": v for n, v in laid.items()}], core_ids=[0])
    return r.results[0]["out"]
```

```python
from contextlib import ExitStack

import numpy as np

import concourse.bass as bass
from concourse import mybir

P = 128
D = 1024
T = 256
TB = T // P
KC = D // P
RING = 4
BODY = 8
F32 = mybir.dt.float32
BF16 = mybir.dt.bfloat16
F32R = mybir.dt.float32r
U32 = mybir.dt.uint32
I32 = mybir.dt.int32
ALU = mybir.AluOpType
ACT = mybir.ActivationFunctionType
AX = mybir.AxisListType.X
ds = bass.ds

LAYERS = 2
DN_ALPHA = (2.0 * LAYERS) ** 0.25
NORM_EPS = 1e-5
RMS_EPS = 1e-6
BIG = 1e30
LOWEST = -3.0e38
ROUND = 12582912.0
TWO_PI_A = 6.28125
TWO_PI_B = float(np.float32(2 * np.pi - 6.28125))
PI_BELOW = 3.1415925

H8 = 8
ML_SCALE = 64 ** -0.5
GATE_ROWS = [slice(0, H8), slice(32, 32 + H8)]
GATE_WIDTH = 32 + H8
KV_RANK, ROPE, Q_RANK = 256, 64, 384
LATENTS = KV_RANK + ROPE + Q_RANK
MLA_SCALE = (128 + 64) ** -0.5
TOPK = 16
EXPERT_TILES = 128
LOOPED_U = EXPERT_TILES - BODY
RET_H = 4
RET_SCALE = 128 ** -0.5
NA_SCALE = 64 ** -0.5
FF_TILES = 2816 // P

PEER_TILES = [("wq", 16), ("keys", 2), ("u", EXPERT_TILES), ("v", EXPERT_TILES), ("ple_proj", 2), ("ple_gate", 8)]
STREAM = (
    [("a_qk", 8), ("a_v", 8), ("a_og", 8), ("a_out", 8)]
    + [(f"{n}0", k) for n, k in PEER_TILES]
    + [("kv_q_down", 8), ("up_k", 2), ("up_v", 2), ("uq_nope", 3), ("uq_rope", 3), ("b_out", 8)]
    + [(f"{n}1", k) for n, k in PEER_TILES]
    + [("ffn1_in", 2 * FF_TILES), ("ffn1_out", FF_TILES)]
    + [("rqk", 8), ("rv", 8), ("rg", 8), ("nqk", 8), ("nv", 4), ("g_ret", 8), ("g_na", 8)]
    + [("ret_out", 8), ("na_out", 4), ("mix_out", 8)]
    + [("ffn2_in", 2 * FF_TILES), ("ffn2_out", FF_TILES)]
)

ACC_ORDER = ["a_v", "a_og", "a_out", "v0", "ple_proj0", "ple_gate0", "kv_q_down", "up_v", "uq_rope", "b_out",
             "v1", "ple_proj1", "ple_gate1", "ffn1_out", "rqk", "rv", "rg", "nv", "g_ret", "g_na",
             "ret_out", "na_out", "mix_out", "ffn2_out"]

TURN_ORDER = ["ml_out", "ln0_0", "ln0_1", "x1", "ln1_0", "ln1_1", "x2", "rms1", "rms2", "rqk", "ret", "merged", "rms3"]


def starts(items):
    out, at = {}, 0
    for name, n in items:
        out[name] = at
        at += n
    return out


def attention_order(name, first, last):
    heads = H8 if name != "ret" else RET_H
    out = [((name, s, 0), 1) for s in first]
    for h in range(heads):
        if h + 1 < heads:
            out += [((name, s, h + 1), 1) for s in first]
        out += [((name, s, h), 1) for s in last]
    return out


def spaced_order(name):
    out = [((name, "scores", 0), 1)]
    for h in range(H8):
        out += [((name, "scores", h + 1), 1)] if h + 1 < H8 else []
        out += [((name, "out", h - 1), 1)] if h else []
        out += [((name, "probs", h), 1)]
    return out + [((name, "out", H8 - 1), 1)]


def peer_slots(layer):
    return [(f"wq{layer}", 16), (f"scores{layer}", 8), (f"u{layer}", LOOPED_U), (f"routes{layer}", 2),
            (f"last_u{layer}", BODY), (f"gates{layer}", T // 4)]


def turn(name):
    return [(f"turn_{name}", 4)]


SLOT_ORDER = (
    [("gates", 1), ("a_qk", 8), ("gate_cols", 1)]
    + attention_order("ml", ["decay", "scores"], ["out"])
    + turn("ml_out") + turn("ln0_0") + peer_slots(0) + turn("ln0_1") + turn("x1")
    + [("latents", 3), ("up_k", 8), ("uq_nope", 8), ("rope", 2)]
    + attention_order("mla", ["scores"], ["probs", "out"])
    + turn("ln1_0") + peer_slots(1) + turn("ln1_1")
    + turn("rms1") + [("ffn1", 2 * FF_TILES)] + turn("rms2") + [("nqk", 8)] + turn("rqk")
    + spaced_order("na") + attention_order("ret", ["scores"], ["out"])
    + turn("ret") + turn("merged") + turn("rms3") + [("ffn2", 2 * FF_TILES)]
)
TILE = starts(STREAM)
SPLIT_STAGES = {"a_qk", "a_v", "a_og", "a_out", "b_out", "wq0", "u0", "v0", "ple_gate0", "kv_q_down", "wq1", "u1", "v1", "ple_gate1", "ffn1_in", "ffn1_out",
                "rqk", "rv", "rg", "nqk", "nv", "g_ret", "g_na", "ret_out", "mix_out", "ffn2_in", "ffn2_out"}
PART_TURNS = ["ml_out", "ln0_0", "ln0_1", "x1", "ln1_0", "ln1_1", "rms1", "rms2", "ret", "merged", "rms3"]
SPLIT = starts([(name, n if name in SPLIT_STAGES else 0) for name, n in STREAM])
TILE_NAMES = [name for name, n in STREAM for _ in range(n)]
SLOT = starts(SLOT_ORDER)
ACC = {name: n for n, name in enumerate(ACC_ORDER)}
TURN = {name: n for n, name in enumerate(TURN_ORDER)}

ROW_SETS = [2, 2, 2, 2, 1, 1, 1]


def program(nc, a, out):
    with ExitStack() as ctx:
        def sbuf(name, shape, dt=F32):
            return ctx.enter_context(nc.sbuf_tensor(name, shape, dt))

        def sem(name):
            return ctx.enter_context(nc.semaphore(name))

        ps = ctx.enter_context(nc.psum_tensor("ps", [P, 8, 512], F32))
        ring = sbuf("ring", [P, RING, D])
        big_at = nc.sbuf_base
        big = sbuf("big", [P, EXPERT_TILES * T])
        X = sbuf("X", [P, TB, D])
        w_hi = sbuf("w_hi", [P, 2, D], F32R)
        w_lo = sbuf("w_lo", [P, 2, D], F32R)
        x_hi_at = nc.sbuf_base
        x_hi = sbuf("x_hi", [P, KC, T], F32R)
        x_lo_at = nc.sbuf_base
        x_lo = sbuf("x_lo", [P, KC, T], F32R)
        SC = sbuf("SC", [P, 4096])
        tops = sbuf("tops", [P, 1024])
        ident = sbuf("ident", [P, P])
        iota = sbuf("iota", [P, P])
        zeros = sbuf("zeros", [P, 512], BF16)
        cols = sbuf("cols", [P, 37])
        col = sbuf("col", [P, 6, 16])
        stats = sbuf("stats", [P, 16, 6])
        mv = sbuf("mv", [P, 16, 2])

        def shaped(v, *shape):
            if len(shape) == 1:
                return v
            names = "abcd"[:len(shape)]
            return v.rearrange(f"p ({' '.join(names)}) -> p {' '.join(names)}",
                               **{k: s for k, s in zip(names, shape)})

        def buf(at, *shape):
            return shaped(big[:, at:at + int(np.prod(shape))], *shape)

        BK = 2048
        acc = ps[:, 0:4, :]

        def acc_rows(tb):
            return ps[:, 2 * tb:2 * tb + 2, :].rearrange("p a b -> p (a b)")

        def bank(s):
            return ps[:, 4 + s % 4, :]

        rows = SC[:, 2 * 1024:4 * 1024].rearrange("p (r n) -> p r n", r=2)
        gated_rows = shaped(SC[:, 0:2048], 4, 4, P)
        pT = shaped(SC[:, 0:512], 2, T)
        place = nc.alloc_sbuf_tensor_at("place", [P, 4, 4, P], F32, offset=x_hi_at)
        distance = nc.alloc_sbuf_tensor_at("distance", [P, 4, 4, P], F32, offset=x_lo_at)
        expert_tokens = big[:, :].rearrange("p (e t) -> p t e", t=T)
        TV = shaped(tops[:, 0:512], TB, 2 * H8, TOPK)
        TI = shaped(tops[:, 512:1024].bitcast(U32), TB, 2 * H8, TOPK)
        TIf = shaped(tops[:, 512:1024], TB, 2 * H8, TOPK)
        FI = shaped(SC[:, 2048:2304].bitcast(U32), TB, H8, TOPK)
        halves = [SC[:, 2304 + k * T:2304 + (k + 1) * T].bitcast(U32) for k in range(2)]
        HL = shaped(SC[:, 2816:3328], 2, TB, H8, TOPK)
        FV = shaped(SC[:, 3328:3584], TB, H8, TOPK)
        route_index = [shaped(tops[:, k * T:(k + 1) * T], TB, H8, TOPK) for k in range(2)]
        route_T = shaped(tops[:, 0:3 * T], 3, T)

        def expert_rows(j, turns):
            at = turns * (BODY * T) + j * T
            return big[:, at:at + T] if isinstance(turns, int) else big[:, ds(at, T)]

        tiles_hi = sem("tiles_hi")
        tiles_split = sem("tiles_split")
        staged_hi = sem("staged_hi")
        staged = sem("staged")
        x_hi_ready = sem("x_hi_ready")
        xt_split = sem("xt_split")
        mla_out_hi = sem("mla_out_hi")
        routes_turned = sem("routes_turned")
        tile_landed = [sem(f"tile_landed{i}") for i in range(RING)]
        tiles_begun = sem("tiles_begun")
        slot_full = [sem(f"slot_full{i}") for i in range(4)]
        slot_moved = [sem(f"slot_moved{i}") for i in range(4)]
        acc_full = sem("acc_full")
        acc_moved = sem("acc_moved")
        turn_ready = sem("turn_ready")
        act_step = sem("act_step")
        dve_step = sem("dve_step")
        pool_step = sem("pool_step")
        sqrt_wanted = sem("sqrt_wanted")
        sqrt_done = sem("sqrt_done")
        xt_in = sem("xt_in")
        x_in = sem("x_in")
        gate_w_in = sem("gate_w_in")
        consts_in = sem("consts_in")
        rows_in = sem("rows_in")
        rows_used = sem("rows_used")
        x_rows = sem("x_rows")
        p_in = sem("p_in")
        rope_in = sem("rope_in")
        mix_in = sem("mix_in")
        na_bias_in = sem("na_bias_in")
        zeros_set = sem("zeros_set")
        gates_split = sem("gates_split")
        gates_log = sem("gates_log")
        gates_scanned = sem("gates_scanned")
        floor_ready = sem("floor_ready")
        gate_cols_ready = sem("gate_cols_ready")
        decay_ready = sem("decay_ready")
        ones_set = sem("ones_set")
        sums_ready = sem("sums_ready")
        angles_ready = sem("angles_ready")
        sines_ready = sem("sines_ready")
        latents_here = sem("latents_here")
        latents_ready = sem("latents_ready")
        rope_ready = sem("rope_ready")
        maxima_ready = sem("maxima_ready")
        exps_ready = sem("exps_ready")
        probs_ready = sem("probs_ready")
        logits_ready = sem("logits_ready")
        routes_ready = sem("routes_ready")
        softmax_wanted = sem("softmax_wanted")
        softmax_exps = sem("softmax_exps")
        gate_rows = sem("gate_rows")
        place_rows = sem("place_rows")
        distances = sem("distances")
        inner_step = sem("inner_step")
        decay_wanted = sem("decay_wanted")
        stored = sem("stored")

        def tile_here(pe, i, turns=0):
            pe.wait_ge(tile_landed[i % RING], turns * 16 + 16 * (i // RING + 1))

        def tile(i):
            return ring[:, i % RING, :]

        def tall(i):
            return ring[:, i % RING, :].rearrange("p (k n) -> p k n", k=KC)

        def part(t, i):
            return t[:, i % 2, :]

        def part_free(eng, i, turns=0):
            if not isinstance(turns, int) or (i >= 2 and TILE_NAMES[i - 2] in SPLIT_STAGES):
                eng.wait_ge(tiles_begun, turns * BODY + i)

        def used(name):
            return slice(0, LATENTS if name == "kv_q_down" else D)

        def take_high(act, name, j, turns=0):
            i = TILE[name] + j
            tile_here(act, i, turns * (BODY // RING))
            part_free(act, i, turns)
            nc.scalar.copy(part(w_hi, i)[:, used(name)], tile(i)[:, used(name)]).then_inc(tiles_hi, 1)

        def take_low(dve, name, j, turns=0):
            i = TILE[name] + j
            dve.wait_ge(tiles_hi, turns * BODY + SPLIT[name] + j + 1)
            at = used(name)
            nc.vector.tensor_tensor(part(w_lo, i)[:, at], tile(i)[:, at], part(w_hi, i)[:, at], ALU.subtract
                                    ).then_inc(tiles_split, 1)

        def slot_free(pe, s, turns=0):
            if s >= 4:
                pe.wait_ge(slot_moved[s % 4], turns + s // 4)

        def slot_here(eng, s, turns=0):
            eng.wait_ge(slot_full[s % 4], turns + s // 4 + 1)

        def moved(eng, s, n=1):
            for k in range(max(s, s + n - 4), s + n):
                eng.wait_ge(slot_moved[k % 4], k // 4 + 1)

        def full(ins, s):
            return ins.then_inc(slot_full[s % 4], 1)

        def free(ins, s):
            return ins.then_inc(slot_moved[s % 4], 1)

        def acc_here(eng, name, tb=TB - 1):
            eng.wait_ge(acc_full, TB * ACC[name] + tb + 1)

        def acc_gone(eng, name):
            eng.wait_ge(acc_moved, TB * ACC[name] + TB)

        def acc_free(pe, name, tb):
            if ACC[name]:
                pe.wait_ge(acc_moved, TB * (ACC[name] - 1) + tb + 1)

        def head_rows(h):
            return slice(64 * (h % 2), 64 * (h % 2) + 64)

        class Steps:

            def __init__(self, eng, s):
                self.eng, self.sem, self.n = eng, s, 0

            def __call__(self, ins):
                ins.then_inc(self.sem, 1)
                self.n += 1

            def wait(self):
                self.eng.wait_ge(self.sem, self.n)

        AFTER_PEER = ["kv_q_down", "ffn1_in"]

        XT = buf(11 * BK, KC, T)
        ml_qk = buf(0, KC, T)
        ml_v = buf(BK, TB, H8, 129)
        ml_sig = buf(3 * BK, TB, D)
        ml_raw = buf(4 * BK, TB, H8, 129)
        ml_hn = buf(6 * BK, TB, D)
        ml_w = buf(8 * BK, 2, 384)
        ml_p = buf(8 * BK + 768, 2, 384)
        ml_rows = buf(9 * BK, 14, T)
        ml_sel = buf(15 * BK, H8, P)
        ml_gate_w = buf(12 * BK, KC, GATE_WIDTH)
        ml_bias = buf(12 * BK + 512, 1)
        ml_mask = buf(12 * BK + 640, P)
        gate_cols = buf(13 * BK, 4, H8)
        ple_sig = buf(3 * BK, TB, D)
        ple_side = buf(4 * BK, TB, D)
        peer_q = big[:, 112 * T:128 * T].rearrange("p (j t) -> p j t", t=T)
        latent = buf(0, TB, LATENTS)
        latT = buf(BK, 6, T)
        k_nope = buf(2 * BK, H8, T)
        mla_v = buf(3 * BK, TB, D)
        q_nope = buf(4 * BK, H8, T)
        q_rope = buf(5 * BK, TB, 2, H8, 32)
        q_rot = buf(5 * BK + 1024, TB, H8, 2, 32)
        q_ropeT = buf(6 * BK, 4, T)
        rope_k2 = buf(6 * BK + 1024, TB, 2, 2, 32)
        rope_tmp = buf(6 * BK + 1280, 2, 256)
        mla_p = buf(8 * BK, 2, 384)
        mla_pT = buf(8 * BK + 768, 2, 384)
        angle = buf(9 * BK, 2, TB, 32)
        turns_ = buf(9 * BK + 128, 2, TB, 32)
        sincos = buf(9 * BK + 256, 2, TB, 32)
        inv_freq = buf(9 * BK + 384, 32)
        pos_i = big[:, 9 * BK + 416:9 * BK + 418].bitcast(I32)
        pos_f = buf(9 * BK + 420, TB)
        mla_mask = buf(9 * BK + 512, P)
        sq_junk = buf(10 * BK, D)
        act_hi = nc.alloc_sbuf_tensor_at("act_hi", [P, FF_TILES, T], F32R, offset=big_at)
        act_lo = nc.alloc_sbuf_tensor_at("act_lo", [P, FF_TILES, T], F32R, offset=big_at + 9 * BK * 4)
        act_f = buf(3 * BK + 1024, T)
        silu_g = buf(3 * BK, 4, T)
        xn = buf(4 * BK, TB, D)
        na_bias = buf(5 * BK, TB, H8, 4, 64)
        post_tmp = buf(7 * BK, TB, D)
        rqk = buf(0, TB, 2 * RET_H, 2, 64)
        rqk_rot = buf(BK, TB, 2 * RET_H, 2, 64)
        rqkT = buf(2 * BK, 2 * RET_H, T)
        ret_v = buf(3 * BK, TB, D)
        ret_g = buf(4 * BK, TB, D)
        na_qk = buf(7 * BK, KC, T)
        na_v = buf(8 * BK, TB, 512)
        ret_cos = buf(8 * BK + 1024, TB, 64)
        ret_sin = buf(8 * BK + 1152, TB, 64)
        na_colmask = buf(8 * BK + 1280, 64)
        ret_logit = buf(8 * BK + 1344, 2 * RET_H)
        ret_lg = buf(8 * BK + 1352, 4, 2 * RET_H)
        sig_ret = buf(9 * BK, TB, D)
        sig_na = buf(10 * BK, TB, D)
        ret_y = buf(11 * BK, TB, RET_H, 256)
        ret_d = buf(12 * BK, 2, 512)
        ret_p = buf(12 * BK + 1024, 2, 512)
        na_s = buf(13 * BK, 2, 512)
        na_pT = buf(13 * BK + 1024, 2, 512)
        na_oT = buf(14 * BK, 4, T)
        ret_up = buf(14 * BK + 1024, 512)
        ret_down = buf(15 * BK, 512)
        rot_tmp = buf(15 * BK + 512, 2, 512)
        ret_junk = buf(13 * BK, 256)
        merged = buf(0, TB, D)
        merged_tmp = buf(BK, TB, D)
        GAIN_ML, GAIN_KV, GAIN_Q, GAIN_FFN1, GAIN_MIX, GAIN_FFN2 = 0, 8, 10, 13, 21, 29

        CONSTS = [(ident[:], "ident"), (iota[:], "iota"), (ml_sel[0:H8], "ml_sel"), (ml_mask, "ml_mask"),
                  (cols[:], "cols")]
        CONST_LOADS = len(CONSTS)

        block = ctx.enter_context(nc.Block())

        @block.sync
        def _(sp):
            def load(name, w, j):
                i = TILE[name] + j
                if i >= RING:
                    before = TILE_NAMES[i - RING]
                    if before in SPLIT_STAGES:
                        sp.wait_ge(tiles_split, SPLIT[before] + i - RING - TILE[before] + 1)
                    else:
                        sp.wait_ge(tiles_begun, i - RING + 2)
                sp.dma_start(tile(i)[:, 0:w.shape[2]], w[j]).then_inc(tile_landed[i % RING], 16)

            def stream(name, w):
                n, j = w.shape[0], 0
                if n >= 3 * BODY:
                    for j in range(BODY):
                        load(name, w, j)
                    with sp.Fori(1, n // BODY, 1) as turns:
                        for j in range(BODY):
                            i = TILE[name] + j
                            sp.wait_ge(tiles_split, turns * BODY + (SPLIT[name] + j - RING + 1))
                            sp.dma_start(tile(i), w[ds(turns * BODY + j, 1), :, :].rearrange("a p n -> p (a n)")
                                         ).then_inc(tile_landed[i % RING], 16)
                    j = n - n % BODY
                for j in range(j, n):
                    load(name, w, j)

            for name, _ in STREAM:
                stream(name, a[name])
            for tb in range(TB):
                sp.wait_ge(x_rows, 2 * TB + tb + 1)
                sp.dma_start(out[:, tb, :], X[:, tb, :]).then_inc(stored, 16)
            sp.wait_ge(stored, 16 * TB)

        @block.gpsimd
        def _(pool):
            step = Steps(pool, pool_step)
            nc.gpsimd.memset(zeros[:], 0.0).then_inc(zeros_set, 1)
            nc.gpsimd.memset(ml_v[:, :, :, 128:129], 1.0).then_inc(ones_set, 1)

            def load_rows(k, wait=None):
                if k:
                    pool.wait_ge(rows_used, k)
                if wait:
                    pool.wait_ge(*wait)
                for r in range(ROW_SETS[k]):
                    pool.dma_start(rows[:, r, :], a[f"rows{k}"][r:r + 1, :].to_broadcast([P, D])).then_inc(rows_in, 16)

            def load_p(layer):
                moved(pool, SLOT[f"gates{layer}"], T // 4)
                pool.dma_start(pT, a[f"p{layer}"]).then_inc(p_in, 16)

            load_rows(0, (gates_split, 1))
            load_rows(1, (routes_turned, 1))
            load_p(0)
            load_rows(2)
            load_rows(3, (routes_turned, 2))
            load_p(1)
            load_rows(4)
            pool.wait_ge(turn_ready, 2 * TURN["rms1"] + 2)
            for tb in range(TB):
                for r in range(2):
                    first = 3 - (2 * tb + r)
                    pool.dma_start(na_bias[64 * r:64 * r + 64, tb], a["na_bias"][:, :, first:first + 4, :]
                                   ).then_inc(na_bias_in, 16)
            for dst, name in ((ret_cos, "ret_cos"), (ret_sin, "ret_sin"), (na_colmask, "na_colmask"),
                              (ret_logit, "ret_logit"), (ret_up, "ret_up"), (ret_down, "ret_down")):
                src = a[name] if name != "ret_logit" else a[name].to_broadcast([P, 2 * RET_H])
                pool.dma_start(dst, src).then_inc(mix_in, 16)
            load_rows(5)
            load_rows(6)

        @block.tensor
        def _(pe):
            def begins_tile(mm):
                mm.then_inc(tiles_begun, 1)

            def to_acc(name, lhs, n, width=D):
                halves = [(f, min(512, width - 512 * f)) for f in range((width + 511) // 512)]
                for k in range(n):
                    i = TILE[name] + k
                    tile_here(pe, i)
                    for tb in range(TB):
                        if k == 0:
                            acc_free(pe, name, tb)
                        for f, cnt in halves:
                            mm = nc.tensor.matmul(acc[:, 2 * tb + f, 0:cnt], lhs(k, tb),
                                                  tile(i)[:, 512 * f:512 * f + cnt],
                                                  start=(k == 0), stop=(k == n - 1))
                            if tb == f == 0:
                                begins_tile(mm)
                mm.then_inc(acc_full, TB)

            def hi_here(name, j, turns=0):
                pe.wait_ge(tiles_hi, turns * BODY + (SPLIT[name] + j + 1))

            def lo_here(name, j, turns=0):
                pe.wait_ge(tiles_split, turns * BODY + (SPLIT[name] + j + 1))

            def split_tall(name, j, s, turns=0):
                i = TILE[name] + j
                hi_here(name, j, turns)
                slot_free(pe, s, turns * 2)
                hi, lo = (part(t, i).rearrange("p (k n) -> p k n", k=KC) for t in (w_hi, w_lo))
                for k in range(KC):
                    mm = nc.tensor.matmul(bank(s)[:, 0:T], hi[:, k, :], x_hi[:, k, :], start=(k == 0), stop=False)
                    if k == 0:
                        begins_tile(mm)
                    nc.tensor.matmul(bank(s)[:, 0:T], hi[:, k, :], x_lo[:, k, :], start=False, stop=False)
                lo_here(name, j, turns)
                for k in range(KC):
                    mm = nc.tensor.matmul(bank(s)[:, 0:T], lo[:, k, :], x_hi[:, k, :],
                                          start=False, stop=(k == KC - 1))
                full(mm, s)

            def split_wide(name, j, xs, k, first, last, turns=0, width=D, per_tile=1):
                halves = [(f, min(512, width - 512 * f)) for f in range((width + 511) // 512)]
                i = TILE[name] + j
                hi_here(name, j, turns)
                for tbs in ((0,), (1,)) if first or last else ((0, 1),):
                    if first:
                        acc_free(pe, name, tbs[0])
                    for n, (x, w) in enumerate(((xs[0], w_hi), (xs[1], w_hi), (xs[0], w_lo))):
                        if w is w_lo:
                            lo_here(name, j, turns)
                        for c in range(per_tile):
                            for tb in tbs:
                                for f, cnt in halves:
                                    at = c * width + 512 * f
                                    mm = nc.tensor.matmul(acc[:, 2 * tb + f, 0:cnt],
                                                          x[:, k + c, tb * P:(tb + 1) * P],
                                                          part(w, i)[:, at:at + cnt],
                                                          start=(first and n == 0 and c == 0),
                                                          stop=(last and n == 2 and c == per_tile - 1))
                                    if n == c == tb == f == 0:
                                        begins_tile(mm)
                    if last:
                        mm.then_inc(acc_full, 1)

            def split_to_acc(name, width=D, per_tile=1):
                for k in range(0, KC, per_tile):
                    split_wide(name, k // per_tile, (x_hi, x_lo), k, k == 0, k == KC - per_tile,
                               width=width, per_tile=per_tile)

            def turn_over(name, src, width=P):
                for q in range(4):
                    if q % 2 == 0:
                        pe.wait_ge(turn_ready, 2 * TURN[name] + q // 2 + 1)
                    s = SLOT[f"turn_{name}"] + q
                    slot_free(pe, s)
                    for c in range(2):
                        for tb in range(TB):
                            at = (2 * q + c) * P
                            mm = nc.tensor.transpose(bank(s)[:, (2 * c + tb) * P:(2 * c + tb + 1) * P],
                                                     src[:, tb, at:at + P], ident[:])
                    full(mm, s)

            def tokens(src):
                return lambda k, tb: src[:, k, tb * P:(tb + 1) * P]

            pe.wait_ge(xt_in, 16)
            pe.wait_ge(gate_w_in, 48)
            pe.wait_ge(zeros_set, 1)
            s = SLOT["gates"]
            for k in range(KC):
                mm = nc.tensor.matmul(bank(s)[0:GATE_WIDTH, 0:T], ml_gate_w[:, k, :], XT[:, k, :],
                                      start=(k == 0), stop=(k == KC - 1))
            full(mm, s)
            for j in range(8):
                if j == 0:
                    pe.wait_ge(xt_split, 1)
                split_tall("a_qk", j, SLOT["a_qk"] + j)
            split_to_acc("a_v")
            pe.wait_ge(consts_in, 16 * CONST_LOADS)
            pe.wait_ge(gates_scanned, 1)
            pe.wait_ge(floor_ready, 1)
            s = SLOT["gate_cols"]
            slot_free(pe, s)
            for c, row in ((0, 6), (2, 9)):
                for tb in range(TB):
                    mm = nc.tensor.matmul(bank(s)[:, (c + tb) * H8:(c + tb + 1) * H8],
                                          ml_rows[0:H8, row, tb * P:(tb + 1) * P], ident[0:H8, 0:H8],
                                          start=True, stop=True)
            full(mm, s)

            def ml_first(h):
                s = SLOT[("ml", "decay", h)]
                slot_free(pe, s)
                nc.tensor.matmul(bank(s)[:, 0:T], ml_sel[0:H8, h, :], ml_rows[0:H8, 7, :], start=True, stop=False)
                nc.tensor.matmul(bank(s)[:, 0:P], ident[:], ml_mask[:], start=False, stop=True)
                nc.tensor.matmul(bank(s)[:, T:T + P], ml_sel[0:H8, h, :], ml_rows[0:H8, 7, P:T],
                                 start=True, stop=False)
                full(nc.tensor.matmul(bank(s)[:, T:T + P], ident[:], ml_mask[:], start=False, stop=True), s)
                s = SLOT[("ml", "scores", h)]
                slot_free(pe, s)
                r, q, k = head_rows(h), h // 2, 4 + h // 2
                nc.tensor.matmul(bank(s)[:, 0:T], ml_qk[r, k, 0:P], ml_qk[r, q, :], start=True, stop=True)
                full(nc.tensor.matmul(bank(s)[:, T:T + P], ml_qk[r, k, P:T], ml_qk[r, q, P:T],
                                      start=True, stop=True), s)

            moved(pe, SLOT["a_qk"], 8)
            acc_gone(pe, "a_v")
            pe.wait_ge(ones_set, 1)
            ml_first(0)
            for h in range(H8):
                split_wide("a_og", h, (x_hi, x_lo), h, h == 0, h == H8 - 1)
                if h + 1 < H8:
                    ml_first(h + 1)
                moved(pe, SLOT[("ml", "scores", h)])
                s = SLOT[("ml", "out", h)]
                slot_free(pe, s)
                w = ml_p[:, h % 2]
                nc.tensor.matmul(bank(s)[:, 0:129], w[:, 0:P], ml_v[:, 0, h, :], start=True, stop=True)
                nc.tensor.matmul(bank(s)[:, T:T + 129], w[:, P:T], ml_v[:, 0, h, :], start=True, stop=False)
                full(nc.tensor.matmul(bank(s)[:, T:T + 129], w[:, T:T + P], ml_v[:, 1, h, :],
                                      start=False, stop=True), s)
            turn_over("ml_out", ml_hn)
            moved(pe, SLOT["turn_ml_out"], 4)
            split_to_acc("a_out")

            def peer(layer):
                turn_over(f"ln{layer}_0", X)
                moved(pe, SLOT[f"turn_ln{layer}_0"], 4)
                for j in range(16):
                    split_tall(f"wq{layer}", j, SLOT[f"wq{layer}"] + j)
                moved(pe, SLOT[f"wq{layer}"], 16)
                for half in range(2):
                    i = TILE[f"keys{layer}"] + half
                    tile_here(pe, i)
                    for tb in range(TB):
                        for g in range(2):
                            s = SLOT[f"scores{layer}"] + 4 * half + 2 * tb + g
                            slot_free(pe, s)
                            for j in range(4):
                                mm = nc.tensor.matmul(bank(s)[:, j * P:(j + 1) * P],
                                                      peer_q[:, 8 * half + 4 * g + j, tb * P:(tb + 1) * P],
                                                      tall(i)[:, 4 * g + j, :], start=True, stop=True)
                                if tb == 0 and g == 0 and j == 0:
                                    begins_tile(mm)
                            full(mm, s)
                with pe.Fori(0, LOOPED_U // BODY, 1) as turns:
                    for j in range(BODY):
                        split_tall(f"u{layer}", j, SLOT[f"u{layer}"] + j, turns)
                pe.wait_ge(routes_ready, layer + 1)
                for q in range(2):
                    s = SLOT[f"routes{layer}"] + q
                    slot_free(pe, s)
                    for k, src in enumerate(((route_index[0], route_index[1]), (FV,))[q]):
                        for tb in range(TB):
                            mm = nc.tensor.transpose(bank(s)[:, (2 * k + tb) * P:(2 * k + tb + 1) * P],
                                                     src[:, tb].rearrange("p h k -> p (h k)"), ident[:])
                    full(mm, s)
                for j in range(BODY):
                    split_tall(f"u{layer}", LOOPED_U + j, SLOT[f"last_u{layer}"] + j)
                sbase = SLOT[f"gates{layer}"]
                with pe.Fori(0, T // 16, 1) as turns:
                    for k in range(4):
                        slot_free(pe, sbase + k, turns)
                        pe.wait_ge(gate_rows, turns * 4 + (T // 4 * layer + k + 1))
                        pe.wait_ge(place_rows, turns * 4 + (T // 4 * layer + k + 1))
                        for t in range(4):
                            mm = nc.tensor.matmul(bank(sbase + k)[:, t * P:(t + 1) * P], place[:, k, t],
                                                  gated_rows[:, k, t], start=True, stop=True)
                        full(mm, sbase + k)
                acc_free(pe, f"v{layer}", TB - 1)
                for b in range(4):
                    nc.tensor.matmul(acc[:, b, :], zeros[:, 0:P], zeros[:], start=True, stop=False)
                with pe.Fori(0, EXPERT_TILES // BODY, 1) as turns:
                    for j in range(BODY):
                        pe.wait_ge(staged, turns * BODY + (EXPERT_TILES * layer + j + 1))
                        split_wide(f"v{layer}", j, (x_hi, x_lo), j, False, False, turns)
                for b in range(4):
                    mm = nc.tensor.matmul(acc[:, b, :], zeros[:, 0:P], zeros[:], start=False, stop=True)
                    if b % 2:
                        mm.then_inc(acc_full, 1)
                pe.wait_ge(p_in, 16 * (layer + 1))
                to_acc(f"ple_proj{layer}", tokens(pT), 2)
                turn_over(f"ln{layer}_1", X)
                moved(pe, SLOT[f"turn_ln{layer}_1"], 4)
                split_to_acc(f"ple_gate{layer}")

            peer(0)

            turn_over("x1", X)
            moved(pe, SLOT["turn_x1"], 4)
            split_to_acc("kv_q_down", width=LATENTS)
            pe.wait_ge(latents_ready, 1)
            for q, parts in enumerate((((0, 0), (P, 1)), ((320, 0), (320 + P, 1)), ((320 + 2 * P, 0), (None, 1)))):
                s = SLOT["latents"] + q
                slot_free(pe, s)
                for at, c in parts:
                    for tb in range(TB):
                        src = latent[:, tb, at:at + P] if at is not None else \
                            rope_k2[:, tb].rearrange("p a b c -> p (a b c)")
                        mm = nc.tensor.transpose(bank(s)[:, (2 * c + tb) * P:(2 * c + tb + 1) * P], src, ident[:])
                full(mm, s)
            moved(pe, SLOT["latents"], 3)

            def up(name, lat, n):
                for k in range(n):
                    tile_here(pe, TILE[name] + k)
                for h in range(H8):
                    s = SLOT[name] + h
                    slot_free(pe, s)
                    for k in range(n):
                        if k == n - 1 and h == H8 - 1:
                            begins_tile(nc.tensor.matmul(bank(s)[:, 511:512], zeros[:, 0:P], zeros[:, 0:1],
                                                         start=False, stop=False, skip_group_check=True))
                        mm = nc.tensor.matmul(bank(s)[:, 0:T], tile(TILE[name] + k)[:, h * P:(h + 1) * P],
                                              latT[:, lat + k, :], start=(k == 0), stop=(k == n - 1))
                        if (k == 0 and h == 0) or (0 < k < n - 1 and h == H8 - 1):
                            begins_tile(mm)
                    full(mm, s)

            up("up_k", 0, 2)
            to_acc("up_v", lambda k, tb: latT[:, k, tb * P:(tb + 1) * P], 2)
            up("uq_nope", 2, 3)
            to_acc("uq_rope", lambda k, tb: latT[:, 2 + k, tb * P:(tb + 1) * P], 3, width=512)
            pe.wait_ge(rope_ready, 1)
            for q in range(2):
                s = SLOT["rope"] + q
                slot_free(pe, s)
                for c in range(2):
                    for tb in range(TB):
                        src = q_rot[:, tb].rearrange("p a b c -> p (a b c)")[:, (2 * q + c) * P:(2 * q + c + 1) * P]
                        mm = nc.tensor.transpose(bank(s)[:, (2 * c + tb) * P:(2 * c + tb + 1) * P], src, ident[:])
                full(mm, s)

            def mla_scores(h):
                s = SLOT[("mla", "scores", h)]
                slot_free(pe, s)
                r = head_rows(h)
                for tb in range(TB):
                    n, at = (tb + 1) * P, tb * P
                    o = bank(s)[:, at:at + n]
                    nc.tensor.matmul(o, q_nope[:, h, at:at + P], k_nope[:, h, 0:n], start=True, stop=False)
                    nc.tensor.matmul(o, q_ropeT[r, h // 2, at:at + P], latT[r, 5, 0:n], start=False, stop=False)
                    mm = nc.tensor.matmul(o[:, at:at + P], ident[:], mla_mask[:], start=False, stop=True)
                full(mm, s)

            moved(pe, SLOT["up_k"], 8)
            moved(pe, SLOT["uq_nope"], 8)
            moved(pe, SLOT["rope"], 2)
            acc_gone(pe, "up_v")
            pe.wait_ge(rope_in, 48)
            mla_scores(0)
            for h in range(H8):
                if h + 1 < H8:
                    mla_scores(h + 1)
                pe.wait_ge(probs_ready, h + 1)
                s = SLOT[("mla", "probs", h)]
                slot_free(pe, s)
                for k in range(3):
                    mm = nc.tensor.transpose(bank(s)[:, k * P:(k + 1) * P], mla_p[:, h % 2, k * P:(k + 1) * P],
                                             ident[:])
                full(mm, s)
                moved(pe, s)
                s = SLOT[("mla", "out", h)]
                slot_free(pe, s)
                nc.tensor.matmul(bank(s)[:, 0:T], mla_v[:, 0, h * P:(h + 1) * P], mla_pT[:, h % 2, 0:T],
                                 start=True, stop=False)
                full(nc.tensor.matmul(bank(s)[:, P:T], mla_v[:, 1, h * P:(h + 1) * P], mla_pT[:, h % 2, T:T + P],
                                      start=False, stop=True), s)
            moved(pe, SLOT[("mla", "out", H8 - 1)])
            split_to_acc("b_out")
            peer(1)

            def ffn(n):
                sbase = SLOT[f"ffn{n}"]
                with pe.Fori(0, 2 * FF_TILES // BODY, 1) as turns:
                    for j in range(BODY):
                        split_tall(f"ffn{n}_in", j, sbase + j, turns)
                for j in range(2 * FF_TILES - 2 * FF_TILES % BODY, 2 * FF_TILES):
                    split_tall(f"ffn{n}_in", j, sbase + j)
                for j in range(FF_TILES):
                    moved(pe, sbase + 2 * j + 1)
                    split_wide(f"ffn{n}_out", j, (act_hi, act_lo), j, j == 0, j == FF_TILES - 1)

            turn_over("rms1", xn)
            moved(pe, SLOT["turn_rms1"], 4)
            ffn(1)

            turn_over("rms2", xn)
            moved(pe, SLOT["turn_rms2"], 4)
            split_to_acc("rqk")
            split_to_acc("rv")
            split_to_acc("rg")
            for j in range(8):
                split_tall("nqk", j, SLOT["nqk"] + j)
            turn_over("rqk", rqk_rot.rearrange("p t h a b -> p t (h a b)"))
            split_to_acc("nv", width=512, per_tile=2)

            def na_scores(h):
                s = SLOT[("na", "scores", h)]
                slot_free(pe, s)
                r = head_rows(h)
                for tb in range(TB):
                    mm = nc.tensor.matmul(bank(s)[:, tb * T:(tb + 1) * T], na_qk[r, h // 2, tb * P:(tb + 1) * P],
                                          na_qk[r, 4 + h // 2, :], start=True, stop=True)
                full(mm, s)

            def na_out(h):
                moved(pe, SLOT[("na", "probs", h)])
                s = SLOT[("na", "out", h)]
                slot_free(pe, s)
                for m in range(TB):
                    mm = nc.tensor.matmul(bank(s)[head_rows(h), 0:T], na_v[:, m, h * 64:(h + 1) * 64],
                                          na_pT[:, h % 2, m * T:(m + 1) * T], start=(m == 0), stop=(m == 1))
                full(mm, s)

            moved(pe, SLOT["nqk"], 8)
            acc_gone(pe, "nv")
            na_scores(0)
            for h in range(H8):
                if h + 1 < H8:
                    na_scores(h + 1)
                if h:
                    na_out(h - 1)
                split_wide("g_ret", h, (x_hi, x_lo), h, h == 0, h == KC - 1)
                pe.wait_ge(probs_ready, H8 + h + 1)
                s = SLOT[("na", "probs", h)]
                slot_free(pe, s)
                for m in range(TB):
                    for tb in range(TB):
                        mm = nc.tensor.transpose(bank(s)[:, (2 * m + tb) * P:(2 * m + tb + 1) * P],
                                                 na_s[:, h % 2, tb * T + m * P:tb * T + (m + 1) * P], ident[:])
                full(mm, s)
            na_out(H8 - 1)

            def ret_scores(h):
                s = SLOT[("ret", "scores", h)]
                slot_free(pe, s)
                for m in range(TB):
                    mm = nc.tensor.matmul(bank(s)[:, m * T:(m + 1) * T], rqkT[:, RET_H + h, m * P:(m + 1) * P],
                                          rqkT[:, h, :], start=True, stop=True)
                full(mm, s)

            moved(pe, SLOT["turn_rqk"], 4)
            acc_gone(pe, "rv")
            ret_scores(0)
            for h in range(RET_H):
                split_wide("g_na", 2 * h, (x_hi, x_lo), 2 * h, h == 0, False)
                if h + 1 < RET_H:
                    ret_scores(h + 1)
                split_wide("g_na", 2 * h + 1, (x_hi, x_lo), 2 * h + 1, False, h == RET_H - 1)
                moved(pe, SLOT[("ret", "scores", h)])
                s = SLOT[("ret", "out", h)]
                slot_free(pe, s)
                for tb in range(TB):
                    for m in range(TB):
                        at = m * T + tb * P
                        mm = nc.tensor.matmul(bank(s)[:, tb * T:(tb + 1) * T], ret_p[:, h % 2, at:at + P],
                                              ret_v[:, m, h * T:(h + 1) * T], start=(m == 0), stop=(m == 1))
                full(mm, s)
            turn_over("ret", ret_y.rearrange("p t h n -> p t (h n)"))
            moved(pe, SLOT["turn_ret"], 4)
            split_to_acc("ret_out")
            moved(pe, SLOT[("na", "out", H8 - 1)])
            to_acc("na_out", tokens(na_oT), 4)
            turn_over("merged", merged)
            moved(pe, SLOT["turn_merged"], 4)
            split_to_acc("mix_out")
            turn_over("rms3", xn)
            moved(pe, SLOT["turn_rms3"], 4)
            ffn(2)

        @block.scalar
        def _(act):
            step = Steps(act, act_step)
            sqrts = [0]
            S = nc.scalar

            def square_roots(n):
                sqrts[0] += 1
                act.wait_ge(sqrt_wanted, sqrts[0])
                S.activation(col[:, 1, 0:n], col[:, 0, 0:n], ACT.Sqrt).then_inc(sqrt_done, 1)

            def turned(name, dst, gain=None):
                for q in range(2):
                    s = SLOT[f"turn_{name}"] + q
                    slot_here(act, s)
                    if gain is None:
                        free(S.copy(dst[:, 2 * q:2 * q + 2, :].rearrange("p a b -> p (a b)"), bank(s)), s)
                    else:
                        for c in range(2):
                            k = 2 * q + c
                            ins = S.mul(dst[:, k, :], bank(s)[:, c * T:(c + 1) * T], cols[:, gain + k:gain + k + 1])
                            if c == 0:
                                step(ins)
                        free(ins, s)

            def turned_parts(name, gain=None):
                for q in range(4):
                    s = SLOT[f"turn_{name}"] + q
                    slot_here(act, s)
                    if gain is None:
                        ins = S.copy(x_hi[:, 2 * q:2 * q + 2, :].rearrange("p a b -> p (a b)"), bank(s))
                    else:
                        for c in range(2):
                            k = 2 * q + c
                            ins = S.mul(x_hi[:, k, :], bank(s)[:, c * T:(c + 1) * T], cols[:, gain + k:gain + k + 1])
                    ins.then_inc(x_hi_ready, 1)

            def highs(name, first, last, following=None):
                for j in range(first, last):
                    take_high(act, name, j)
                if following:
                    take_high(act, following, 0)

            def split_from_slots(name, dst, n, first=1, following=None):
                for j in range(first, n + 2):
                    if j < n:
                        take_high(act, name, j)
                    elif j == n and following:
                        take_high(act, following, 0)
                    if j >= 2:
                        s = SLOT[name] + j - 2
                        slot_here(act, s)
                        free(S.copy(dst[:, j - 2, :], bank(s)[:, 0:T]), s)

            def from_slots(name, dst, n):
                for j in range(n):
                    s = SLOT[name] + j
                    slot_here(act, s)
                    free(S.copy(dst[:, j, :], bank(s)[:, 0:T]), s)

            def from_acc(name, dst, func, width=D):
                for tb in range(TB):
                    acc_here(act, name, tb)
                    S.activation(dst(tb), acc_rows(tb)[:, 0:width], func).then_inc(acc_moved, 1)

            act.dma_start(ml_gate_w, a["ml_gate_w"]).then_inc(gate_w_in, 16)
            act.dma_start(XT[:], a["xT"]).then_inc(xt_in, 16)
            for g in range(2):
                act.dma_start(ml_bias[GATE_ROWS[g], :], a["ml_bias"][g]).then_inc(gate_w_in, 16)
            for dst, name in CONSTS:
                act.dma_start(dst, a[name]).then_inc(consts_in, 16)

            def log_sigmoid_part(dst, src, tmp):
                step(S.activation(tmp, src, ACT.Abs))
                step.wait()
                step(S.activation(tmp, tmp, ACT.Exp, scale=-1.0))
                step.wait()
                return S.activation(dst, tmp, ACT.Ln, bias=1.0)

            act.wait_ge(xt_in, 16)
            S.copy(x_hi[:], XT).then_inc(x_hi_ready, 1)
            highs("a_qk", 0, 2)
            act.wait_ge(gates_split, 1)
            log_sigmoid_part(ml_rows[0:H8, 2, :], ml_rows[0:H8, 1, :], ml_rows[0:H8, 3, :]).then_inc(gates_log, 1)
            split_from_slots("a_qk", ml_qk, 8, first=2, following="a_v")
            act.dma_start(X[:], a["x"]).then_inc(x_in, 16)
            highs("a_v", 1, 8, following="a_og")
            for tb in range(TB):
                acc_here(act, "a_v", tb)
                S.copy(ml_v[:, tb, :, 0:P], acc_rows(tb).rearrange("p (h n) -> p h n", h=H8)).then_inc(acc_moved, 1)
            act.wait_ge(gates_scanned, 1)
            S.activation(ml_rows[0:H8, 9, :], ml_rows[0:H8, 8, :], ACT.Exp, scale=-1.0).then_inc(floor_ready, 1)
            act.wait_ge(gate_cols_ready, 1)

            def ml_decay(h):
                s = SLOT[("ml", "decay", h)]
                slot_here(act, s)
                if h >= 2:
                    moved(act, SLOT[("ml", "scores", h - 2)])
                step(S.activation(ml_w[:, h % 2, 0:T], bank(s)[:, 0:T], ACT.Exp, scale=-1.0,
                                  bias=gate_cols[:, 0, h:h + 1]))
                step.wait()
                ins = S.activation(ml_w[:, h % 2, T:T + P], bank(s)[:, T:T + P], ACT.Exp, scale=-1.0,
                                   bias=gate_cols[:, 1, h:h + 1])
                free(ins, s)

            ml_decay(0)
            for h in range(H8):
                if h + 1 < H8:
                    take_high(act, "a_og", h + 1)
                    ml_decay(h + 1)
                s = SLOT[("ml", "out", h)]
                slot_here(act, s)
                free(S.copy(ml_raw[:, :, h, :], bank(s).rearrange("p (t n) -> p t n", t=TB)[:, :, 0:129]), s)
            from_acc("a_og", lambda tb: ml_sig[:, tb, :], ACT.Sigmoid)
            square_roots(16)
            take_high(act, "a_out", 0)
            turned_parts("ml_out", GAIN_ML)
            highs("a_out", 1, 8)
            square_roots(2)

            def peer(layer):
                take_high(act, f"wq{layer}", 0)
                turned_parts(f"ln{layer}_0")
                split_from_slots(f"wq{layer}", peer_q, 16)
                highs(f"u{layer}", 0, 2)
                for half in range(2):
                    for tb in range(TB):
                        for g in range(2):
                            s = SLOT[f"scores{layer}"] + 4 * half + 2 * tb + g
                            slot_here(act, s)
                            at = tb * 2048 + (8 * half + 4 * g) * P
                            free(S.copy(SC[:, at:at + 512], bank(s)), s)
                base = SLOT[f"u{layer}"]

                def experts(j, turns=0):
                    s = base + j if j < LOOPED_U else SLOT[f"last_u{layer}"] + j - LOOPED_U
                    slot_here(act, s, turns * 2)
                    free(S.activation(expert_rows(j, turns), bank(s)[:, 0:T], ACT.Gelu), s)

                for j in range(2, BODY):
                    take_high(act, f"u{layer}", j)
                    experts(j - 2)
                with act.Fori(1, LOOPED_U // BODY, 1) as turns:
                    for j in range(BODY):
                        take_high(act, f"u{layer}", j, turns)
                        experts(j - 2, turns)
                act.wait_ge(softmax_wanted, layer + 1)
                S.activation(FV[:], FV[:], ACT.Exp).then_inc(softmax_exps, 1)
                for j in range(LOOPED_U, EXPERT_TILES):
                    take_high(act, f"u{layer}", j)
                    experts(j - 2)
                for j in range(EXPERT_TILES - 2, EXPERT_TILES):
                    experts(j)
                gates = SLOT[f"gates{layer}"]

                def place_distances(k, turns):
                    slot_here(act, gates + k - 4, turns)
                    for t in range(4):
                        ins = S.activation(distance[:, k, t], iota[:], ACT.Abs,
                                           bias=route_T[:, 1, ds(turns * 16 + (4 * k + t), 1)])
                    ins.then_inc(distances, 1)

                def places(k, turns):
                    act.wait_ge(distances, turns * 4 + (T // 4 * layer + k + 1))
                    S.activation(place[:, k], distance[:, k], ACT.Relu, scale=-1.0, bias=1.0
                                 ).then_inc(place_rows, 1)

                act.wait_ge(routes_turned, layer + 1)
                with act.Fori(0, T // 16, 1) as turns:
                    place_distances(0, turns)
                    for k in range(4):
                        if k + 1 < 4:
                            place_distances(k + 1, turns)
                        places(k, turns)
                moved(act, gates, T // 4)

                def stage(j, turns=0):
                    act.wait_ge(tiles_begun, turns * BODY + (TILE[f"v{layer}"] + j - BODY + 2))
                    S.copy(x_hi[:, j % BODY, :], expert_rows(j, turns)).then_inc(staged_hi, 1)

                stage(0)
                with act.Fori(0, EXPERT_TILES // BODY - 1, 1) as turns:
                    for j in range(BODY):
                        take_high(act, f"v{layer}", j, turns)
                        stage(j + 1, turns)
                for j in range(EXPERT_TILES - BODY, EXPERT_TILES):
                    take_high(act, f"v{layer}", j)
                    if j + 1 < EXPERT_TILES:
                        stage(j + 1)
                square_roots(2)
                take_high(act, f"ple_gate{layer}", 0)
                from_acc(f"ple_proj{layer}", lambda tb: ple_side[:, tb, :], ACT.Copy)
                turned_parts(f"ln{layer}_1")
                highs(f"ple_gate{layer}", 1, 8, following=AFTER_PEER[layer])
                from_acc(f"ple_gate{layer}", lambda tb: ple_sig[:, tb, :], ACT.Sigmoid)

            peer(0)

            act.wait_ge(turn_ready, 2 * TURN["x1"] + 2)
            act.dma_start(inv_freq, a["inv_freq"]).then_inc(rope_in, 16)
            act.dma_start(pos_i, a["positions"]).then_inc(rope_in, 16)
            act.dma_start(mla_mask, a["mla_mask"]).then_inc(rope_in, 16)
            turned_parts("x1")
            highs("kv_q_down", 1, 8)
            act.wait_ge(angles_ready, 1)
            S.activation(sincos.rearrange("p a b c -> p (a b c)"), angle.rearrange("p a b c -> p (a b c)"),
                         ACT.Sin).then_inc(sines_ready, 1)
            acc_here(act, "kv_q_down")
            for tb in range(TB):
                step(S.copy(latent[:, tb, :], acc_rows(tb)[:, 0:LATENTS]))
            step.wait()
            act.sem_inc(latents_here, 1)
            for tb in range(TB):
                for k, (lo, hi) in enumerate(((0, KV_RANK), (KV_RANK + ROPE, LATENTS))):
                    step.wait()
                    step(S.activation(sq_junk[:, 0:hi - lo], acc_rows(tb)[:, lo:hi], ACT.Square,
                                      accum_out=col[:, 2, 2 * tb + k:2 * tb + k + 1]))
            step.wait()
            act.sem_inc(sums_ready, 1)
            act.sem_inc(acc_moved, TB)
            square_roots(4)
            for q, parts in enumerate((((0, GAIN_KV), (1, GAIN_KV + 1)), ((2, GAIN_Q), (3, GAIN_Q + 1)),
                                       ((4, GAIN_Q + 2), (5, None)))):
                s = SLOT["latents"] + q
                slot_here(act, s)
                for c, (k, gain) in enumerate(parts):
                    src = bank(s)[:, c * T:(c + 1) * T]
                    ins = S.copy(latT[:, k, :], src) if gain is None else \
                        S.mul(latT[:, k, :], src, cols[:, gain:gain + 1])
                    if c == 0:
                        step(ins)
                free(ins, s)
            from_slots("up_k", k_nope, 8)
            from_acc("up_v", lambda tb: mla_v[:, tb, :], ACT.Copy)
            from_slots("uq_nope", q_nope, 8)
            for tb in range(TB):
                acc_here(act, "uq_rope", tb)
                ins = S.copy(q_rope[:, tb].rearrange("p a h c -> p h a c"),
                             acc_rows(tb)[:, 0:512].rearrange("p (h a c) -> p h a c", h=H8, a=2))
                ins.then_inc(acc_moved, 1)
            for q in range(2):
                s = SLOT["rope"] + q
                slot_here(act, s)
                free(S.copy(q_ropeT[:, 2 * q:2 * q + 2, :].rearrange("p a b -> p (a b)"), bank(s)), s)

            def exponents(name, n, h, dst, parts, scale):
                act.wait_ge(maxima_ready, n + h + 1)
                for tb, (lo, hi) in enumerate(parts):
                    src = bank(SLOT[(name, "scores", h)]) if name == "mla" else na_s[:, h % 2]
                    step(S.activation(dst[:, h % 2, lo:hi], src[:, lo:hi], ACT.Exp, scale=scale,
                                      bias=col[:, 2 + h % 2, 8 + tb:9 + tb],
                                      accum_out=col[:, 4 + h % 2, tb:tb + 1]))
                step.wait()
                act.sem_inc(exps_ready, 1)

            def probs_over(name, h, dst, width):
                s = SLOT[(name, "probs", h)]
                slot_here(act, s)
                free(S.copy(dst[:, h % 2, :], bank(s)[:, 0:width]), s)

            highs("b_out", 0, 2)
            exponents("mla", 0, 0, mla_p, ((0, P), (P, P + T)), MLA_SCALE)
            for h in range(H8):
                probs_over("mla", h, mla_pT, 384)
                if h + 1 < H8:
                    exponents("mla", 0, h + 1, mla_p, ((0, P), (P, P + T)), MLA_SCALE)
                s = SLOT[("mla", "out", h)]
                slot_here(act, s)
                S.copy(x_hi[:, h, :], bank(s)[:, 0:T]).then_inc(mla_out_hi, 1)
            highs("b_out", 2, 8)
            square_roots(2)
            peer(1)

            def rms_of(ready, src):
                for tb in range(TB):
                    act.wait_ge(*ready(tb))
                    step.wait()
                    step(S.activation(sq_junk, src(tb), ACT.Square, accum_out=col[:, 2, tb:tb + 1]))
                step.wait()
                act.sem_inc(sums_ready, 1)

            def ffn(n):
                base, looped = SLOT[f"ffn{n}"], 2 * FF_TILES // BODY

                def gate(j, turns=0):
                    s = base + 2 * j
                    slot_here(act, s, turns * 2)
                    before = s + 1 - 8
                    act.wait_ge(slot_moved[before % 4], turns * 2 + (before // 4 + 1))
                    free(S.activation(silu_g[:, j % 4, :], bank(s)[:, 0:T], ACT.Silu), s)

                def pair(j, turns=0):
                    take_high(act, f"ffn{n}_in", 2 * j + 1, turns)
                    gate(j, turns)
                    take_high(act, f"ffn{n}_in", 2 * j + 2, turns)

                with act.Fori(0, looped, 1) as turns:
                    for j in range(4):
                        pair(j, turns)
                for j in range(4 * looped, FF_TILES):
                    pair(j)
                highs(f"ffn{n}_out", 1, FF_TILES, following="rqk" if n == 1 else None)

            def post_norm(name):
                rms_of(lambda tb: (acc_full, TB * ACC[name] + tb + 1), acc_rows)
                square_roots(2)

            rms_of(lambda tb: (turn_ready, 2 * TURN["x2"] + 2), lambda tb: X[:, tb, :])
            square_roots(2)
            turned_parts("rms1", GAIN_FFN1)
            ffn(1)
            post_norm("ffn1_out")
            rms_of(lambda tb: (x_rows, tb + 1), lambda tb: X[:, tb, :])
            square_roots(2)
            turned_parts("rms2", GAIN_MIX)
            act.wait_ge(mix_in, 16 * 6)
            highs("rqk", 1, 4)
            log_sigmoid_part(ret_lg[:, 1, :], ret_logit, ret_lg[:, 0, :]).then_inc(logits_ready, 1)
            highs("rqk", 4, 8, following="rv")
            from_acc("rqk", lambda tb: rqk[:, tb].rearrange("p h a b -> p (h a b)"), ACT.Copy)
            highs("rv", 1, 8, following="rg")
            from_acc("rv", lambda tb: ret_v[:, tb, :], ACT.Copy)
            highs("rg", 1, 8, following="nqk")
            from_acc("rg", lambda tb: ret_g[:, tb, :], ACT.Silu)
            split_from_slots("nqk", na_qk, 8, following="nv")
            turned("rqk", rqkT)
            highs("nv", 1, 4, following="g_ret")
            from_acc("nv", lambda tb: na_v[:, tb, :], ACT.Copy, width=512)

            def na_out(h):
                s = SLOT[("na", "out", h)]
                slot_here(act, s)
                free(S.copy(na_oT[head_rows(h), h // 2, :], bank(s)[head_rows(h), 0:T]), s)

            exponents("na", H8, 0, na_s, ((0, T), (T, 2 * T)), 1.0)
            for h in range(H8):
                if h:
                    na_out(h - 1)
                if h + 1 < H8:
                    take_high(act, "g_ret", h + 1)
                    exponents("na", H8, h + 1, na_s, ((0, T), (T, 2 * T)), 1.0)
                else:
                    take_high(act, "g_na", 0)
                probs_over("na", h, na_pT, 512)
            from_acc("g_ret", lambda tb: sig_ret[:, tb, :], ACT.Sigmoid)
            na_out(H8 - 1)

            def ret_decay(h):
                act.wait_ge(decay_wanted, h + 1)
                S.activation(ret_d[:, h % 2, :], ret_d[:, h % 2, :], ACT.Exp).then_inc(decay_ready, 1)

            ret_decay(0)
            for h in range(RET_H):
                if h + 1 < RET_H:
                    ret_decay(h + 1)
                    highs("g_na", 2 * h + 1, 2 * h + 3)
                else:
                    highs("g_na", 2 * h + 1, 2 * h + 2, following="ret_out")
                s = SLOT[("ret", "out", h)]
                slot_here(act, s)
                step(S.copy(ret_y[:, :, h, :], bank(s).rearrange("p (t n) -> p t n", t=TB)))
                for tb in range(TB):
                    step.wait()
                    step(S.activation(ret_junk, bank(s)[:, tb * T:(tb + 1) * T], ACT.Square,
                                      accum_out=col[:, 3, RET_H * tb + h:RET_H * tb + h + 1]))
                step.wait()
                act.sem_inc(slot_moved[s % 4], 1)
            act.sem_inc(sums_ready, 1)
            square_roots(8)
            from_acc("g_na", lambda tb: sig_na[:, tb, :], ACT.Sigmoid)
            turned_parts("ret")
            highs("ret_out", 1, 8)
            acc_here(act, "na_out")
            take_high(act, "mix_out", 0)
            turned_parts("merged")
            highs("mix_out", 1, 8, following="ffn2_in")
            post_norm("mix_out")
            rms_of(lambda tb: (x_rows, TB + tb + 1), lambda tb: X[:, tb, :])
            square_roots(2)
            turned_parts("rms3", GAIN_FFN2)
            ffn(2)
            post_norm("ffn2_out")

        @block.vector
        def _(dve):
            step = Steps(dve, dve_step)
            counts = {"sqrt": 0, "rows": 0, "sums": 0}
            V = nc.vector

            def tt(out, x, y, op):
                step(V.tensor_tensor(out, x, y, op))

            def ts(out, x, s1, s2, op0, op1=None):
                step(V.tensor_scalar(out, x, s1, s2, op0, op1) if op1 is not None
                     else V.tensor_scalar(out, x, s1, None, op0))

            def stt(out, x, s, y, op0, op1):
                step(V.scalar_tensor_tensor(out=out, in0=x, scalar=s, in1=y, op0=op0, op1=op1))

            def wait():
                step.wait()

            def by_halves(op):
                for f in range(2):
                    for tb in range(TB):
                        op(tb, slice(512 * f, 512 * f + 512))
                    wait()
                    dve.sem_inc(turn_ready, 1)

            def inverse_roots(n, wanted=True):
                if wanted:
                    wait()
                    dve.sem_inc(sqrt_wanted, 1)
                counts["sqrt"] += 1
                dve.wait_ge(sqrt_done, counts["sqrt"])
                step(V.reciprocal(col[:, 1, 0:n], col[:, 1, 0:n]))
                wait()

            def turned(name, dst, gain=None):
                for q in range(2, 4):
                    s = SLOT[f"turn_{name}"] + q
                    slot_here(dve, s)
                    if gain is None:
                        free(V.tensor_copy(dst[:, 2 * q:2 * q + 2, :].rearrange("p a b -> p (a b)"), bank(s)), s)
                    else:
                        for c in range(2):
                            k = 2 * q + c
                            ins = V.tensor_scalar(dst[:, k, :], bank(s)[:, c * T:(c + 1) * T],
                                                  cols[:, gain + k:gain + k + 1], None, ALU.mult)
                            if c == 0:
                                step(ins)
                        free(ins, s)

            def turned_parts(name, gain=None):
                for q in range(4):
                    s = SLOT[f"turn_{name}"] + q
                    dve.wait_ge(x_hi_ready, 4 * PART_TURNS.index(name) + q + 2)
                    if gain is None:
                        c = slice(2 * q, 2 * q + 2)
                        ins = V.tensor_tensor(x_lo[:, c, :], bank(s).rearrange("p (a b) -> p a b", a=2),
                                              x_hi[:, c, :], ALU.subtract)
                    else:
                        for c in range(2):
                            k = 2 * q + c
                            ins = V.scalar_tensor_tensor(out=x_lo[:, k, :], in0=bank(s)[:, c * T:(c + 1) * T],
                                                         scalar=cols[:, gain + k:gain + k + 1], in1=x_hi[:, k, :],
                                                         op0=ALU.mult, op1=ALU.subtract)
                    free(ins, s)

            def lows(name, first, last, following=None):
                for j in range(first, last):
                    take_low(dve, name, j)
                if following:
                    take_low(dve, following, 0)

            def rows_here():
                counts["rows"] += 1
                dve.wait_ge(rows_in, 16 * sum(ROW_SETS[:counts["rows"]]))

            def acc_moved_up_to(name, tb):
                dve.wait_ge(acc_moved, TB * ACC[name] + tb + 1)

            def layer_norm(name):
                for tb in range(TB):
                    acc_here(dve, name, tb)
                    V.scalar_tensor_tensor(out=X[:, tb, :], in0=X[:, tb, :], scalar=DN_ALPHA, in1=acc_rows(tb),
                                           op0=ALU.mult, op1=ALU.add).then_inc(acc_moved, 1)
                    acc_moved_up_to(name, tb)
                    for f in range(2):
                        step(V.bn_stats(stats[:, 2 * tb + f, :], X[:, tb, 512 * f:512 * f + 512]))
                wait()
                for tb in range(TB):
                    step(V.bn_aggr(mv[:, tb, :], stats[:, 2 * tb:2 * tb + 2, :]))
                wait()
                ts(col[:, 0, 0:TB], mv[:, 0:TB, 1], NORM_EPS, None, ALU.add)
                wait()
                dve.sem_inc(sqrt_wanted, 1)
                rows_here()
                for tb in range(TB):
                    stt(X[:, tb, :], X[:, tb, :], mv[:, tb, 0:1], rows[:, 0, :], ALU.subtract, ALU.mult)
                inverse_roots(TB, wanted=False)
                by_halves(lambda tb, at: stt(X[:, tb, at], X[:, tb, at], col[:, 1, tb:tb + 1], rows[:, 1, at],
                                             ALU.mult, ALU.add))
                dve.sem_inc(rows_used, 1)

            def mean_square_roots(n, width, eps, src=2):
                counts["sums"] += 1
                dve.wait_ge(sums_ready, counts["sums"])
                ts(col[:, 0, 0:n], col[:, src, 0:n], 1.0 / width, eps, ALU.mult, ALU.add)
                inverse_roots(n)

            def pre_norm():
                mean_square_roots(TB, D, RMS_EPS)
                by_halves(lambda tb, at: ts(xn[:, tb, at], X[:, tb, at], col[:, 1, tb:tb + 1], None, ALU.mult))

            def post_norm(name, weight):
                mean_square_roots(TB, D, RMS_EPS)
                rows_here()
                for tb in range(TB):
                    stt(post_tmp[:, tb, :], acc_rows(tb), col[:, 1, tb:tb + 1], rows[:, 0, :], ALU.mult, ALU.mult)
                wait()
                dve.sem_inc(acc_moved, TB)
                for tb in range(TB):
                    stt(X[:, tb, :], post_tmp[:, tb, :], weight, X[:, tb, :], ALU.mult, ALU.add)
                    wait()
                    dve.sem_inc(x_rows, 1)
                dve.sem_inc(rows_used, 1)

            dve.wait_ge(gate_w_in, 48)
            dve.wait_ge(x_hi_ready, 1)
            V.tensor_tensor(x_lo[:], XT, x_hi[:], ALU.subtract).then_inc(xt_split, 1)
            lows("a_qk", 0, 2)
            s = SLOT["gates"]
            slot_here(dve, s)
            R = lambda k: ml_rows[0:H8, k, :]
            step(V.memset(R(10), 1.0))
            step(V.memset(R(11), 0.0))
            for g in range(2):
                ts(R(g), bank(s)[GATE_ROWS[g], 0:T], ml_bias[GATE_ROWS[g], 0:1], None, ALU.add)
            wait()
            dve.sem_inc(slot_moved[s % 4], 1)
            dve.sem_inc(gates_split, 1)
            lows("a_qk", 2, 3)
            ts(R(4), R(1), 0.0, None, ALU.min)
            wait()
            dve.wait_ge(gates_log, 1)
            tt(R(4), R(4), R(2), ALU.subtract)
            wait()
            step(V.tensor_tensor_scan(R(5), R(10), R(4), 0.0, ALU.mult, ALU.add))
            lows("a_qk", 3, 5)
            wait()
            tt(R(6), R(0), R(5), ALU.subtract)
            wait()
            step(V.tensor_tensor_scan(R(7), R(6), R(11), 0.0, ALU.max, ALU.add))
            lows("a_qk", 5, 7)
            wait()
            tt(R(8), R(5), R(7), ALU.add)
            wait()
            dve.sem_inc(gates_scanned, 1)
            lows("a_qk", 7, 8)
            lows("a_v", 0, 8, following="a_og")
            s = SLOT["gate_cols"]
            slot_here(dve, s)
            step(V.tensor_copy(gate_cols.rearrange("p a b -> p (a b)"), bank(s)[:, 0:32]))
            wait()
            dve.sem_inc(slot_moved[s % 4], 1)
            dve.sem_inc(gate_cols_ready, 1)

            def weighted_scores(h):
                s = SLOT[("ml", "scores", h)]
                slot_here(dve, s)
                moved(dve, SLOT[("ml", "decay", h)])
                if h >= 2:
                    slot_here(dve, SLOT[("ml", "out", h - 2)])
                free(V.scalar_tensor_tensor(out=ml_p[:, h % 2, :], in0=bank(s)[:, 0:384], scalar=ML_SCALE,
                                            in1=ml_w[:, h % 2, :], op0=ALU.mult, op1=ALU.mult), s)

            def head_stats(h):
                moved(dve, SLOT[("ml", "out", h)])
                for tb in range(TB):
                    step(V.bn_stats(stats[:, H8 * tb + h, :], ml_raw[:, tb, h, 0:P]))
                wait()
                for tb in range(TB):
                    step(V.bn_aggr(mv[:, H8 * tb + h, :], stats[:, H8 * tb + h:H8 * tb + h + 1, :]))
                wait()
                for tb in range(TB):
                    ts(ml_hn[:, tb, h * P:(h + 1) * P], ml_raw[:, tb, h, 0:P], mv[:, H8 * tb + h, 0:1], None,
                       ALU.subtract)

            weighted_scores(0)
            for h in range(H8):
                if h + 1 < H8:
                    take_low(dve, "a_og", h + 1)
                    weighted_scores(h + 1)
                head_stats(h)
            c16 = lambda k: col[:, k, 0:16].rearrange("p (t h) -> p t h", t=TB)
            stt(c16(2), ml_raw[:, :, :, 128], -1.0, ml_raw[:, :, :, 128], ALU.mult, ALU.max)
            wait()
            tt(c16(3), c16(2), gate_cols[:, 2:4, :], ALU.max)
            wait()
            step(V.reciprocal(col[:, 2, :], col[:, 3, :]))
            wait()
            tt(col[:, 3, :], col[:, 2, :], col[:, 2, :], ALU.mult)
            wait()
            tt(col[:, 4, :], col[:, 3, :], mv[:, :, 1], ALU.mult)
            wait()
            ts(col[:, 0, :], col[:, 4, :], NORM_EPS, None, ALU.add)
            inverse_roots(16)
            tt(col[:, 5, :], col[:, 1, :], col[:, 2, :], ALU.mult)
            wait()
            acc_gone(dve, "a_og")

            def gated_heads(tb, features):
                for h in range(features.start // P, features.stop // P):
                    k = H8 * tb + h
                    at = ml_hn[:, tb, h * P:(h + 1) * P]
                    stt(at, at, col[:, 5, k:k + 1], ml_sig[:, tb, h * P:(h + 1) * P], ALU.mult, ALU.mult)

            by_halves(gated_heads)
            take_low(dve, "a_out", 0)
            turned_parts("ml_out", GAIN_ML)
            lows("a_out", 1, 8)
            dve.wait_ge(x_in, 16)
            layer_norm("a_out")

            def top16(lists, values, where, between):
                n = len(lists)
                every = 5 if n == 16 else 3
                for r in range(2):
                    for k in range(n):
                        step(V.max(values(k)[:, 8 * r:8 * r + 8], lists[k]))
                        between(k % every == 0)
                    wait()
                    for k in range(n):
                        step(V.max_index(where(k)[:, 8 * r:8 * r + 8], values(k)[:, 8 * r:8 * r + 8], lists[k]))
                        between(k % every == 0)
                    if r == 0:
                        wait()
                        for k in range(n):
                            step(V.match_replace(lists[k], values(k)[:, 0:8], lists[k], LOWEST))
                            between(k % every == 0)
                        wait()

            def routing(layer, between):
                for tb in range(TB):
                    top16([SC[:, tb * 2048 + j * P:tb * 2048 + (j + 1) * P] for j in range(16)],
                          lambda k: TV[:, tb, k, :], lambda k: TI[:, tb, k, :], between)
                wait()
                step(V.tensor_copy(TIf, TI))
                wait()
                v = lambda tb: TV[:, tb].rearrange("p (h c) k -> p h c k", c=2)
                c = shaped(SC[:, 0:2048], H8, TOPK, TOPK)
                for tb in range(TB):
                    tt(c, v(tb)[:, :, 0, :, None].to_broadcast([P, H8, TOPK, TOPK]),
                       v(tb)[:, :, 1, None, :].to_broadcast([P, H8, TOPK, TOPK]), ALU.add)
                    between()
                    wait()
                    top16([c[:, h].rearrange("p a b -> p (a b)") for h in range(H8)],
                          lambda k: FV[:, tb, k, :], lambda k: FI[:, tb, k, :], between)
                    wait()
                top = col[:, 2, 0:16]
                fv = FV.rearrange("p t h k -> p (t h) k")
                step(V.tensor_copy(top, fv[:, :, 0]))
                fi = FI.rearrange("p t h k -> p (t h k)")
                step(V.tensor_scalar(halves[0], fi, 4, None, ALU.logical_shift_right))
                step(V.tensor_scalar(halves[1], fi, 15, None, ALU.bitwise_and))
                wait()
                tt(fv, fv, top[:, :, None].to_broadcast([P, 16, TOPK]), ALU.subtract)
                for k in range(2):
                    step(V.tensor_copy(HL[:, k].rearrange("p t h k -> p (t h k)"), halves[k]))
                wait()
                dve.sem_inc(softmax_wanted, 1)
                for tb in range(TB):
                    for k in range(2):
                        lists = TIf[:, tb].rearrange("p (h c) k -> p h c k", c=2)
                        between()
                        tt(c, HL[:, k, tb, :, :, None].to_broadcast([P, H8, TOPK, TOPK]),
                           iota[:, None, None, 0:TOPK].to_broadcast([P, H8, TOPK, TOPK]), ALU.is_equal)
                        between()
                        wait()
                        tt(c, c, lists[:, :, k, None, :].to_broadcast([P, H8, TOPK, TOPK]), ALU.mult)
                        between()
                        wait()
                        step(V.tensor_reduce(route_index[k][:, tb].rearrange("p h k -> p (h k)"),
                                             c.rearrange("p h a b -> p (h a) b"), AX, ALU.add))
                        wait()

            def gates_from_exps(layer):
                fv = FV.rearrange("p t h k -> p (t h) k")
                dve.wait_ge(softmax_exps, layer + 1)
                step(V.tensor_reduce(col[:, 2, 0:16], fv, AX, ALU.add))
                wait()
                step(V.reciprocal(col[:, 3, 0:16], col[:, 2, 0:16]))
                wait()
                tt(fv, fv, col[:, 3, 0:16, None].to_broadcast([P, 16, TOPK]), ALU.mult)
                wait()
                dve.sem_inc(routes_ready, 1)

            def peer(layer):
                take_low(dve, f"wq{layer}", 0)
                turned_parts(f"ln{layer}_0")
                lows(f"wq{layer}", 1, 16)
                lows(f"u{layer}", 0, 2)
                moved(dve, SLOT[f"scores{layer}"], 8)
                done = [2]

                def between(now=True):
                    if now and done[0] < LOOPED_U - BODY:
                        take_low(dve, f"u{layer}", done[0])
                        done[0] += 1

                routing(layer, between)
                while done[0] % BODY:
                    between()
                with dve.Fori(done[0] // BODY, LOOPED_U // BODY, 1) as turns:
                    for j in range(BODY):
                        take_low(dve, f"u{layer}", j, turns)
                take_low(dve, f"u{layer}", LOOPED_U)
                gates_from_exps(layer)
                for q in range(2):
                    s = SLOT[f"routes{layer}"] + q
                    slot_here(dve, s)
                    step(V.tensor_copy(route_T[:, 2 * q, :], bank(s)[:, 0:T]))
                    if q == 0:
                        ts(route_T[:, 1, :], bank(s)[:, T:2 * T], -1.0, None, ALU.mult)
                    wait()
                    dve.sem_inc(slot_moved[s % 4], 1)
                dve.sem_inc(routes_turned, 1)
                lows(f"u{layer}", LOOPED_U + 1, EXPERT_TILES)
                moved(dve, SLOT[f"last_u{layer}"], BODY)
                base = SLOT[f"gates{layer}"]

                def gate_group(k, turns=0):
                    for t in range(4):
                        at = turns * 16 + (4 * k + t)
                        ins = V.tensor_scalar(gated_rows[:, k % 4, t], iota[:], route_T[:, 0, ds(at, 1)],
                                              route_T[:, 2, ds(at, 1)], ALU.is_equal, ALU.mult)
                    ins.then_inc(gate_rows, 1)

                def apply_gates(k, turns=0):
                    slot_here(dve, base + k, turns)
                    h = expert_tokens[:, ds(turns * 16 + 4 * k, 4), :]
                    free(V.tensor_tensor(h, h, bank(base + k).rearrange("p (t e) -> p t e", t=4), ALU.mult),
                         base + k)

                for k in range(4):
                    gate_group(k)
                    if k >= 2:
                        apply_gates(k - 2)
                with dve.Fori(1, T // 16, 1) as turns:
                    for k in range(4):
                        gate_group(k, turns)
                        apply_gates(k - 2, turns)
                for k in range(T // 4 - 2, T // 4):
                    apply_gates(k)
                moved(dve, base, T // 4)

                def stage(j, turns=0):
                    dve.wait_ge(staged_hi, turns * BODY + (EXPERT_TILES * layer + j + 1))
                    V.tensor_tensor(x_lo[:, j % BODY, :], expert_rows(j, turns), x_hi[:, j % BODY, :],
                                    ALU.subtract).then_inc(staged, 1)

                stage(0)
                with dve.Fori(0, EXPERT_TILES // BODY - 1, 1) as turns:
                    for j in range(BODY):
                        take_low(dve, f"v{layer}", j, turns)
                        stage(j + 1, turns)
                for j in range(EXPERT_TILES - BODY, EXPERT_TILES):
                    take_low(dve, f"v{layer}", j)
                    if j + 1 < EXPERT_TILES:
                        stage(j + 1)
                layer_norm(f"v{layer}")
                take_low(dve, f"ple_gate{layer}", 0)
                turned_parts(f"ln{layer}_1")
                lows(f"ple_gate{layer}", 1, 8, following=AFTER_PEER[layer])
                for tb in range(TB):
                    dve.wait_ge(acc_moved, TB * ACC[f"ple_gate{layer}"] + tb + 1)
                    tt(ple_sig[:, tb, :], ple_sig[:, tb, :], ple_side[:, tb, :], ALU.mult)
                wait()
                by_halves(lambda tb, at: tt(X[:, tb, at], X[:, tb, at], ple_sig[:, tb, at], ALU.add))

            peer(0)
            turned_parts("x1")
            lows("kv_q_down", 1, 4)
            dve.wait_ge(rope_in, 48)
            step(V.tensor_copy(pos_f, pos_i))
            wait()
            for tb in range(TB):
                ts(angle[:, 0, tb, :], inv_freq, pos_f[:, tb:tb + 1], None, ALU.mult)
            wait()
            ts(turns_[:, 0], angle[:, 0], 1.0 / (2 * np.pi), ROUND, ALU.mult, ALU.add)
            ts(turns_[:, 1], angle[:, 0], 1.0 / (2 * np.pi), 0.25, ALU.mult, ALU.add)
            wait()
            ts(turns_[:, 1], turns_[:, 1], ROUND, None, ALU.add)
            wait()
            ts(turns_[:], turns_[:], ROUND, None, ALU.subtract)
            wait()
            stt(angle[:, 1], turns_[:, 1], -TWO_PI_A, angle[:, 0], ALU.mult, ALU.add)
            wait()
            stt(angle[:, 0], turns_[:, 0], -TWO_PI_A, angle[:, 0], ALU.mult, ALU.add)
            wait()
            flat = lambda v: v.rearrange("p a b c -> p (a b c)")
            stt(flat(angle), flat(turns_), -TWO_PI_B, flat(angle), ALU.mult, ALU.add)
            wait()
            ts(angle[:, 1], angle[:, 1], float(np.pi / 2), None, ALU.add)
            wait()
            ts(flat(angle), flat(angle), -PI_BELOW, PI_BELOW, ALU.max, ALU.min)
            wait()
            dve.sem_inc(angles_ready, 1)
            lows("kv_q_down", 4, 8)
            dve.wait_ge(sines_ready, 1)

            def rotate(o1, o2, x1, x2, cos, sin, tmp, pause=lambda n: None):
                wait()
                tt(o1, x1, cos, ALU.mult)
                tt(tmp, x2, sin, ALU.mult)
                tt(o2, x1, sin, ALU.mult)
                pause(0)
                wait()
                tt(o1, o1, tmp, ALU.subtract)
                pause(1)
                wait()
                tt(tmp, x2, cos, ALU.mult)
                pause(2)
                wait()
                tt(o2, o2, tmp, ALU.add)

            dve.wait_ge(latents_here, 1)
            for tb in range(TB):
                x1, x2 = latent[:, tb, 256:288], latent[:, tb, 288:320]
                rotate(rope_k2[:, tb, 0, 0], rope_k2[:, tb, 0, 1], x1, x2, sincos[:, 1, tb], sincos[:, 0, tb],
                       rope_tmp[:, 0, 0:32])
            wait()
            step(V.tensor_copy(rope_k2[:, :, 1], rope_k2[:, :, 0]))
            counts["sums"] += 1
            dve.wait_ge(sums_ready, counts["sums"])
            for k, width in ((0, KV_RANK), (1, Q_RANK)):
                ts(col[:, 0, k:4:2], col[:, 2, k:4:2], 1.0 / width, NORM_EPS, ALU.mult, ALU.add)
            inverse_roots(4)
            for tb in range(TB):
                ts(latent[:, tb, 0:KV_RANK], latent[:, tb, 0:KV_RANK], col[:, 1, 2 * tb:2 * tb + 1], None, ALU.mult)
                ts(latent[:, tb, 320:LATENTS], latent[:, tb, 320:LATENTS], col[:, 1, 2 * tb + 1:2 * tb + 2], None, ALU.mult)
            wait()
            dve.sem_inc(latents_ready, 1)
            acc_gone(dve, "uq_rope")
            for tb in range(TB):
                bc = lambda v: v[:, None, :].to_broadcast([P, H8, 32])
                rotate(q_rot[:, tb, :, 0, :], q_rot[:, tb, :, 1, :], q_rope[:, tb, 0], q_rope[:, tb, 1],
                       bc(sincos[:, 1, tb]), bc(sincos[:, 0, tb]),
                       rope_tmp[:, 0, :].rearrange("p (h c) -> p h c", h=H8))
            wait()
            dve.sem_inc(rope_ready, 1)

            def maxima(h, src, parts, scale):
                for tb, (lo, hi) in enumerate(parts):
                    step(V.tensor_reduce(col[:, 2 + h % 2, 10 + tb:11 + tb], src[:, lo:hi], AX, ALU.max))
                wait()
                ts(col[:, 2 + h % 2, 8:10], col[:, 2 + h % 2, 10:12], -scale, None, ALU.mult)
                wait()
                dve.sem_inc(maxima_ready, 1)

            def normalise(n, h, p, parts):
                dve.wait_ge(exps_ready, n + h + 1)
                step(V.reciprocal(col[:, 4 + h % 2, 2:4], col[:, 4 + h % 2, 0:2]))
                wait()
                for tb, (lo, hi) in enumerate(parts):
                    ts(p[:, h % 2, lo:hi], p[:, h % 2, lo:hi], col[:, 4 + h % 2, 2 + tb:3 + tb], None, ALU.mult)
                wait()
                dve.sem_inc(probs_ready, 1)

            def mla_max(h):
                s = SLOT[("mla", "scores", h)]
                slot_here(dve, s)
                if h >= 2:
                    slot_here(dve, SLOT[("mla", "probs", h - 2)])
                maxima(h, bank(s), parts, MLA_SCALE)

            parts = ((0, P), (P, P + T))
            lows("b_out", 0, 2)
            mla_max(0)
            for h in range(H8):
                normalise(0, h, mla_p, parts)
                dve.sem_inc(slot_moved[SLOT[("mla", "scores", h)] % 4], 1)
                if h + 1 < H8:
                    mla_max(h + 1)
                s = SLOT[("mla", "out", h)]
                dve.wait_ge(mla_out_hi, h + 1)
                free(V.tensor_tensor(x_lo[:, h, :], bank(s)[:, 0:T], x_hi[:, h, :], ALU.subtract), s)
            lows("b_out", 2, 8)
            layer_norm("b_out")
            peer(1)

            def ffn(n):
                base, looped = SLOT[f"ffn{n}"], 2 * FF_TILES // BODY

                def product(j, turns=0):
                    s = base + 2 * j + 1
                    slot_here(dve, s, turns * 2)
                    dve.wait_ge(slot_moved[(s - 1) % 4], turns * 2 + ((s - 1) // 4 + 1))
                    at = slice(j, j + 1) if isinstance(turns, int) else ds(turns * 4 + j, 1)
                    inner = act_f[:, None, :]
                    k = turns * 8 + 2 * (FF_TILES * (n - 1) + j)
                    V.tensor_tensor(inner, silu_g[:, j % 4:j % 4 + 1, :], bank(s)[:, None, 0:T], ALU.mult
                                    ).then_inc(inner_step, 1)
                    dve.wait_ge(inner_step, k + 1)
                    V.tensor_copy(act_hi[:, at, :], inner).then_inc(inner_step, 1)
                    dve.wait_ge(inner_step, k + 2)
                    free(V.tensor_tensor(act_lo[:, at, :], inner, act_hi[:, at, :], ALU.subtract), s)
                    dve.wait_ge(slot_moved[s % 4], turns * 2 + (s // 4 + 1))

                def pair(j, turns=0):
                    take_low(dve, f"ffn{n}_in", 2 * j + 1, turns)
                    take_low(dve, f"ffn{n}_in", 2 * j + 2, turns)
                    product(j, turns)

                with dve.Fori(0, looped, 1) as turns:
                    for j in range(4):
                        pair(j, turns)
                for j in range(4 * looped, FF_TILES):
                    pair(j)
                lows(f"ffn{n}_out", 1, FF_TILES, following="rqk" if n == 1 else None)

            pre_norm()
            turned_parts("rms1", GAIN_FFN1)
            ffn(1)
            post_norm("ffn1_out", 0.5)
            pre_norm()
            turned_parts("rms2", GAIN_MIX)
            lows("rqk", 1, 5)
            dve.wait_ge(mix_in, 16 * 6)
            dve.wait_ge(logits_ready, 1)
            ts(ret_lg[:, 2, :], ret_logit, 0.0, None, ALU.min)
            dve.wait_ge(na_bias_in, 64)
            for tb in range(TB):
                v = na_bias[:, tb].rearrange("p h r c -> p (h r) c")
                tt(v, v, na_colmask[:, None, :].to_broadcast([P, 32, 64]), ALU.add)
                lows("rqk", 5 + 2 * tb, min(7 + 2 * tb, 8))
            wait()
            tt(ret_lg[:, 3, :], ret_lg[:, 2, :], ret_lg[:, 1, :], ALU.subtract)
            lows("rv", 0, 2)
            acc_gone(dve, "rqk")
            for tb in range(TB):
                bc = lambda v: v[:, None, :].to_broadcast([P, 2 * RET_H, 64])
                rotate(rqk_rot[:, tb, :, 0, :], rqk_rot[:, tb, :, 1, :], rqk[:, tb, :, 0, :], rqk[:, tb, :, 1, :],
                       bc(ret_cos[:, tb]), bc(ret_sin[:, tb]),
                       rot_tmp[:, 0, :].rearrange("p (h c) -> p h c", c=64),
                       pause=lambda n: take_low(dve, "rv", 2 + 3 * tb + n))
            wait()
            dve.sem_inc(turn_ready, 2)
            lows("rg", 0, 8)
            lows("nqk", 0, 8)
            take_low(dve, "nv", 0)
            turned("rqk", rqkT)
            lows("nv", 1, 4, following="g_ret")
            nparts = ((0, T), (T, 2 * T))

            def na_max(h):
                s = SLOT[("na", "scores", h)]
                slot_here(dve, s)
                if h >= 2:
                    slot_here(dve, SLOT[("na", "probs", h - 2)])
                for tb in range(TB):
                    stt(na_s[:, h % 2, tb * T:(tb + 1) * T], bank(s)[:, tb * T:(tb + 1) * T], NA_SCALE,
                        na_bias[:, tb, h].rearrange("p r c -> p (r c)"), ALU.mult, ALU.add)
                wait()
                dve.sem_inc(slot_moved[s % 4], 1)
                maxima(h, na_s[:, h % 2], nparts, 1.0)

            na_max(0)
            for h in range(H8):
                normalise(H8, h, na_s, nparts)
                if h + 1 < H8:
                    na_max(h + 1)
                    take_low(dve, "g_ret", h + 1)
                else:
                    take_low(dve, "g_na", 0)

            def ret_exponent(h):
                exponent = ret_d[:, h % 2, :]
                ts(exponent, ret_down, ret_lg[:, 3, RET_H + h:RET_H + h + 1], None, ALU.mult)
                wait()
                stt(exponent, ret_up, ret_lg[:, 3, h:h + 1], exponent, ALU.mult, ALU.add)
                wait()
                dve.sem_inc(decay_wanted, 1)

            ret_exponent(0)
            for h in range(RET_H):
                if h + 1 < RET_H:
                    ret_exponent(h + 1)
                s = SLOT[("ret", "scores", h)]
                slot_here(dve, s)
                dve.wait_ge(decay_ready, h + 1)
                if h >= 2:
                    slot_here(dve, SLOT[("ret", "out", h - 2)])
                step(V.scalar_tensor_tensor(out=ret_p[:, h % 2, :], in0=bank(s), scalar=RET_SCALE,
                                            in1=ret_d[:, h % 2, :], op0=ALU.mult, op1=ALU.mult))
                wait()
                dve.sem_inc(slot_moved[s % 4], 1)
                if h + 1 < RET_H:
                    lows("g_na", 2 * h + 1, 2 * h + 3)
                else:
                    lows("g_na", 2 * h + 1, 2 * h + 2, following="ret_out")
            mean_square_roots(2 * RET_H, T, RMS_EPS, src=3)
            acc_gone(dve, "rg")

            def gated_retention(tb, features):
                for h in range(features.start // T, features.stop // T):
                    k = RET_H * tb + h
                    stt(ret_y[:, tb, h, :], ret_y[:, tb, h, :], col[:, 1, k:k + 1],
                        ret_g[:, tb, h * T:(h + 1) * T], ALU.mult, ALU.mult)

            by_halves(gated_retention)
            turned_parts("ret")
            lows("ret_out", 1, 8)
            for name, dst, gate in (("ret_out", merged_tmp, sig_ret), ("na_out", merged, sig_na)):
                for tb in range(TB):
                    acc_here(dve, name, tb)
                    V.tensor_tensor(dst[:, tb, :], gate[:, tb, :], acc_rows(tb), ALU.mult).then_inc(acc_moved, 1)
            acc_moved_up_to("na_out", TB - 1)
            by_halves(lambda tb, at: tt(merged[:, tb, at], merged[:, tb, at], merged_tmp[:, tb, at], ALU.add))
            take_low(dve, "mix_out", 0)
            turned_parts("merged")
            lows("mix_out", 1, 8, following="ffn2_in")
            post_norm("mix_out", 1.0)
            pre_norm()
            turned_parts("rms3", GAIN_FFN2)
            ffn(2)
            post_norm("ffn2_out", 0.5)





def tall(w):
    n = w.shape[1] // P
    return np.ascontiguousarray(w.reshape(KC, P, n, P).transpose(2, 1, 0, 3)).reshape(n, P, D)


def wide(w):
    return np.ascontiguousarray(w.reshape(-1, P, w.shape[1]))


def by_feature(v):
    return np.ascontiguousarray(v.T.reshape(-1, P, v.shape[0]).transpose(1, 0, 2))


def by_token(v):
    return np.ascontiguousarray(np.swapaxes(v.reshape(TB, P, *v.shape[1:]), 0, 1))


def columns(v):
    return v.reshape(-1, P).T


def constants():
    f = np.float32
    q, k = np.arange(P)[None, :], np.arange(P)[:, None]
    pos = np.arange(T, dtype=f)
    ang = pos[:, None] * (f(1.0) / (f(10000.0) ** np.linspace(0.0, 1.0, 64, dtype=f)))[None, :]
    diff = (np.arange(T)[None, None, :] - (np.arange(P)[:, None, None] + P * np.arange(TB)[None, :, None]))
    c = np.arange(P) % 64
    first = np.clip(c - 8, 0, 48)[:, None]
    cc = np.arange(64)[None, :]
    sel = np.zeros((H8, H8, P), f)
    sel[np.arange(H8), np.arange(H8)] = 1.0
    return {
        "ident": np.eye(P, dtype=f),
        "iota": np.tile(np.arange(P, dtype=f), (P, 1)),
        "ml_sel": sel,
        "ml_mask": np.where(q < k, f(BIG), f(0.0)),
        "mla_mask": np.where(q > k, f(-BIG), f(0.0)),
        "inv_freq": np.tile(f(10000.0) ** (-np.arange(0, ROPE, 2, dtype=f) / f(ROPE)), (P, 1)),
        "ret_cos": by_token(np.cos(ang)), "ret_sin": by_token(np.sin(ang)),
        "ret_up": np.maximum(diff, 0).astype(f).reshape(P, TB * T),
        "ret_down": np.maximum(-diff, 0).astype(f).reshape(P, TB * T),
        "na_colmask": np.where((cc >= first) & (cc < first + 16), f(0.0), f(-BIG)),
    }


def layout(i):
    w, wmix = i["a_w_in"][0], i["w_mix_in_2"][0]
    gate_w = np.zeros((D, GATE_WIDTH), w.dtype)
    for g, at in enumerate(GATE_ROWS):
        gate_w[:, at] = w[:, 2048 + g * H8:2048 + (g + 1) * H8]
    kv_up, uq = i["kv_w_up"].reshape(KV_RANK, H8, 2 * P), i["b_w_uq"][0].reshape(Q_RANK, H8, P + ROPE)
    at = np.clip(np.arange(64)[None, :] - np.arange(64)[:, None] + 15, 0, 30)
    m = {
        "x": by_token(i["x"][0]), "xT": by_feature(i["x"][0]),
        "positions": by_token(i["positions"][0]),
        "ml_gate_w": np.ascontiguousarray(gate_w.reshape(KC, P, GATE_WIDTH).transpose(1, 0, 2)),
        "ml_bias": i["a_b_if"][0][:, :, None],
        "cols": np.ascontiguousarray(np.concatenate(
            [columns(v) for v in (i["a_hn_g"][0], i["kv_norm_g"], i["b_q_norm_g"][0], i["ffn1_pre_norm_2"][0],
                                  i["mix_pre_norm_2"][0], i["ffn2_pre_norm_2"][0])], axis=1)),
        "a_qk": tall(w[:, 0:1024]), "a_v": wide(w[:, 1024:2048]), "a_og": wide(w[:, 2064:3088]),
        "a_out": wide(i["a_w_out"][0]),
        "kv_q_down": wide(np.concatenate([i["kv_w_down"], i["b_w_dq"][0]], axis=1)),
        "up_k": wide(kv_up[:, :, 0:P].reshape(KV_RANK, D)), "up_v": wide(kv_up[:, :, P:].reshape(KV_RANK, D)),
        "uq_nope": wide(uq[:, :, 0:P].reshape(Q_RANK, D)), "uq_rope": wide(uq[:, :, P:].reshape(Q_RANK, 512)),
        "b_out": wide(i["b_w_out"][0]),
        "rqk": wide(wmix[:, 0:1024]), "rv": wide(wmix[:, 1024:2048]), "rg": wide(wmix[:, 2048:3072]),
        "nqk": tall(wmix[:, 3072:4096]),
        "nv": np.ascontiguousarray(wmix[:, 4096:4608].reshape(4, 2, P, 512).transpose(0, 2, 1, 3)).reshape(4, P, D),
        "g_ret": wide(wmix[:, 4608:5632]), "g_na": wide(wmix[:, 5632:6656]),
        "ret_out": wide(i["w_ret_out_2"][0]), "na_out": wide(i["w_na_out_2"][0]),
        "mix_out": wide(i["w_mix_out_2"][0]),
        "ret_logit": np.concatenate([i["ret_decay_fwd_2"], i["ret_decay_bwd_2"]], axis=1),
        "na_bias": np.ascontiguousarray(i["na_rel_bias_2"][0][:, 4:11, :][:, :, at].transpose(2, 0, 1, 3)),
    }
    for n in (1, 2):
        t = tall(i[f"ffn{n}_w_in_2"][0])
        m[f"ffn{n}_in"] = np.stack([t[:FF_TILES], t[FF_TILES:]], axis=1).reshape(2 * FF_TILES, P, D)
        m[f"ffn{n}_out"] = wide(i[f"ffn{n}_w_out_2"][0])
    for l in range(LAYERS):
        m[f"p{l}"] = by_feature(i["p"][l, 0])
        m[f"wq{l}"] = tall(i["peer_w_q"][l])
        m[f"keys{l}"] = np.ascontiguousarray(
            i["peer_sub_keys"][l].reshape(2, KC, P, P).transpose(0, 3, 1, 2)).reshape(2, P, D)
        m[f"u{l}"] = np.ascontiguousarray(
            i["peer_u"][l].reshape(EXPERT_TILES, P, KC, P).transpose(0, 3, 2, 1)).reshape(EXPERT_TILES, P, D)
        m[f"v{l}"] = i["peer_v"][l].reshape(EXPERT_TILES, P, D)
        m[f"ple_proj{l}"] = wide(i["ple_w_proj"][l])
        m[f"ple_gate{l}"] = wide(i["ple_w_gate"][l])
    rows = [(i["ln_g"][l, k], i["ln_b"][l, k]) for l in range(LAYERS) for k in range(2)]
    rows += [(i[n][0],) for n in ("ffn1_post_norm_2", "mix_post_norm_2", "ffn2_post_norm_2")]
    for k, r in enumerate(rows):
        m[f"rows{k}"] = np.stack(r)
    return m


def kernel(**inputs):
    import concourse.bacc as bacc
    from concourse.bass_utils import run_bass_kernel_spmd

    laid = {**layout({k: np.asarray(v) for k, v in inputs.items()}), **constants()}
    nc = bacc.Bacc("TRN2", target_bir_lowering=False, num_devices=1)
    aps = {n: nc.dram_tensor(f"in_{n}", v.shape, mybir.dt.from_np(v.dtype), kind="ExternalInput").ap()
           for n, v in laid.items()}
    out = nc.dram_tensor("out", (1, T, D), F32, kind="ExternalOutput").ap()
    program(nc, aps, out.rearrange("a (t p) d -> p (a t) d", p=P))
    r = run_bass_kernel_spmd(nc, [{f"in_{n}": v for n, v in laid.items()}], core_ids=[0])
    return r.results[0]["out"]
```
